# Optimizing a Trainium2 kernel written in Bass

```python
import math
import jax, jax.numpy as jnp
from jax import lax
import numpy as np

D_MODEL = 2048
BATCH = 1
SEQ = 256
DEPTH = 2

CHUNK = 64
EPS = 1e-6
D_MIX = D_MODEL
D_LRU = D_MIX // 2
LRU_BLOCKS = 16
LRU_BLOCK = D_LRU // LRU_BLOCKS
CONV_WIDTH = 4
LRU_C = 8.0
HEAD_DIM = 64
N_Q_HEADS = (D_MIX - D_LRU) // HEAD_DIM
N_KV_HEADS = 2
Q_PER_KV = N_Q_HEADS // N_KV_HEADS
Q_DIM = N_Q_HEADS * HEAD_DIM
KV_DIM = N_KV_HEADS * HEAD_DIM
IN_COLS = 2 * D_LRU + Q_DIM + 2 * KV_DIM
WINDOW = 128
WINDOW_CHUNKS = WINDOW // CHUNK
S5_GROUP = 16
S5_GROUPS = D_MODEL // S5_GROUP
S5_STATE = 64
D_FF = 4 * D_MODEL
N_EVEN = (DEPTH + 1) // 2
N_ODD = DEPTH // 2
NEG_INF = -1e30

kernel_name = "hybrid_rglru_swa_sink_s5_trunk"

def rmsnorm(x, g):
    xf = x.astype(jnp.float32)
    y = xf * lax.rsqrt(jnp.mean(xf * xf, axis=-1, keepdims=True) + EPS) * g.astype(jnp.float32)
    return y.astype(x.dtype)

def _linear_combine(c1, c2):
    a1, b1 = c1
    a2, b2 = c2
    return a1 * a2, a2 * b1 + b2

def causal_depthwise_conv(x, w, b):
    L = x.shape[1]
    xp = jnp.pad(x, ((0, 0), (CONV_WIDTH - 1, 0), (0, 0)))
    y = b + xp[:, 0:L] * w[0]
    for k in range(1, CONV_WIDTH):
        y = y + xp[:, k:k + L] * w[k]
    return y

def rg_lru(x, w_a, b_a, w_x, b_x, lam):
    B_, L, _ = x.shape
    xf = x.astype(jnp.float32)
    xb = xf.reshape(B_, L, LRU_BLOCKS, LRU_BLOCK)
    r = jax.nn.sigmoid(jnp.einsum('blhi,hij->blhj', xb, w_a.astype(jnp.float32)).reshape(B_, L, D_LRU)
                       + b_a.astype(jnp.float32))
    i = jax.nn.sigmoid(jnp.einsum('blhi,hij->blhj', xb, w_x.astype(jnp.float32)).reshape(B_, L, D_LRU)
                       + b_x.astype(jnp.float32))
    log_a = -LRU_C * r * jax.nn.softplus(-lam.astype(jnp.float32))
    a = jnp.exp(log_a)
    u = jnp.sqrt(-jnp.expm1(2.0 * log_a)) * (i * xf)
    _, h = lax.associative_scan(_linear_combine, (a, u), axis=1)
    return h

def swa_sink_attention(q, k, v, q_gain, k_gain, sinks):
    B_, L = q.shape[:2]
    n_chunks = L // CHUNK
    q = rmsnorm(q.astype(jnp.float32), q_gain)
    k = rmsnorm(k.astype(jnp.float32), k_gain)
    v = v.astype(jnp.float32)
    qc = q.reshape(B_, n_chunks, CHUNK, N_KV_HEADS, Q_PER_KV, HEAD_DIM)

    def band(t):
        t = t.reshape(B_, n_chunks, CHUNK, N_KV_HEADS, HEAD_DIM)
        tp = jnp.pad(t, ((0, 0), (WINDOW_CHUNKS - 1, 0), (0, 0), (0, 0), (0, 0)))
        return jnp.concatenate([tp[:, s:s + n_chunks] for s in range(WINDOW_CHUNKS)], axis=2)

    kb, vb = band(k), band(v)
    chunk_idx = jnp.arange(n_chunks)[:, None]
    key_slot = jnp.arange(WINDOW_CHUNKS * CHUNK)[None, :] // CHUNK
    valid = chunk_idx >= (WINDOW_CHUNKS - 1 - key_slot)
    scores = jnp.einsum('bnqkgd,bnjkd->bnkgqj', qc, kb) * (HEAD_DIM ** -0.5)
    scores = jnp.where(valid[None, :, None, None, None, :], scores, NEG_INF)
    sink = sinks.astype(jnp.float32).reshape(N_KV_HEADS, Q_PER_KV)[None, None, :, :, None, None]
    m = jnp.maximum(jnp.max(scores, axis=-1, keepdims=True), sink)
    p = jnp.exp(scores - m)
    denom = jnp.sum(p, axis=-1, keepdims=True) + jnp.exp(sink - m)
    o = jnp.einsum('bnkgqj,bnjkd->bnqkgd', p / denom, vb)
    return o.reshape(B_, L, Q_DIM)

def s5_grouped(u, lam_re, lam_im, log_step, b_re, b_im, c_re, c_im, d_skip):
    B_, L, _ = u.shape
    uf = u.astype(jnp.float32).reshape(B_, L, S5_GROUPS, S5_GROUP)
    lam = lax.complex(lam_re.astype(jnp.float32), lam_im.astype(jnp.float32))
    step = jnp.exp(log_step.astype(jnp.float32))[:, None]
    lam_bar = jnp.exp(lam * step)
    b = lax.complex(b_re.astype(jnp.float32), b_im.astype(jnp.float32))
    b_bar = ((lam_bar - 1.0) / lam)[:, :, None] * b
    bu = jnp.einsum('blgh,gph->blgp', uf.astype(jnp.complex64), b_bar)
    a = jnp.broadcast_to(lam_bar, bu.shape)
    _, h = lax.associative_scan(_linear_combine, (a, bu), axis=1)
    c = lax.complex(c_re.astype(jnp.float32), c_im.astype(jnp.float32))
    y = jnp.real(jnp.einsum('blgp,ghp->blgh', h, c)) \
        + d_skip.astype(jnp.float32).reshape(S5_GROUPS, S5_GROUP) * uf
    return y.reshape(B_, L, D_MODEL)

def setup_inputs(seed: int = 0) -> dict:
    key = jax.random.key(seed)
    ks = jax.random.split(key, 32)
    f32 = jnp.float32
    nrm = lambda k, shape, s: jax.random.normal(k, shape, f32) * s
    x = jax.random.normal(ks[0], (BATCH, SEQ, D_MODEL), f32)
    mix_norm_e = 1.0 + nrm(ks[1], (N_EVEN, D_MODEL), 0.02)
    w_in_e = nrm(ks[2], (N_EVEN, D_MODEL, IN_COLS), D_MODEL ** -0.5)
    conv_w = nrm(ks[3], (N_EVEN, CONV_WIDTH, D_LRU), CONV_WIDTH ** -0.5)
    conv_b = nrm(ks[4], (N_EVEN, D_LRU), 0.01)
    lru_wa = nrm(ks[5], (N_EVEN, LRU_BLOCKS, LRU_BLOCK, LRU_BLOCK), LRU_BLOCK ** -0.5)
    lru_ba = nrm(ks[6], (N_EVEN, D_LRU), 0.01)
    lru_wx = nrm(ks[7], (N_EVEN, LRU_BLOCKS, LRU_BLOCK, LRU_BLOCK), LRU_BLOCK ** -0.5)
    lru_bx = nrm(ks[8], (N_EVEN, D_LRU), 0.01)
    a_pow = jax.random.uniform(ks[9], (N_EVEN, D_LRU), f32, 0.9, 0.999)
    s = a_pow ** (1.0 / LRU_C)
    lru_lambda = jnp.log(s) - jnp.log1p(-s)
    q_gain = 1.0 + nrm(ks[10], (N_EVEN, HEAD_DIM), 0.02)
    k_gain = 1.0 + nrm(ks[11], (N_EVEN, HEAD_DIM), 0.02)
    sinks = nrm(ks[12], (N_EVEN, N_Q_HEADS), 0.5)
    w_out_e = nrm(ks[13], (N_EVEN, D_MIX, D_MODEL), D_MIX ** -0.5)
    mix_norm_o = 1.0 + nrm(ks[14], (N_ODD, D_MODEL), 0.02)
    n_idx = jnp.broadcast_to(jnp.arange(S5_STATE, dtype=f32), (N_ODD, S5_GROUPS, S5_STATE))
    s5_lam_re = -0.5 + nrm(ks[15], (N_ODD, S5_GROUPS, S5_STATE), 0.01)
    s5_lam_im = jnp.pi * n_idx + nrm(ks[16], (N_ODD, S5_GROUPS, S5_STATE), 0.01)
    s5_log_step = jax.random.uniform(ks[17], (N_ODD, S5_GROUPS), f32, math.log(1e-3), math.log(1e-1))
    s5_b_re = nrm(ks[18], (N_ODD, S5_GROUPS, S5_STATE, S5_GROUP), (2 * S5_GROUP) ** -0.5)
    s5_b_im = nrm(ks[19], (N_ODD, S5_GROUPS, S5_STATE, S5_GROUP), (2 * S5_GROUP) ** -0.5)
    s5_c_re = nrm(ks[20], (N_ODD, S5_GROUPS, S5_GROUP, S5_STATE), 0.5)
    s5_c_im = nrm(ks[21], (N_ODD, S5_GROUPS, S5_GROUP, S5_STATE), 0.5)
    s5_d = nrm(ks[22], (N_ODD, D_MODEL), 1.0)
    w_glu = nrm(ks[23], (N_ODD, D_MODEL, 2 * D_MODEL), D_MODEL ** -0.5)
    ffn_norm = 1.0 + nrm(ks[24], (DEPTH, D_MODEL), 0.02)
    w_up = nrm(ks[25], (DEPTH, D_MODEL, D_FF), D_MODEL ** -0.5)
    w_down = nrm(ks[26], (DEPTH, D_FF, D_MODEL), D_FF ** -0.5)
    return {"x": x, "mix_norm_e": mix_norm_e, "w_in_e": w_in_e, "conv_w": conv_w, "conv_b": conv_b,
            "lru_wa": lru_wa, "lru_ba": lru_ba, "lru_wx": lru_wx, "lru_bx": lru_bx,
            "lru_lambda": lru_lambda, "q_gain": q_gain, "k_gain": k_gain, "sinks": sinks,
            "w_out_e": w_out_e, "mix_norm_o": mix_norm_o, "s5_lam_re": s5_lam_re,
            "s5_lam_im": s5_lam_im, "s5_log_step": s5_log_step, "s5_b_re": s5_b_re,
            "s5_b_im": s5_b_im, "s5_c_re": s5_c_re, "s5_c_im": s5_c_im, "s5_d": s5_d,
            "w_glu": w_glu, "ffn_norm": ffn_norm, "w_up": w_up, "w_down": w_down}

def reference(x, mix_norm_e, w_in_e, conv_w, conv_b, lru_wa, lru_ba, lru_wx, lru_bx, lru_lambda,
              q_gain, k_gain, sinks, w_out_e, mix_norm_o, s5_lam_re, s5_lam_im, s5_log_step,
              s5_b_re, s5_b_im, s5_c_re, s5_c_im, s5_d, w_glu, ffn_norm, w_up, w_down):
    B_, L, _ = x.shape
    split_at = [D_LRU, 2 * D_LRU, 2 * D_LRU + Q_DIM, 2 * D_LRU + Q_DIM + KV_DIM]
    for layer in range(DEPTH):
        j = layer // 2
        if layer % 2 == 0:
            h = rmsnorm(x, mix_norm_e[j])
            proj = h @ w_in_e[j]
            x_br, gate_br, q, k, v = jnp.split(proj, split_at, axis=-1)
            x_br = causal_depthwise_conv(x_br, conv_w[j], conv_b[j])
            y_lru = rg_lru(x_br, lru_wa[j], lru_ba[j], lru_wx[j], lru_bx[j], lru_lambda[j]) \
                * jax.nn.gelu(gate_br.astype(jnp.float32))
            y_att = swa_sink_attention(q.reshape(B_, L, N_Q_HEADS, HEAD_DIM),
                                       k.reshape(B_, L, N_KV_HEADS, HEAD_DIM),
                                       v.reshape(B_, L, N_KV_HEADS, HEAD_DIM),
                                       q_gain[j], k_gain[j], sinks[j])
            mixed = jnp.concatenate([y_lru, y_att], axis=-1).astype(x.dtype)
            x = x + mixed @ w_out_e[j]
        else:
            h = rmsnorm(x, mix_norm_o[j])
            y = s5_grouped(h, s5_lam_re[j], s5_lam_im[j], s5_log_step[j], s5_b_re[j], s5_b_im[j],
                           s5_c_re[j], s5_c_im[j], s5_d[j])
            g = jax.nn.gelu(y).astype(x.dtype) @ w_glu[j]
            val, gate = jnp.split(g, 2, axis=-1)
            x = x + val * jax.nn.sigmoid(gate)
        h = rmsnorm(x, ffn_norm[layer])
        x = x + jnp.square(jax.nn.relu(h @ w_up[layer])) @ w_down[layer]
    return x


_drawn_inputs = setup_inputs


def setup_inputs(seed=0):
    import zlib

    import numpy as np

    out = dict(_drawn_inputs(seed))
    spreads = {}
    factors = {'mix_norm_e': 6.058,
     'conv_b': 8.342,
     'lru_ba': 48.781,
     'lru_bx': 46.082,
     'q_gain': 8.0,
     'k_gain': 8.0,
     'sinks': 8.0,
     'mix_norm_o': 184.435,
     's5_lam_re': 200.0,
     'ffn_norm': 8.0}
    for name, (base, spread) in spreads.items():
        noise = np.random.default_rng([zlib.crc32(name.encode()), seed]).standard_normal(out[name].shape)
        drawn = base * np.exp(spread * noise) if base else spread * noise
        out[name] = __import__('jax').numpy.asarray(drawn.astype(out[name].dtype))
    for name, factor in factors.items():
        out[name] = (out[name] * factor).astype(out[name].dtype)
    return out
```

```python
from contextlib import ExitStack, contextmanager
import math

import concourse.bass as bass
from concourse import mybir

F32 = mybir.dt.float32
F32R = mybir.dt.float32r
ACT = mybir.ActivationFunctionType
ALU = mybir.AluOpType
AX = mybir.AxisListType

P = 128
D = 2048
L = 256
KC = D // P
EPS = 1e-6
DL = D // 2
LC = DL // P
NKV = 2
HD = 64
CH = 64
NCH = L // CH
QKV0 = 2 * DL
LRU_C = 8.0
FF = 4 * D
QTR = FF // D
UK = 4
NU = KC // UK
TW = 2 * P
NT = 64
TPC = 4
SH = 16
TROW = 2 * TPC * L + 2 * TPC * SH
TWO_PI_INV = 1.0 / (2.0 * math.pi)
MAGIC = 1.5 * 2.0 ** 23
PI_HI = 6.28125
PI_MID = 0.0019350051879882812
PI_LO = 2.0 * math.pi - PI_HI - PI_MID
PI_CLAMP = 3.1415925

P_Q = 0
P_KV = P_Q + 4
P_XB = P_KV + 1
P_GT = P_XB + 4
P_OUT = P_GT + 4
P_MLP0 = P_OUT + 8
P_GLU = P_MLP0 + 16 * QTR
P_MLP1 = P_GLU + 16
P_END = P_MLP1 + 16 * QTR

G_MIX0, G_MIX1, G_FF0, G_FF1, C_D, C_CW, C_CB = 0, 16, 32, 48, 64, 80, 112
N_PCOL = 120
C_BA, C_BX, C_LAM, C_QG, C_KG = 0, 8, 16, 24, 25
N_PCOL2 = 26
N_PAR = 21


class Tally:

    def __init__(self, sem, value=0):
        self.sem, self.start, self.count, self.seen = sem, value, 0, 0

    @property
    def value(self):
        return self.start + self.count

    def skip(self, n):
        self.count += n
        self.seen += n

    def inc(self, ins):
        ins.then_inc(self.sem, 1)
        self.skip(1)

    def wait(self, eng, n=1):
        self.skip(n)
        eng.wait_ge(self.sem, self.value)

    def again(self, eng):
        eng.wait_ge(self.sem, self.value)


@contextmanager
def trips(eng, n, *per_trip):
    entry = [t.value for t, _ in per_trip]
    seen = [t.seen for t, _ in per_trip]
    with eng.Fori(0, n) as i:
        for (t, k), at in zip(per_trip, entry):
            t.start, t.count = at + i * k, 0
        yield i
        for (t, k), was in zip(per_trip, seen):
            assert t.seen - was == k, (t.sem, t.seen - was, k)
    for (t, k), at, was in zip(per_trip, entry, seen):
        t.start, t.count, t.seen = at + n * k, 0, was + n * k


def trunk_kernel(nc, x, mix_norm_e, w_in_e, conv_w, conv_b, lru_wa, lru_ba, lru_wx, lru_bx, lru_lambda,
                 q_gain, k_gain, sinks, w_out_e, mix_norm_o, s5_lam_re, s5_lam_im, s5_log_step,
                 s5_b_re, s5_b_im, s5_c_re, s5_c_im, s5_d, w_glu, ffn_norm, w_up, w_down, out, stop=99):
    w_in, w_out, w_gl = w_in_e[0], w_out_e[0], w_glu[0]
    ctx = ExitStack()
    with ctx:
        def sb(name, shape, dt=F32, on=ctx):
            return on.enter_context(nc.sbuf_tensor(name, shape, dt))

        def sem(name):
            return ctx.enter_context(nc.semaphore(name))

        tab_d = nc.dram_tensor("s5_tables", (KC, P, 2 * TPC * L), F32, kind="Internal").ap()
        bbar_d = nc.dram_tensor("s5_bbar", (KC, P, 2 * TPC * SH), F32, kind="Internal").ap()

        xT = sb("xT", [P, KC, L])
        with ExitStack() as o:
            xc = sb("xc", [P, LC, L], on=o)
            lr = sb("lr", [P, LC, L], on=o)
            li = sb("li", [P, LC, L], on=o)
            lt = sb("lt", [P, LC, L], on=o)
        with ExitStack() as o:
            qv = sb("qv", [P, LC + 1, L], on=o)
            qr = sb("qr", [P, LC + 1, L], on=o)
            qt = sb("qt", [P, LC + 1, L], on=o)
        with ExitStack() as o:
            tab = sb("tab", [P, 2, 2, TPC, L], on=o)
            bch = sb("bch", [P, KC, 2 * TPC * SH], on=o)
            craw = sb("craw", [P, 2, KC, HD], on=o)
        A1 = sb("A1", [P, KC, 2 * L], F32R)
        with ExitStack() as o:
            braw = sb("braw", [P, 2, NT, SH], on=o)
            btmp = sb("btmp", [P, 2, NT, SH], on=o)
            bbar = sb("bbar", [P, KC, 2, TPC, SH], on=o)
            s5w = sb("s5w", [P, 20, NT], on=o)
            prow = sb("prow", [N_PCOL, P], on=o)
            prow2 = sb("prow2", [N_PCOL2, P], on=o)
            lrow = sb("lrow", [P, P], on=o)
            srow = sb("srow", [1, 2 * NT + 2 * LC], on=o)
        A2 = sb("A2", [P, KC, 2 * L], F32R)
        raw = sb("raw", [P, NU, UK, TW])
        Wh = sb("Wh", [P, NU, UK, TW], F32R)
        Wl = sb("Wl", [P, NU, UK, TW], F32R)
        with ExitStack() as o:
            xin = sb("xin", [P, 2, D], on=o)
        with ExitStack() as o:
            ab = sb("ab", [P, 2, 2, 2, L], on=o)
            zb = sb("zb", [P, 2, 2, L], on=o)
            gb = sb("gb", [P, 2, 2, L], on=o)
            cdb = sb("cdb", [P, 2, 2, 2, L], on=o)
            yb = sb("yb", [P, 2, L], on=o)
            uc = sb("uc", [P, 2, L], on=o)
            bx = sb("bx", [P, 2, 2, TPC, 2, SH], on=o)
            cx = sb("cx", [P, 2, 2, P], on=o)
            lhs5 = sb("lhs5", [P, 2, 4, P], on=o)
            ncim = sb("ncim", [P, 2, 2, P], on=o)
        qT = sb("qT", [P, LC, L])
        kvT = sb("kvT", [P, 2, L])
        xb = sb("xb", [P, LC, L + 3])
        gT = sb("gT", [P, LC, L])
        wax = sb("wax", [P, 2, LC, P])
        pb = sb("pb", [P, 2, NCH, P])
        pt = sb("pt", [P, 2, NCH, P])
        kd = sb("kd", [P, NKV, L])
        vw = sb("vw", [P, 3, P])
        ctab = sb("ctab", [P, 2, 2, L])
        ttmp = sb("ttmp", [P, 2, 2, 2, L // 2])
        cross = sb("cross", [P, 2, 2, L])
        sq = sb("sq", [P, 2, L])
        ss = sb("ss", [P, 2, L])
        rs = sb("rs", [P, L])
        nv = sb("nv", [P, L])
        nw = sb("nw", [P, L])
        ident = sb("ident", [P, P])
        ones = sb("ones", [P, P])
        hones = sb("hones", [P, P])
        pcol = sb("pcol", [P, N_PCOL])
        pcol2 = sb("pcol2", [P, N_PCOL2])
        lcol = sb("lcol", [P, 2, NT])
        scol = sb("scol", [P, NT + LC])
        rot1 = sb("rot1", [P, 2, NT])
        rho = sb("rho", [P, NT])
        ls = sb("ls", [P, 6, LC])
        par = sb("par", [P, 2])
        am = sb("am", [P, 2, 6, NCH])

        ps = ctx.enter_context(nc.psum_tensor("ps", [P, 4, 512], F32))
        px = ctx.enter_context(nc.psum_tensor("px", [P, 4, 512], F32))

        x_loaded = [sem(f"x_loaded{i}") for i in range(2)]
        par_loaded = sem("par_loaded")
        b_loaded = sem("b_loaded")
        wax_loaded = sem("wax_loaded")
        kd_loaded = sem("kd_loaded")
        landed = [sem(f"landed{s}") for s in range(NU)]
        tab_loaded = [sem(f"tab_loaded{s}") for s in range(2)]
        bc_loaded = sem("bc_loaded")
        tab_stored = sem("tab_stored")
        bbar_stored = sem("bbar_stored")
        out_stored = sem("out_stored")
        consts = sem("consts")
        hi_split = sem("hi_split")
        lo_split = sem("lo_split")
        unit_done = sem("unit_done")
        crossed = sem("crossed")
        pair_read = sem("pair_read")
        hid_ready = sem("hid_ready")
        op_hi = sem("op_hi")
        a1_ready = sem("a1_ready")
        a2_ready = sem("a2_ready")
        gated = sem("gated")
        x_final = sem("x_final")
        squared = sem("squared")
        rms_sum = sem("rms_sum")
        rms_var = sem("rms_var")
        rms_root = sem("rms_root")
        par_t = sem("par_t")
        par_ready = sem("par_ready")
        xt_done = sem("xt_done")
        dve_seq = sem("dve_seq")
        act_seq = sem("act_seq")
        pool_seq = sem("pool_seq")
        s5_exp = sem("s5_exp")
        s5_arg = sem("s5_arg")
        s5_small = sem("s5_small")
        bbar_ready = sem("bbar_ready")
        tab_made = sem("tab_made")
        lru_sp = sem("lru_sp"); lru_arg = sem("lru_arg"); conv_done = sem("conv_done")
        gates_mm = sem("gates_mm"); gates_sg = sem("gates_sg"); lru_a = sem("lru_a"); lru_m2 = sem("lru_m2")
        lru_m = sem("lru_m"); lru_h = sem("lru_h"); lru_y = sem("lru_y"); op_hi2 = sem("op_hi2")
        qk_sq = sem("qk_sq"); qk_sum = sem("qk_sum"); qk_var = sem("qk_var"); qk_root = sem("qk_root")
        qk_norm = sem("qk_norm"); kd_ready = sem("kd_ready"); v_t = sem("v_t"); v_ready = sem("v_ready")
        scored = sem("scored"); maxed = sem("maxed"); expd = sem("expd"); probs = sem("probs")
        p_t = sem("p_t"); p_copied = sem("p_copied"); att_o = sem("att_o")
        s5_bu = sem("s5_bu"); s5_rot = sem("s5_rot"); s5_z = sem("s5_z"); s5_g = sem("s5_g")
        s5_cs = sem("s5_cs"); s5_sn = sem("s5_sn"); s5_y = sem("s5_y"); s5_yf = sem("s5_yf"); s5_ge = sem("s5_ge")
        s5_mask = sem("s5_mask"); s5_tr = sem("s5_tr"); s5_lhs = sem("s5_lhs"); s5_neg = sem("s5_neg")
        bx_zero = sem("bx_zero"); u_ready = sem("u_ready"); out_t = sem("out_t"); out_c = sem("out_c"); zeroed = sem("zeroed")
        block = ctx.enter_context(nc.Block())

        def bu_bank(tl):
            return (px[:, 0], px[:, 1], ps[:, 2], ps[:, 3])[tl % 4]

        def gain(col):
            return pcol[:, bass.ds(col, 1)]

        def double_pairs(eng, n_pairs, body, *per_pair, first=0, last=0):
            for j in range(first):
                body(j, j % 2)
            mid = (n_pairs - first - last) // 2
            if mid:
                with trips(eng, mid, *per_pair) as i:
                    body(i * 2 + first, 0)
                    body(i * 2 + (first + 1), 1)
            for j in range(n_pairs - last, n_pairs):
                body(j, j % 2)

        @block.sync
        def _(sp):
            for i in range(2):
                sp.dma_start(xin[:, i, :], x[0, i * P:(i + 1) * P, :]).then_inc(x_loaded[i], 16)

            def load_pair(g, wide, row0, col0):
                for s in range(NU):
                    if not (isinstance(g, int) and g == 0):
                        sp.wait_ge(lo_split, (g - 1) * NU + (s + 1))
                    src = wide[bass.ds(row0 + s * UK * P, UK * P), bass.ds(col0, TW)]
                    sp.dma_start(raw[:, s], src.rearrange("(c p) n -> p c n", p=P)).then_inc(landed[s], 16)

            def load_mlp(g0, layer):
                with sp.Fori(0, QTR) as q:
                    with sp.Fori(0, 8) as j:
                        load_pair(q * 16 + j + g0, w_up[layer], 0, q * D + j * TW)
                    with sp.Fori(0, 8) as j:
                        load_pair(q * 16 + j + (g0 + 8), w_down[layer], q * D, j * TW)

            load_pair(0, w_in, 0, QKV0)
            with sp.Fori(1, 5) as j:
                load_pair(j + P_Q, w_in, 0, j * TW + QKV0)
            with sp.Fori(0, 8) as j:
                load_pair(j + P_XB, w_in, 0, j * TW)
            with sp.Fori(0, 8) as j:
                load_pair(j + P_OUT, w_out, 0, j * TW)
            load_mlp(P_MLP0, 0)
            for j in range(2):
                load_pair(P_GLU + j, w_gl, 0, j * D)
            sp.wait_ge(bbar_stored, 16)
            sp.dma_start(bch[:, :, :], bbar_d.rearrange("c p f -> p c f")).then_inc(bc_loaded, 16)
            for k, s5_c in enumerate((s5_c_re, s5_c_im)):
                rows = s5_c[0].rearrange("g h p -> (g h) p")
                sp.dma_start(craw[:, k], rows.rearrange("(c p) n -> p c n", p=P)).then_inc(bc_loaded, 16)

            def load_tables(c, b):
                if not isinstance(c, int):
                    sp.wait_ge(s5_yf, c - 1)
                sp.dma_start(tab[:, b].rearrange("p k j t -> p (k j t)"),
                             tab_d[bass.ds(c, 1)].rearrange("o p f -> p (o f)")).then_inc(tab_loaded[b], 16)

            sp.wait_ge(tab_stored, KC * 32)
            for c in range(2):
                load_tables(c, c)
            with sp.Fori(1, KC // 2) as i:
                for b in range(2):
                    load_tables(i * 2 + b, b)
            with sp.Fori(1, 8) as j:
                for h in range(2):
                    load_pair(j * 2 + (h + P_GLU), w_gl, 0, j * TW + h * D)
            load_mlp(P_MLP1, 1)
            with sp.Fori(0, KC // 2) as i:
                sp.wait_ge(out_c, i + 1)
                sp.dma_start(out[0].rearrange("(a p) d -> p a d", p=P)[:, :, bass.ds(i * TW, TW)],
                             xin.rearrange("p a (i d) -> p a i d", i=8)[:, :, bass.ds(i, 1), :]
                             .rearrange("p a o d -> p a (o d)")).then_inc(out_stored, 16)
            sp.wait_ge(out_stored, 16 * (KC // 2))

        @block.tensor
        def _(pe):
            mm = nc.tensor.matmul

            pe.wait_ge(consts, 1)
            pe.wait_ge(par_loaded, 16 * N_PAR)
            row = px[:, 3]
            nc.tensor.transpose(row[:, 0:N_PCOL], prow[:, :], ident[0:N_PCOL, 0:N_PCOL])
            nc.tensor.transpose(row[:, 120:120 + N_PCOL2], prow2[:, :], ident[0:N_PCOL2, 0:N_PCOL2])
            nc.tensor.transpose(row[:, 146:146 + P], lrow[:, :], ident[:, :])
            steps = srow[0:1, 0:2 * NT].rearrange("a (j g) -> a g j", g=2)
            snk = srow[0:1, 2 * NT:].rearrange("a (j g) -> a g j", g=2)
            for g in range(2):
                mm(row[64 * g:64 * g + 64, 274:274 + NT], ones[0:1, 0:64], steps[:, g], start=True, stop=True)
                last = mm(row[64 * g:64 * g + 64, 274 + NT:274 + NT + LC], ones[0:1, 0:64], snk[:, g],
                          start=True, stop=True)
            last.then_inc(par_t, 1)
            for i in range(2):
                pe.wait_ge(x_loaded[i], 16)
            for i in range(KC // 2):
                if i >= 3:
                    pe.wait_ge(op_hi, i - 2)
                for c in range(2):
                    for a in range(2):
                        last = nc.tensor.transpose(px[:, i % 3, c * L + a * P:c * L + a * P + P],
                                                   xin[:, a, bass.ts(2 * i + c, P)], ident[:, :])
                last.then_inc(xt_done, 1)

            def pair(g, d, A, ready=None, base=0, per_unit=0):
                b = 2 * d
                if not (isinstance(g, int) and g < 2):
                    pe.wait_ge(pair_read, g - 1)
                for s in range(NU):
                    pe.wait_ge(lo_split, g * NU + (s + 1))
                    if ready is not None:
                        pe.wait_ge(ready, base + per_unit * (s + 1))
                    for t in range(2):
                        for c in range(UK):
                            k = s * UK + c
                            cols = slice(t * P, t * P + P)
                            wide = lambda: mm(ps[:, b + t, :], Wh[:, s, c, cols], A[:, k, :],
                                              start=(k == 0), stop=(k == KC - 1))
                            half = lambda: mm(ps[:, b + t, 0:L], Wl[:, s, c, cols], A[:, k, 0:L],
                                              start=False, stop=False)
                            if k == KC - 1:
                                half()
                                last = wide()
                            else:
                                wide()
                                last = half()
                    last.then_inc(unit_done, 1)

            def channel_sum(n):
                pe.wait_ge(squared, 8 * n)
                mm(px[:, 3, 0:L], ones[:, :], ss[:, 0], start=True, stop=False)
                mm(px[:, 3, 0:L], ones[:, :], ss[:, 1], start=False, stop=True).then_inc(rms_sum, 1)

            def phase(g0, n, A, **ready):
                def body(j, d):
                    pair(j + g0, (g0 + d) % 2, A, **ready)
                double_pairs(pe, n, body)

            pair(0, 0, A1, a1_ready, 0, 2)
            pe.wait_ge(par_ready, 1)
            channel_sum(1)
            pair(1, 1, A1)
            phase(P_Q + 2, 2, A1)
            pair(P_KV, P_KV % 2, A1)
            phase(P_XB, 8, A1)
            if stop < 1:
                return

            pe.wait_ge(qk_sq, 1)
            for i in range(LC + 1):
                last = mm(px[:, i // 2, (i % 2) * L:(i % 2) * L + L] if i < LC else ps[:, 0, 0:L],
                          hones[:, :], qt[:, i, :], start=True, stop=True)
            last.then_inc(qk_sum, 1)
            for w in range(3):
                last = nc.tensor.transpose(ps[:, 1, w * P:w * P + P], kvT[:, 1, w * CH:w * CH + P], ident[:, :])
            last.then_inc(v_t, 1)
            pe.wait_ge(qk_norm, 1)
            pe.wait_ge(kd_loaded, 32)

            def scores(i):
                if i >= 2:
                    pe.wait_ge(expd, i - 1)
                for n in range(NCH):
                    for h in range(2):
                        half = slice(64 * h, 64 * h + 64)
                        k0 = max(n - 1, 0) * CH
                        nk = P if n else CH
                        last = mm(px[half, i % 2, n * P:n * P + nk], qT[half, i, n * CH:n * CH + CH],
                                  kd[half, i // 4, k0:k0 + nk], start=True, stop=True)
                last.then_inc(scored, 1)

            scores(0)
            for i in range(LC):
                if i + 1 < LC:
                    scores(i + 1)
                pe.wait_ge(probs, i + 1)
                if i >= 1:
                    pe.wait_ge(p_copied, i)
                for n in range(NCH):
                    nk = P if n else CH
                    last = nc.tensor.transpose(px[0:nk, 2, n * P:n * P + P], pb[:, i % 2, n, 0:nk], ident[:, :])
                last.then_inc(p_t, 1)
                pe.wait_ge(p_copied, i + 1)
                pe.wait_ge(v_ready, 1)
                if i >= 1:
                    pe.wait_ge(a2_ready, i)
                for n in range(NCH):
                    for h in range(2):
                        nk = P if n else CH
                        last = mm(px[64 * h:64 * h + 64, 3, n * CH:n * CH + CH],
                                  vw[0:nk, max(n - 1, 0), 64 * (i // 4):64 * (i // 4) + 64],
                                  pt[0:nk, i % 2, n, 64 * h:64 * h + 64], start=True, stop=True)
                last.then_inc(att_o, 1)

            pe.wait_ge(wax_loaded, 64)
            for c in range(LC):
                pe.wait_ge(conv_done, c + 1)
                if c >= 2:
                    pe.wait_ge(gates_sg, c - 1)
                for k in range(2):
                    last = mm(px[:, c % 2, k * L:k * L + L], wax[:, k, c, :], xc[:, c, :], start=True, stop=True)
                last.then_inc(gates_mm, 1)
            if stop < 2:
                return

            phase(P_OUT, 8, A2, ready=a2_ready, base=KC)

            def mlp(g0, a1_at, a1_unit, a2_at, norm):
                def up(j, d, q=0, quarter0=True):
                    pair(q * 16 + j + g0, (g0 + d) % 2, A1, a1_ready, a1_at, a1_unit)
                    if quarter0 and isinstance(j, int) and j == 0:
                        channel_sum(norm)

                def down(j, d, q=0):
                    pair(q * 16 + j + (g0 + 8), (g0 + d) % 2, A2, a2_ready, q * 8 + a2_at, 2)

                double_pairs(pe, 8, up, first=2)
                double_pairs(pe, 8, down)
                with pe.Fori(1, QTR) as q:
                    double_pairs(pe, 8, lambda j, d: up(j, d, q, False))
                    double_pairs(pe, 8, lambda j, d: down(j, d, q))

            mlp(P_MLP0, 8, 2, 16, 2)
            if stop < 3:
                return

            channel_sum(3)
            pe.wait_ge(pair_read, P_GLU)

            def s5_prepare(c, b):
                pe.wait_ge(s5_mask, c + 1)
                for k in range(2):
                    nc.tensor.transpose(px[:, 2, k * P:k * P + P],
                                        bx[:, b, k].rearrange("p j g h -> p (j g h)"), ident[:, :])
                for k in range(2):
                    last = nc.tensor.transpose(px[:, 2, (2 + k) * P:(3 + k) * P], cx[:, b, k], ident[:, :])
                last.then_inc(s5_tr, 1)

            def s5_in(t, c, b, tl):
                if not isinstance(t, int) or t >= 4:
                    pe.wait_ge(s5_rot, t - 3)
                if tl == 0:
                    pe.wait_ge(s5_neg, c + 1)
                    pe.wait_ge(u_ready, c + 1)
                rows = slice(32 * tl, 32 * tl + 32)
                for k in range(2):
                    last = mm(bu_bank(tl)[:, k * L:k * L + L], lhs5[rows, b, k, :], uc[rows, b, :],
                              start=True, stop=True)
                last.then_inc(s5_bu, 1)

            def s5_out(t, b, tl):
                pe.wait_ge(s5_cs, t + 1)
                pe.wait_ge(s5_sn, t + 1)
                own = slice(32 * tl, 32 * tl + 32)
                y, d = ps[own, b, 0:L], tl % 2
                mm(y, lhs5[:, b, 2, own], cdb[:, d, 0, 0], start=True, stop=False)
                mm(y, ncim[:, b, 1, own], cdb[:, d, 0, 1], start=False, stop=False)
                mm(y, ncim[:, b, 0, own], cdb[:, d, 1, 1], start=False, stop=False)
                mm(y, ncim[:, b, 1, own], cdb[:, d, 1, 0], start=False, stop=True).then_inc(s5_y, 1)

            def s5_trip(i, more):
                for tl in range(2 * TPC):
                    t, c, b = i * (2 * TPC) + tl, i * 2 + tl // TPC, tl // TPC
                    n = tl + 3
                    if tl % TPC == 0 and (b == 0 or more):
                        s5_prepare(c + 1, 1 - b)
                    if n < 2 * TPC or more:
                        s5_in(t + 3, i * 2 + n // TPC, (n // TPC) % 2, n % TPC)
                    if tl % TPC == 0 and (not isinstance(c, int) or c >= 2):
                        pe.wait_ge(s5_yf, c - 1)
                    s5_out(t, b, tl % TPC)

            s5_prepare(0, 0)
            for tl in range(3):
                s5_in(tl, 0, 0, tl)
            s5_trip(0, True)
            with pe.Fori(1, KC // 2 - 1) as i:
                s5_trip(i, True)
            s5_trip(KC // 2 - 1, False)
            if stop < 4:
                return

            phase(P_GLU, 16, A2, ready=a2_ready, base=48, per_unit=4)
            mlp(P_MLP1, 16, 2, 64, 4)

            for i in range(KC // 2):
                pe.wait_ge(x_final, 73 + i)
                if i >= 2:
                    pe.wait_ge(out_c, i - 1)
                for a in range(2):
                    for c in range(2):
                        last = nc.tensor.transpose(px[:, i % 2, (2 * a + c) * P:(2 * a + c + 1) * P],
                                                   xT[:, 2 * i + c, a * P:a * P + P], ident[:, :])
                last.then_inc(out_t, 1)

        @block.scalar
        def _(act):
            fn = nc.scalar.activation
            def rows(col, src, n):
                act.dma_start(prow[col:col + n, :], src.rearrange("(c p) -> c p", p=P)).then_inc(par_loaded, 16)

            def rows2(col, src, n):
                act.dma_start(prow2[col:col + n, :], src.rearrange("(c p) -> c p", p=P)).then_inc(par_loaded, 16)

            rows(G_MIX0, mix_norm_e[0], KC)
            rows(G_MIX1, mix_norm_o[0], KC)
            rows(G_FF0, ffn_norm[0], KC)
            rows(G_FF1, ffn_norm[1], KC)
            rows(C_D, s5_d[0], KC)
            for k in range(4):
                rows(C_CW + k * LC, conv_w[0, k], LC)
            rows(C_CB, conv_b[0], LC)
            rows2(C_BA, lru_ba[0], LC)
            rows2(C_BX, lru_bx[0], LC)
            rows2(C_LAM, lru_lambda[0], LC)
            for col, src in ((C_QG, q_gain), (C_KG, k_gain)):
                for h in range(2):
                    act.dma_start(prow2[col:col + 1, h * HD:h * HD + HD], src).then_inc(par_loaded, 16)
            act.dma_start(lrow[0:NT, :], s5_lam_re[0].rearrange("(j g) p -> j (g p)", g=2)).then_inc(par_loaded, 16)
            act.dma_start(lrow[NT:P, :], s5_lam_im[0].rearrange("(j g) p -> j (g p)", g=2)).then_inc(par_loaded, 16)
            act.dma_start(srow[0:1, 0:2 * NT], s5_log_step).then_inc(par_loaded, 16)
            act.dma_start(srow[0:1, 2 * NT:], sinks).then_inc(par_loaded, 16)
            for k, s5_b in enumerate((s5_b_re, s5_b_im)):
                act.dma_start(braw[:, k], s5_b[0].rearrange("(j g) p h -> (g p) j h", g=2)).then_inc(b_loaded, 16)
            act.wait_ge(zeroed, 1)
            for k, w in enumerate((lru_wa, lru_wx)):
                for h in range(2):
                    half = slice(64 * h, 64 * h + 64)
                    act.dma_start(wax[half, k, :, half],
                                  w[0].rearrange("(c h) i j -> h i c j", h=2)[h]).then_inc(wax_loaded, 16)

            hi = Tally(op_hi)
            xf = Tally(x_final)
            hid = Tally(hid_ready)
            var = Tally(rms_var)
            root = Tally(rms_root)
            gate = Tally(gated)

            act.preload_act_table(ACT.Copy)
            act.wait_ge(par_ready, 1)
            for i in range(KC // 2):
                act.wait_ge(xt_done, i + 1)
                src = px[:, i % 3, :].rearrange("p (c t) -> p c t", c=2)
                fn(xT[:, 2 * i:2 * i + 2, :], src, ACT.Copy)
                for c in range(2):
                    last = fn(A1[:, 2 * i + c, 0:L], src[:, c], ACT.Copy, scale=gain(G_MIX0 + 2 * i + c))
                hi.inc(last)

            def split(g, s):
                act.wait_ge(landed[s], (g + 1) * 16)
                if not (isinstance(g, int) and g == 0):
                    act.wait_ge(unit_done, (g - 1) * NU + (s + 1))
                fn(Wh[:, s], raw[:, s], ACT.Copy).then_inc(hi_split, 1)

            def pair(g, d, nxt=True, before=None):
                if nxt:
                    for s in range(NU):
                        split(g + 1, s)
                if before:
                    before()
                act.wait_ge(unit_done, (g + 1) * NU)
                fn(cross[:, d], ps[:, 2 * d:2 * d + 2, L:2 * L], ACT.Copy).then_inc(crossed, 1)

            def rms():
                var.wait(act)
                root.inc(fn(rs[:, :], nv[:, :], ACT.Sqrt))

            def operand_from_x(j, col):
                xf.wait(act)
                for c in range(2):
                    last = fn(A1[:, bass.ds(j * 2 + c, 1), 0:L], xT[:, bass.ds(j * 2 + c, 1), :], ACT.Copy,
                              scale=gain(j * 2 + (col + c)))
                hi.inc(last)

            for s in range(NU):
                split(0, s)

            act.wait_ge(s5_arg, 1)
            fn(s5w[:, 0, :], scol[:, 0:NT], ACT.Exp).then_inc(s5_exp, 1)
            act.wait_ge(s5_arg, 2)
            fn(s5w[:, 7, :], s5w[:, 1, :], ACT.Exp)
            fn(s5w[:, 8, :], s5w[:, 6, :], ACT.Tanh, scale=0.5)
            fn(ls[:, 1, :], ls[:, 0, :], ACT.Exp, scale=-1.0)
            fn(s5w[:, 4, :], s5w[:, 4, :], ACT.Sin)
            fn(s5w[:, 5, :], s5w[:, 5, :], ACT.Sin).then_inc(s5_exp, 1)

            pair(0, 0, before=rms)
            pair(1, 1)

            def phase(g0, n, **kw):
                double_pairs(act, n, lambda j, d: pair(j + g0, (g0 + d) % 2, **kw))

            phase(P_Q + 2, 2)
            pair(P_KV, P_KV % 2)
            phase(P_XB, 8)
            if stop < 1:
                return

            act.wait_ge(bbar_stored, 16)
            act.wait_ge(qk_var, 1)
            fn(qr[:, :, :], qv[:, :, :], ACT.Sqrt).then_inc(qk_root, 1)
            act.wait_ge(kd_ready, 1)
            act.dma_start(kd[64:P, 0, :], kvT[0:64, 0, :]).then_inc(kd_loaded, 16)
            act.dma_start(kd[0:64, 1, :], kvT[64:P, 0, :]).then_inc(kd_loaded, 16)
            for i in range(LC):
                d = i % 2
                act.wait_ge(maxed, i + 1)
                for n in range(NCH):
                    k0 = 0 if n else CH
                    nk = P - k0
                    fn(pb[:, d, n, 0:nk], px[:, d, n * P:n * P + nk], ACT.Exp, bias=am[:, d, 1, n:n + 1],
                       scale=HD ** -0.5, accum_out=am[:, d, 2, n:n + 1])
                fn(am[:, d, 3, :], am[:, d, 1, :], ACT.Exp, bias=scol[:, NT + i:NT + i + 1]).then_inc(expd, 1)
                act.wait_ge(p_t, i + 1)
                fn(pt[0:64, d, 0, :], px[0:64, 2, 0:P], ACT.Copy)
                fn(pt[:, d, 1:NCH, :], px[:, 2, P:NCH * P].rearrange("p (n q) -> p n q", n=NCH - 1), ACT.Copy)\
                    .then_inc(p_copied, 1)
                act.wait_ge(att_o, i + 1)
                hi.inc(fn(A2[:, LC + i, 0:L], px[:, 3, 0:L], ACT.Copy))

            for c in range(LC):
                act.wait_ge(gates_mm, c + 1)
                fn(lr[:, c], px[:, c % 2, 0:L], ACT.Sigmoid, bias=pcol2[:, C_BA + c:C_BA + c + 1])
                fn(li[:, c], px[:, c % 2, L:2 * L], ACT.Sigmoid, bias=pcol2[:, C_BX + c:C_BX + c + 1])\
                    .then_inc(gates_sg, 1)
            act.wait_ge(gates_sg, LC)
            act.wait_ge(lru_sp, 1)
            for c in range(LC):
                fn(lt[:, c], lr[:, c], ACT.Tanh, scale=ls[:, 4, c:c + 1])
            for c in range(LC):
                fn(lr[:, c], lr[:, c], ACT.Exp, scale=ls[:, 5, c:c + 1]).then_inc(lru_a, 1)
            for c in range(LC):
                act.wait_ge(lru_m2, c + 1)
                fn(lt[:, c], lt[:, c], ACT.Sqrt, scale=2.0).then_inc(lru_m, 1)
            for c in range(LC):
                fn(gT[:, c], gT[:, c], ACT.Gelu_apprx_tanh).then_inc(lru_h, 1)
            for c in range(LC):
                act.wait_ge(lru_y, c + 1)
                hi.inc(fn(A2[:, c, 0:L], gT[:, c], ACT.Copy))
            if stop < 2:
                return

            def out_pair(j, d):
                pair(j + P_OUT, (P_OUT + d) % 2)
                operand_from_x(j, G_FF0)
            double_pairs(act, 8, out_pair, (hi, 2), (xf, 2))

            def mlp(g0, last_gain, final):
                def up(j, d, q=0, quarter0=True):
                    pair(q * 16 + j + g0, (g0 + d) % 2,
                         before=rms if quarter0 and isinstance(j, int) and j == 0 else None)
                    hid.wait(act)
                    c = (g0 + d) % 2
                    hi.inc(fn(A2[:, bass.ds(j * 2, 2), 0:L], cross[:, c], ACT.Copy))

                def down(j, d, q=0, nxt=True):
                    pair(q * 16 + j + (g0 + 8), (g0 + d) % 2, nxt=nxt)

                double_pairs(act, 8, up, (hi, 2), (hid, 2), first=2)
                double_pairs(act, 8, down)
                with trips(act, QTR - 2, (hi, 8), (hid, 8)) as q:
                    double_pairs(act, 8, lambda j, d: up(j, d, q + 1, False), (hi, 2), (hid, 2))
                    double_pairs(act, 8, lambda j, d: down(j, d, q + 1))
                double_pairs(act, 8, lambda j, d: up(j, d, QTR - 1, False), (hi, 2), (hid, 2))
                xf.skip(8 * (QTR - 1))
                if not final:
                    double_pairs(act, 8, lambda j, d: down(j, d, QTR - 1))
                    xf.skip(8)
                else:
                    double_pairs(act, 8, lambda j, d: down(j, d, QTR - 1, nxt=not (isinstance(j, int) and j == 7)),
                                 last=2)

            mlp(P_MLP0, G_MIX1, False)
            if stop < 3:
                return

            rms()
            act.preload_act_table(ACT.Gelu_apprx_tanh)
            act.wait_ge(bc_loaded, 48)
            act.wait_ge(bx_zero, 1)

            def s5_masks(c, b):
                if not isinstance(c, int) or c >= 2:
                    act.wait_ge(s5_tr, c - 1)
                for g in range(2):
                    half = slice(64 * g, 64 * g + 64)
                    fn(bx[half, b, :, :, g, :].rearrange("p k j h -> p (k j) h"),
                       bch[half, bass.ds(c, 1), :].rearrange("p o (m h) -> p (o m) h", h=SH), ACT.Copy)
                for g in range(2):
                    last = fn(cx[:, b, :, 64 * g:64 * g + 64],
                              craw[:, :, bass.ds(c, 1), :].rearrange("p k o n -> p (k o) n"), ACT.Copy,
                              scale=par[:, g:g + 1])
                last.then_inc(s5_mask, 1)

            def s5_stationary(c, b):
                act.wait_ge(s5_tr, c + 1)
                fn(lhs5[:, b].rearrange("p k n -> p (k n)"), px[:, 2, :], ACT.Copy)
                fn(ncim[:, b].rearrange("p k n -> p (k n)"), px[:, 2, 2 * P:], ACT.Copy, scale=-1.0)\
                    .then_inc(s5_neg, 1)

            def s5_gelu(c, b):
                act.wait_ge(s5_yf, c + 1)
                fn(yb[:, b], yb[:, b], ACT.Gelu_apprx_tanh).then_inc(s5_ge, 1)
                act.wait_ge(s5_ge, c + 1)
                hi.inc(fn(A2[:, bass.ds(c, 1), 0:L], yb[:, b:b + 1], ACT.Copy))

            s5_masks(0, 0)
            s5_stationary(0, 0)
            s5_masks(1, 1)

            def s5_chunk(c, b, gelu=True, more=2):
                if more >= 1:
                    s5_stationary(c + 1, 1 - b)
                if gelu:
                    s5_gelu(c - 1, 1 - b)
                if more >= 2:
                    s5_masks(c + 2, b)

            s5_chunk(0, 0, gelu=False)
            s5_chunk(1, 1)
            with trips(act, KC // 2 - 2, (hi, 2)) as i:
                s5_chunk(i * 2 + 2, 0)
                s5_chunk(i * 2 + 3, 1)
            s5_chunk(KC - 2, 0, more=1)
            s5_chunk(KC - 1, 1, more=0)
            s5_gelu(KC - 1, 1)
            if stop < 4:
                return

            act.preload_act_table(ACT.Sigmoid)

            def glu(j, d):
                c = (P_GLU + d) % 2
                pair(j + P_GLU, c)
                if d == 1:
                    act.wait_ge(pair_read, j + (P_GLU + 1))
                    gate.inc(fn(cross[:, c], cross[:, c], ACT.Sigmoid))
                    xf.wait(act)
                    for k in range(2):
                        last = fn(A1[:, bass.ds(j + (k - 1), 1), 0:L], xT[:, bass.ds(j + (k - 1), 1), :], ACT.Copy,
                                  scale=gain(j + (G_FF1 + k - 1)))
                    hi.inc(last)
            double_pairs(act, 16, glu, (hi, 1), (xf, 1), (gate, 1))
            mlp(P_MLP1, None, True)

            for i in range(KC // 2):
                act.wait_ge(out_t, i + 1)
                fn(xin.rearrange("p a (i d) -> p a i d", i=8)[:, :, i, :],
                   px[:, i % 2, :].rearrange("p (a d) -> p a d", a=2), ACT.Copy).then_inc(out_c, 1)

        @block.vector
        def _(dve):
            tt, ts, stt = nc.vector.tensor_tensor, nc.vector.tensor_scalar, nc.vector.scalar_tensor_tensor
            seq = Tally(dve_seq)
            hi = Tally(op_hi)
            sums = Tally(rms_sum)
            root = Tally(rms_root)
            gate = Tally(gated)

            def link(ins):
                seq.inc(ins)
                seq.again(dve)

            dve.wait_ge(par_t, 1)
            row = px[:, 3]
            nc.vector.tensor_copy(pcol[:, :], row[:, 0:N_PCOL])
            nc.vector.tensor_copy(pcol2[:, :], row[:, 120:120 + N_PCOL2])
            nc.vector.tensor_copy(lcol[:, :, :], row[:, 146:146 + P].rearrange("p (k j) -> p k j", k=2))
            nc.vector.tensor_copy(scol[:, :], row[:, 274:274 + NT + LC]).then_inc(par_ready, 1)
            dve.wait_ge(par_ready, 1)
            dve.wait_ge(consts, 1)
            idv = ident.rearrange("p (a g h) -> p g a h", g=2, h=SH)
            link(nc.vector.tensor_reduce(par[:, :], idv, AX.XY, ALU.add))
            link(ts(ls[:, 1, :], pcol2[:, C_LAM:C_LAM + LC], -1.0, None, ALU.mult))
            tt(ls[:, 0, :], ls[:, 1, :], pcol2[:, C_LAM:C_LAM + LC], ALU.max).then_inc(s5_arg, 1)

            for i in range(KC // 2):
                hi.wait(dve)
                for c in range(2):
                    k = 2 * i + c
                    last = stt(A1[:, k, L:2 * L], xT[:, k, :], gain(G_MIX0 + k), A1[:, k, 0:L].bitcast(F32),
                               ALU.mult, ALU.subtract)
                last.then_inc(a1_ready, 1)

            def split(g, s):
                dve.wait_ge(hi_split, g * NU + (s + 1))
                tt(Wl[:, s], raw[:, s], Wh[:, s].bitcast(F32), ALU.subtract).then_inc(lo_split, 1)

            for s in range(NU):
                split(0, s)

            W = [s5w[:, k, :] for k in range(20)]
            step, a, hb, tmp, s2, c2, ac, ea, th = W[:9]
            lre, lim = lcol[:, 0, :], lcol[:, 1, :]
            dve.wait_ge(s5_exp, 1)
            link(tt(a, lre, step, ALU.mult))
            link(tt(hb, lim, step, ALU.mult))
            link(ts(hb, hb, 0.5, None, ALU.mult))
            link(ts(ac, a, -1.0, 1.0, ALU.max, ALU.min))
            for out_, turn in ((s2, 0.0), (c2, 0.25)):
                link(ts(tmp, hb, TWO_PI_INV, turn, ALU.mult, ALU.add))
                link(ts(tmp, tmp, MAGIC, None, ALU.add))
                link(ts(tmp, tmp, -MAGIC, None, ALU.add))
                link(stt(out_, tmp, -PI_HI, hb, ALU.mult, ALU.add))
                link(stt(out_, tmp, -PI_MID, out_, ALU.mult, ALU.add))
                link(stt(out_, tmp, -PI_LO, out_, ALU.mult, ALU.add))
                link(ts(out_, out_, 2.0 * math.pi * turn, None, ALU.add))
                link(ts(out_, out_, -PI_CLAMP, PI_CLAMP, ALU.max, ALU.min))
            ts(tmp, tmp, 0.0, None, ALU.mult).then_inc(s5_arg, 1)
            dve.wait_ge(s5_arg, 2)

            dve.wait_ge(s5_exp, 2)
            S = [ls[:, k, :] for k in range(6)]
            link(ts(S[2], S[1], 2.0, None, ALU.add))
            link(nc.vector.reciprocal(S[2], S[2]))
            link(tt(S[2], S[1], S[2], ALU.mult))
            link(tt(S[3], S[2], S[2], ALU.mult))
            link(ts(S[4], S[3], 1.0 / 15, 1.0 / 13, ALU.mult, ALU.add))
            for k in (11, 9, 7, 5, 3, 1):
                link(tt(S[4], S[4], S[3], ALU.mult))
                link(ts(S[4], S[4], 1.0 / k, None, ALU.add))
            link(tt(S[4], S[4], S[2], ALU.mult))
            link(ts(S[5], pcol2[:, C_LAM:C_LAM + LC], -1.0, 0.0, ALU.mult, ALU.max))
            link(stt(S[4], S[4], 2.0, S[5], ALU.mult, ALU.add))
            link(ts(S[4], S[4], LRU_C, None, ALU.mult))
            link(ts(S[5], S[4], -1.0, None, ALU.mult))

            em1, mask, t1, t2_, sinb, cosb, X, Y = W[9:17]
            link(ts(t1, th, -1.0, 1.0, ALU.mult, ALU.add))
            link(nc.vector.reciprocal(t1, t1))
            link(tt(t1, t1, th, ALU.mult))
            link(ts(mask, a, -1.0, None, ALU.is_gt))
            link(ts(t2_, a, 1.0, None, ALU.is_lt))
            link(tt(mask, mask, t2_, ALU.mult))
            link(ts(em1, ea, -1.0, None, ALU.add))
            link(stt(t1, t1, 2.0, em1, ALU.mult, ALU.subtract))
            link(tt(t1, t1, mask, ALU.mult))
            link(tt(em1, em1, t1, ALU.add))
            link(ts(rho[:, :], em1, 1.0, None, ALU.add))
            link(tt(t1, s2, s2, ALU.mult))
            link(ts(t1, t1, 2.0, None, ALU.mult))
            link(ts(cosb, t1, -1.0, 1.0, ALU.mult, ALU.add))
            link(tt(sinb, s2, c2, ALU.mult))
            link(ts(sinb, sinb, 2.0, None, ALU.mult))
            link(nc.vector.tensor_copy(rot1[:, 0, :], cosb))
            link(nc.vector.tensor_copy(rot1[:, 1, :], sinb))
            link(tt(X, em1, cosb, ALU.mult))
            link(tt(X, X, t1, ALU.subtract))
            link(tt(Y, rho[:, :], sinb, ALU.mult))
            cr, ci, n2 = W[17], W[18], W[19]
            link(tt(n2, lre, lre, ALU.mult))
            link(tt(t1, lim, lim, ALU.mult))
            link(tt(n2, n2, t1, ALU.add))
            link(nc.vector.reciprocal(n2, n2))
            link(tt(cr, X, lre, ALU.mult))
            link(tt(t1, Y, lim, ALU.mult))
            link(tt(cr, cr, t1, ALU.add))
            link(tt(cr, cr, n2, ALU.mult))
            link(tt(ci, Y, lre, ALU.mult))
            link(tt(t1, X, lim, ALU.mult))
            link(tt(ci, ci, t1, ALU.subtract))
            tt(ci, ci, n2, ALU.mult).then_inc(s5_small, 1)

            def inv_root(v, r, w):
                link(nc.vector.reciprocal(r, r))
                link(tt(w, r, r, ALU.mult))
                link(tt(w, w, v, ALU.mult))
                link(ts(w, w, -0.5, 1.5, ALU.mult, ALU.add))
                link(tt(r, r, w, ALU.mult))

            def rms():
                sums.wait(dve)
                ts(nv[:, :], px[:, 3, 0:L], 1.0 / D, EPS, ALU.mult, ALU.add).then_inc(rms_var, 1)
                root.wait(dve)
                inv_root(nv[:, :], rs[:, :], nw[:, :])

            rs2 = rs[:, :].unsqueeze(1).to_broadcast([P, 2, L])

            def pair(g, d, nxt=True, before=None):
                if nxt:
                    for s in range(NU):
                        split(g + 1, s)
                if before:
                    before()
                dve.wait_ge(crossed, g + 1)
                tt(cross[:, d], ps[:, 2 * d:2 * d + 2, 0:L], cross[:, d], ALU.add).then_inc(pair_read, 1)
                dve.wait_ge(pair_read, g + 1)

            def projection(g, d, dest, **kw):
                pair(g, d, **kw)
                link(tt(dest, cross[:, d], rs2, ALU.mult))

            def residual(j, d):
                xs = xT[:, bass.ds(j * 2, 2), :]
                tt(xs, xs, cross[:, d], ALU.add).then_inc(x_final, 1)

            def operand_from_x(j, col):
                hi.wait(dve)
                for c in range(2):
                    k = bass.ds(j + c, 1)
                    last = stt(A1[:, k, L:2 * L], xT[:, k, :], gain(j + (col + c)), A1[:, k, 0:L].bitcast(F32),
                               ALU.mult, ALU.subtract)
                last.then_inc(a1_ready, 1)

            projection(0, 0, qT[:, 0:2, :], before=rms)
            projection(1, 1, qT[:, 2:4, :])
            projection(2, 0, qT[:, 4:6, :])
            projection(3, 1, qT[:, 6:8, :])
            projection(P_KV, 0, kvT[:, :, :])
            double_pairs(dve, 4, lambda j, d: projection(j + P_XB, (P_XB + d) % 2,
                                                         xb[:, bass.ds(j * 2, 2), 3:3 + L]), (seq, 2))
            double_pairs(dve, 4, lambda j, d: projection(j + P_GT, (P_GT + d) % 2,
                                                         gT[:, bass.ds(j * 2, 2), :]), (seq, 2))
            if stop < 1:
                return

            link(tt(qt[:, 0:LC], qT[:, :, :], qT[:, :, :], ALU.mult))
            tt(qt[:, LC], kvT[:, 0], kvT[:, 0], ALU.mult).then_inc(qk_sq, 1)
            dve.wait_ge(qk_sum, 1)
            for i in range(4):
                ts(qv[:, 2 * i:2 * i + 2], px[:, i, :].rearrange("p (c t) -> p c t", c=2), 1.0 / HD, EPS,
                   ALU.mult, ALU.add)
            ts(qv[:, LC], ps[:, 0, 0:L], 1.0 / HD, EPS, ALU.mult, ALU.add).then_inc(qk_var, 1)
            dve.wait_ge(qk_root, 1)
            inv_root(qv[:, :, :], qr[:, :, :], qt[:, :, :])
            link(stt(kvT[:, 0], kvT[:, 0], pcol2[:, C_KG:C_KG + 1], qr[:, LC], ALU.mult, ALU.mult))
            nc.vector.tensor_copy(kd[0:64, 0, :], kvT[0:64, 0, :])
            nc.vector.tensor_copy(kd[64:P, 1, :], kvT[64:P, 0, :]).then_inc(kd_ready, 1)
            dve.wait_ge(v_t, 1)
            nc.vector.tensor_copy(vw[:, :, :], ps[:, 1, 0:3 * P].rearrange("p (w n) -> p w n", w=3)).then_inc(v_ready, 1)
            stt(qT[:, :, :], qT[:, :, :], pcol2[:, C_QG:C_QG + 1], qr[:, 0:LC], ALU.mult, ALU.mult).then_inc(qk_norm, 1)

            def softmax_max(i):
                d = i % 2
                dve.wait_ge(scored, i + 1)
                s = px[:, d, :].rearrange("p (n k) -> p n k", n=NCH)
                nc.vector.reduce_max(am[:, d, 0, 0:1], s[:, 0, 0:CH], AX.X)
                link(nc.vector.reduce_max(am[:, d, 0, 1:NCH], s[:, 1:NCH], AX.X))
                link(ts(am[:, d, 0, :], am[:, d, 0, :], HD ** -0.5, scol[:, NT + i:NT + i + 1], ALU.mult, ALU.max))
                ts(am[:, d, 1, :], am[:, d, 0, :], -1.0, None, ALU.mult).then_inc(maxed, 1)

            def softmax_norm(i):
                d = i % 2
                dve.wait_ge(expd, i + 1)
                link(tt(am[:, d, 4, :], am[:, d, 2, :], am[:, d, 3, :], ALU.add))
                link(nc.vector.reciprocal(am[:, d, 4, :], am[:, d, 4, :]))
                tt(pb[:, d, 0, 0:CH], pb[:, d, 0, 0:CH], am[:, d, 4, 0:1].to_broadcast([P, CH]), ALU.mult)
                tt(pb[:, d, 1:NCH], pb[:, d, 1:NCH], am[:, d, 4, 1:NCH].unsqueeze(2).to_broadcast([P, NCH - 1, P]),
                   ALU.mult).then_inc(probs, 1)

            softmax_max(0)
            for i in range(LC):
                if i + 1 < LC:
                    softmax_max(i + 1)
                softmax_norm(i)
                hi.wait(dve)
                tt(A2[:, LC + i, L:2 * L], px[:, 3, 0:L], A2[:, LC + i, 0:L].bitcast(F32), ALU.subtract)\
                    .then_inc(a2_ready, 1)

            link(nc.vector.memset(xb[:, :, 0:3], 0.0))
            for c in range(LC):
                w = [pcol[:, C_CW + k * LC + c:C_CW + k * LC + c + 1] for k in range(4)]
                link(ts(xc[:, c], xb[:, c, 0:L], w[0], pcol[:, C_CB + c:C_CB + c + 1], ALU.mult, ALU.add))
                for k in range(1, 4):
                    ins = stt(xc[:, c], xb[:, c, k:k + L], w[k], xc[:, c], ALU.mult, ALU.add)
                    if k < 3:
                        link(ins)
                ins.then_inc(conv_done, 1)
            ts(am[:, 0, 0, :], am[:, 0, 0, :], 0.0, None, ALU.mult).then_inc(lru_sp, 1)
            dve.wait_ge(gates_sg, LC)
            link(tt(li[:, :, :], li[:, :, :], xc[:, :, :], ALU.mult))
            for c in range(LC):
                dve.wait_ge(lru_a, c + 1)
                link(ts(xc[:, c], lt[:, c], 1.0, None, ALU.add))
                link(nc.vector.reciprocal(xc[:, c], xc[:, c]))
                tt(lt[:, c], lt[:, c], xc[:, c], ALU.mult).then_inc(lru_m2, 1)
            for c in range(LC):
                dve.wait_ge(lru_m, c + 1)
                link(tt(li[:, c], li[:, c], lt[:, c], ALU.mult))
                link(nc.vector.tensor_tensor_scan(xc[:, c], lr[:, c], li[:, c], 0.0, ALU.mult, ALU.add))
                dve.wait_ge(lru_h, c + 1)
                tt(gT[:, c], gT[:, c], xc[:, c], ALU.mult).then_inc(lru_y, 1)
            for c in range(LC):
                hi.wait(dve)
                tt(A2[:, c, L:2 * L], gT[:, c], A2[:, c, 0:L].bitcast(F32), ALU.subtract).then_inc(a2_ready, 1)
            if stop < 2:
                return

            def out_pair(j, d):
                c = (P_OUT + d) % 2
                pair(j + P_OUT, c)
                residual(j, c)
                operand_from_x(j * 2, G_FF0)
            double_pairs(dve, 8, out_pair, (hi, 2))

            def mlp(g0, final):
                def up(j, d, q=0, quarter0=True):
                    c = (g0 + d) % 2
                    pair(q * 16 + j + g0, c, before=rms if quarter0 and isinstance(j, int) and j == 0 else None)
                    link(tt(cross[:, c], cross[:, c], rs2, ALU.mult))
                    stt(cross[:, c], cross[:, c], 0.0, cross[:, c], ALU.max, ALU.mult).then_inc(hid_ready, 1)
                    hi.wait(dve)
                    k = bass.ds(j * 2, 2)
                    tt(A2[:, k, L:2 * L], cross[:, c], A2[:, k, 0:L].bitcast(F32), ALU.subtract).then_inc(a2_ready, 1)

                def down(j, d, q=0, nxt=True):
                    c = (g0 + d) % 2
                    pair(q * 16 + j + (g0 + 8), c, nxt=nxt)
                    residual(j, c)

                double_pairs(dve, 8, up, (hi, 2), (seq, 2), first=2)
                double_pairs(dve, 8, down)
                with trips(dve, QTR - 2, (hi, 8), (seq, 8)) as q:
                    double_pairs(dve, 8, lambda j, d: up(j, d, q + 1, False), (hi, 2), (seq, 2))
                    double_pairs(dve, 8, lambda j, d: down(j, d, q + 1))
                double_pairs(dve, 8, lambda j, d: up(j, d, QTR - 1, False), (hi, 2), (seq, 2))
                double_pairs(dve, 8, lambda j, d: down(j, d, QTR - 1,
                                                       nxt=not (final and isinstance(j, int) and j == 7)), last=2)

            mlp(P_MLP0, False)
            if stop < 3:
                return

            rms()

            def s5_u(c, b):
                k = bass.ds(c, 1)
                if not isinstance(c, int) or c >= 2:
                    dve.wait_ge(s5_yf, c - 1)
                stt(uc[:, b:b + 1], xT[:, k, :], gain(c + G_MIX1), rs[:, :].unsqueeze(1), ALU.mult, ALU.mult)\
                    .then_inc(u_ready, 1)

            def comps(t):
                return t.unsqueeze(1).to_broadcast([P, 2, L])

            def s5_scan(t, tl, b):
                d = tl % 2
                dve.wait_ge(s5_z, t + 1)
                if not (isinstance(t, int) and t < 2):
                    dve.wait_ge(s5_sn, t - 1)
                for k in range(2):
                    last = nc.vector.tensor_tensor_scan(gb[:, d, k], rho[:, bass.ds(t, 1)].to_broadcast([P, L]),
                                                        zb[:, d, k], 0.0, ALU.mult, ALU.add)
                last.then_inc(s5_g, 1)
                dve.wait_ge(s5_g, t + 1)
                if not (isinstance(t, int) and t < 2):
                    dve.wait_ge(s5_y, t - 1)
                tt(cdb[:, d, 0], gb[:, d], comps(tab[:, b, 0, tl % TPC]), ALU.mult).then_inc(s5_cs, 1)

            def s5_finish(c, b):
                dve.wait_ge(s5_y, c * TPC + TPC)
                stt(yb[:, b], uc[:, b], gain(c + C_D), ps[:, b, 0:L], ALU.mult, ALU.add).then_inc(s5_yf, 1)

            def s5_lo(c, b):
                hi.wait(dve)
                k = bass.ds(c, 1)
                tt(A2[:, k, L:2 * L], yb[:, b:b + 1], A2[:, k, 0:L].bitcast(F32), ALU.subtract).then_inc(a2_ready, 1)

            def s5_trip(i, first=False, more=True):
                for tl in range(2 * TPC):
                    t, b = i * (2 * TPC) + tl, tl // TPC
                    c = i * 2 + b
                    if tl % TPC == 1:
                        if not (first and b == 0):
                            s5_finish(c - 1, 1 - b)
                        if b == 0 or more:
                            s5_u(c + 1, 1 - b)
                    if tl + 1 < 2 * TPC:
                        s5_rotate_at(t + 1, tl + 1, i, (tl + 1) // TPC)
                    elif more:
                        s5_rotate_at(t + 1, 0, i + 1, 0)
                    if tl % TPC == 2 and not (first and b == 0):
                        s5_lo(c - 1, 1 - b)
                    s5_scan(t, tl, b)

            def s5_rotate_at(t, tl, i, b):
                if tl % TPC == 0:
                    dve.wait_ge(tab_loaded[b], i * 16 + 16)
                d = tl % 2
                dve.wait_ge(s5_bu, t + 1)
                if not (isinstance(t, int) and t < 2):
                    dve.wait_ge(s5_z, t - 1)
                bu = bu_bank(tl).rearrange("p (k t) -> p k t", k=2)
                for w in range(2):
                    last = tt(ab[:, d, w], bu, comps(tab[:, b, w, tl % TPC]), ALU.mult)
                last.then_inc(s5_rot, 1)

            s5_u(0, 0)
            s5_rotate_at(0, 0, 0, 0)
            s5_trip(0, first=True)
            with trips(dve, KC // 2 - 2, (hi, 2)) as i:
                s5_trip(i + 1)
            s5_trip(KC // 2 - 1, more=False)
            s5_finish(KC - 1, 1)
            s5_lo(KC - 1, 1)
            if stop < 4:
                return

            def glu(j, d):
                c = (P_GLU + d) % 2
                pair(j + P_GLU, c)
                if d == 1:
                    gate.wait(dve)
                    link(tt(cross[:, c], cross[:, c], cross[:, 1 - c], ALU.mult))
                    xs = xT[:, bass.ds(j - 1, 2), :]
                    tt(xs, xs, cross[:, c], ALU.add).then_inc(x_final, 1)
                    operand_from_x(j - 1, G_FF1)
            double_pairs(dve, 16, glu, (hi, 1), (seq, 1), (gate, 1))
            mlp(P_MLP1, True)

        @block.gpsimd
        def _(pool):
            tt = nc.gpsimd.tensor_tensor
            seq = Tally(pool_seq)
            xf = Tally(x_final)

            def link(ins):
                seq.inc(ins)
                seq.again(pool)

            link(nc.gpsimd.memset(ident[:, :], 0.0))
            link(nc.gpsimd.memset(ones[:, :], 1.0))
            link(nc.gpsimd.memset(hones[:, :], 0.0))
            link(nc.gpsimd.memset(hones[0:64, 0:64], 1.0))
            link(nc.gpsimd.memset(hones[64:P, 64:P], 1.0))
            nc.gpsimd.affine_select(out=ident[:, :], in_=ident[:, :], compare_op=ALU.not_equal, fill=1.0, base=0,
                                    pattern=[[-1, P]], channel_multiplier=1).then_inc(consts, 1)
            nc.gpsimd.memset(wax[:, :, :, :], 0.0).then_inc(zeroed, 1)

            def zero_squares():
                link(nc.gpsimd.memset(ss[:, :, :], 0.0))

            sqd = Tally(squared)

            def add_squares(xs):
                sqd.again(pool) if not (isinstance(sqd.value, int) and sqd.value == 0) else None
                link(tt(sq[:, :, :], xs, xs, ALU.mult))
                sqd.inc(tt(ss[:, :, :], ss[:, :, :], sq[:, :, :], ALU.add))

            zero_squares()
            for i in range(KC // 2):
                pool.wait_ge(op_hi, i + 1)
                add_squares(xT[:, 2 * i:2 * i + 2, :])
            pool.wait_ge(s5_small, 1)
            pool.wait_ge(b_loaded, 32)
            cr = s5w[:, 17, :].unsqueeze(2).to_broadcast([P, NT, SH])
            ci = s5w[:, 18, :].unsqueeze(2).to_broadcast([P, NT, SH])
            for k, (u, v, op) in enumerate(((cr, ci, ALU.subtract), (ci, cr, ALU.add))):
                link(tt(btmp[:, 0], braw[:, 0], u, ALU.mult))
                link(tt(btmp[:, 1], braw[:, 1], v, ALU.mult))
                t = btmp.rearrange("p k (c j) h -> p k c j h", c=KC)
                link(tt(bbar[:, :, k], t[:, 0], t[:, 1], op))
            pool.dma_start(bbar_d.rearrange("c p f -> p c f"), bbar.rearrange("p c k j h -> p c (k j h)"))\
                .then_inc(bbar_stored, 16)

            def tables(i, stored):
                if stored:
                    pool.wait_ge(tab_stored, i * 16)
                link(nc.gpsimd.tensor_copy(ctab[:, :, :, 0], rot1[:, :, bass.ds(i * 2, 2)]))
                n = 1
                while n < L:
                    a, b = ttmp[:, 0, :, :, 0:n], ttmp[:, 1, :, :, 0:n]
                    turn = [ctab[:, k, :, n - 1:n].unsqueeze(1).to_broadcast([P, 2, 2, n]) for k in range(2)]
                    link(tt(a, ctab[:, :, :, 0:n], turn[0], ALU.mult))
                    link(tt(b, ctab[:, :, :, 0:n], turn[1], ALU.mult))
                    link(tt(ctab[:, 0, :, n:2 * n], a[:, 0], b[:, 1], ALU.subtract))
                    link(tt(ctab[:, 1, :, n:2 * n], a[:, 1], b[:, 0], ALU.add))
                    n *= 2

            def store(c, h):
                pool.dma_start(tab_d[bass.ds(c, 1)].rearrange("o p (k j t) -> p (o k) j t", k=2, j=TPC)
                               [:, :, 2 * h:2 * h + 2, :], ctab[:, :, :, :]).then_inc(tab_stored, 16)

            STEPS = 1 + 4 * 8
            EARLY = 6

            def table_chunks(first, n):
                with trips(pool, n, (seq, 2 * STEPS)) as c:
                    for h in range(2):
                        tables(c * 2 + (2 * first + h), True)
                        store(c + first, h)

            for h in range(2):
                tables(h, h > 0)
                store(0, h)
            table_chunks(1, EARLY - 1)

            def norm_squares(count, skip):
                pool.wait_ge(rms_sum, count - 1)
                xf.skip(skip)
                zero_squares()
                with trips(pool, KC // 2, (xf, 1), (seq, 1), (sqd, 1)) as i:
                    xf.wait(pool)
                    add_squares(xT[:, bass.ds(i * 2, 2), :])

            norm_squares(2, 0)
            table_chunks(EARLY, KC - EARLY)
            nc.gpsimd.memset(bx[:, :, :, :, :, :], 0.0).then_inc(bx_zero, 1)
            norm_squares(3, 8 * (QTR - 1))
            if stop < 3:
                return

            def s5_z_of(t, tl):
                d = tl % 2
                pool.wait_ge(s5_rot, t + 1)
                if not (isinstance(t, int) and t < 2):
                    pool.wait_ge(s5_g, t - 1)
                tt(zb[:, d, 0], ab[:, d, 0, 0], ab[:, d, 1, 1], ALU.add)
                tt(zb[:, d, 1], ab[:, d, 0, 1], ab[:, d, 1, 0], ALU.subtract).then_inc(s5_z, 1)

            def s5_sin(t, tl, b):
                d = tl % 2
                pool.wait_ge(s5_g, t + 1)
                if not (isinstance(t, int) and t < 2):
                    pool.wait_ge(s5_y, t - 1)
                tt(cdb[:, d, 1], gb[:, d], tab[:, b, 1, tl % TPC].unsqueeze(1).to_broadcast([P, 2, L]), ALU.mult)\
                    .then_inc(s5_sn, 1)

            def s5_trip(i, more=True):
                for tl in range(2 * TPC):
                    t = i * (2 * TPC) + tl
                    if tl + 1 < 2 * TPC or more:
                        s5_z_of(t + 1, tl + 1)
                    s5_sin(t, tl, tl // TPC)

            s5_z_of(0, 0)
            s5_trip(0)
            with pool.Fori(1, KC // 2 - 1) as i:
                s5_trip(i)
            s5_trip(KC // 2 - 1, more=False)
            if stop < 4:
                return
            norm_squares(4, 0)


_INS = ["x", "mix_norm_e", "w_in_e", "conv_w", "conv_b", "lru_wa", "lru_ba", "lru_wx", "lru_bx", "lru_lambda",
        "q_gain", "k_gain", "sinks", "w_out_e", "mix_norm_o", "s5_lam_re", "s5_lam_im", "s5_log_step",
        "s5_b_re", "s5_b_im", "s5_c_re", "s5_c_im", "s5_d", "w_glu", "ffn_norm", "w_up", "w_down"]
_OUTS = [((1, L, D), "float32")]


def kernel(**inputs):
    import numpy as _np
    import concourse.bacc as _bacc
    from concourse import mybir as _mybir
    from concourse.bass_utils import run_bass_kernel_spmd as _run

    nc = _bacc.Bacc("TRN2", target_bir_lowering=False, num_devices=1)
    arrays, args = {}, []
    for name in _INS:
        a = _np.ascontiguousarray(inputs[name])
        arrays[f"in_{name}_dram"] = a
        args.append(nc.dram_tensor(f"in_{name}_dram", a.shape, _mybir.dt.from_np(a.dtype), kind="ExternalInput").ap())
    for i, (shape, dtype) in enumerate(_OUTS):
        dt = _mybir.dt.from_np(_np.dtype(dtype))
        args.append(nc.dram_tensor(f"out_{i}_dram", shape, dt, kind="ExternalOutput").ap())
    trunk_kernel(nc, *args)
    r = _run(nc, [arrays], core_ids=[0])
    got = tuple(r.results[0][f"out_{i}_dram"] for i in range(len(_OUTS)))
    return got[0]
```

```python
from contextlib import ExitStack, contextmanager
import math

import concourse.bass as bass
from concourse import mybir

F32 = mybir.dt.float32
F32R = mybir.dt.float32r
ACT = mybir.ActivationFunctionType
ALU = mybir.AluOpType
AX = mybir.AxisListType

P = 128
D = 2048
L = 256
KC = D // P
EPS = 1e-6
DL = D // 2
LC = DL // P
NKV = 2
NH = 2 * LC + NKV
HD = 64
CH = 64
NCH = L // CH
QKV0 = 2 * DL
LRU_C = 8.0
FF = 4 * D
QTR = FF // D
UK = 4
NU = KC // UK
TW = 2 * P
NT = 64
TPC = 4
SH = 16
TROW = 2 * TPC * L + 2 * TPC * SH
TWO_PI_INV = 1.0 / (2.0 * math.pi)
MAGIC = 1.5 * 2.0 ** 23
PI_HI = 6.28125
PI_MID = 0.0019350051879882812
PI_LO = 2.0 * math.pi - PI_HI - PI_MID
PI_CLAMP = 3.1415925

P_Q = 0
P_KV = P_Q + 4
P_XB = P_KV + 1
P_GT = P_XB + 4
P_OUT = P_GT + 4
P_MLP0 = P_OUT + 8
P_GLU = P_MLP0 + 16 * QTR
P_MLP1 = P_GLU + 16
P_END = P_MLP1 + 16 * QTR

SLOT_SUM, SLOT_VAR, SLOT_ROOT, SLOT_INV, SLOT_WIDE, SLOT_Q = 1, 1, 2, 3, 4, 5
ATT0 = 7
GATE0 = ATT0 + 2 * LC + 1

G_MIX0, G_MIX1, G_FF0, G_FF1, C_D, C_CW, C_CB = 0, 16, 32, 48, 64, 80, 112
N_PCOL = 120
C_BA, C_BX, C_LAM, C_QG, C_KG = 0, 8, 16, 24, 25
N_PCOL2 = 26
N_PAR = 21


class Tally:

    def __init__(self, sem, value=0):
        self.sem, self.start, self.count, self.seen = sem, value, 0, 0

    @property
    def value(self):
        return self.start + self.count

    def skip(self, n):
        self.count += n
        self.seen += n

    def inc(self, ins):
        ins.then_inc(self.sem, 1)
        self.skip(1)

    def wait(self, eng, n=1):
        self.skip(n)
        eng.wait_ge(self.sem, self.value)

    def again(self, eng):
        eng.wait_ge(self.sem, self.value)


@contextmanager
def trips(eng, n, *per_trip):
    entry = [t.value for t, _ in per_trip]
    seen = [t.seen for t, _ in per_trip]
    with eng.Fori(0, n) as i:
        for (t, k), at in zip(per_trip, entry):
            t.start, t.count = at + i * k, 0
        yield i
        for (t, k), was in zip(per_trip, seen):
            assert t.seen - was == k, (t.sem, t.seen - was, k)
    for (t, k), at, was in zip(per_trip, entry, seen):
        t.start, t.count, t.seen = at + n * k, 0, was + n * k


def trunk_kernel(nc, x, mix_norm_e, w_in_e, conv_w, conv_b, lru_wa, lru_ba, lru_wx, lru_bx, lru_lambda,
                 q_gain, k_gain, sinks, w_out_e, mix_norm_o, s5_lam_re, s5_lam_im, s5_log_step,
                 s5_b_re, s5_b_im, s5_c_re, s5_c_im, s5_d, w_glu, ffn_norm, w_up, w_down, out, stop=99):
    w_in, w_out, w_gl = w_in_e[0], w_out_e[0], w_glu[0]
    ctx = ExitStack()
    with ctx:
        def sb(name, shape, dt=F32, on=ctx):
            return on.enter_context(nc.sbuf_tensor(name, shape, dt))

        def sem(name):
            return ctx.enter_context(nc.semaphore(name))

        tab_d = nc.dram_tensor("s5_tables", (KC, P, 2 * TPC * L), F32, kind="Internal").ap()
        bbar_d = nc.dram_tensor("s5_bbar", (KC, P, 2 * TPC * SH), F32, kind="Internal").ap()

        xT = sb("xT", [P, KC, L])
        with ExitStack() as o:
            lt = sb("lt", [P, LC, L], on=o)
            la = sb("la", [P, LC, L], on=o)
        with ExitStack() as o:
            tab = sb("tab", [P, 2, 2, TPC, L], on=o)
            bch = sb("bch", [P, KC, 2 * TPC * SH], on=o)
            craw = sb("craw", [P, 2, KC, HD], on=o)
        A1 = sb("A1", [P, KC, 2 * L], F32R)
        with ExitStack() as o:
            braw = sb("braw", [P, 2, NT, SH], on=o)
            btmp = sb("btmp", [P, 2, NT, SH], on=o)
            bbar = sb("bbar", [P, KC, 2, TPC, SH], on=o)
            s5w = sb("s5w", [P, 20, NT], on=o)
            prow = sb("prow", [N_PCOL, P], on=o)
            prow2 = sb("prow2", [N_PCOL2, P], on=o)
            lrow = sb("lrow", [P, P], on=o)
            srow = sb("srow", [1, 2 * NT + 2 * LC], on=o)
        with ExitStack() as o:
            xc = sb("xc", [P, LC, L], on=o)
            lr = sb("lr", [P, LC, L], on=o)
        A2 = sb("A2", [P, KC, 2 * L], F32R)
        raw = sb("raw", [P, NU, UK, TW])
        Wh = sb("Wh", [P, NU, UK, TW], F32R)
        Wl = sb("Wl", [P, NU, UK, TW], F32R)
        with ExitStack() as o:
            xin = sb("xin", [P, 2, D], on=o)
        with ExitStack() as o:
            ab = sb("ab", [P, 2, 2, 2, L], on=o)
            zb = sb("zb", [P, 2, 2, L], on=o)
            gb = sb("gb", [P, 2, 2, L], on=o)
            cdb = sb("cdb", [P, 2, 2, 2, L], on=o)
            yb = sb("yb", [P, 2, L], on=o)
            uc = sb("uc", [P, 2, L], on=o)
            bx = sb("bx", [P, 2, 2, TPC, 2, SH], on=o)
            cx = sb("cx", [P, 2, 2, P], on=o)
            lhs5 = sb("lhs5", [P, 2, 4, P], on=o)
            ncim = sb("ncim", [P, 2, 2, P], on=o)
        qT = sb("qT", [P, LC, L])
        kvT = sb("kvT", [P, 2, L])
        with ExitStack() as o:
            li = sb("li", [P, LC, L], on=o)
        xb = sb("xb", [P, LC, L + 3])
        gT = sb("gT", [P, LC, L])
        wax = sb("wax", [P, 2, LC, P])
        pb = sb("pb", [P, 2, NCH, P])
        pt = sb("pt", [P, 2, NCH, P])
        kd = sb("kd", [P, NKV, L])
        vw = sb("vw", [P, 3, P])
        with ExitStack() as o:
            rsel = sb("rsel", [NH, NH, HD], on=o)
        ctab = sb("ctab", [P, 2, 2, L])
        ttmp = sb("ttmp", [P, 2, 2, 2, L // 2])
        cross = sb("cross", [P, 2, 2, L])
        sq = sb("sq", [P, 2, L])
        ss = sb("ss", [P, 2, L])
        rs = sb("rs", [P, L])
        nv = sb("nv", [P, L])
        nw = sb("nw", [P, L])
        ident = sb("ident", [P, P])
        ones = sb("ones", [P, P])
        hsel = sb("hsel", [P, 34])
        pcol = sb("pcol", [P, N_PCOL])
        pcol2 = sb("pcol2", [P, N_PCOL2])
        lcol = sb("lcol", [P, 2, NT])
        scol = sb("scol", [P, NT + LC])
        rot1 = sb("rot1", [P, 2, NT])
        rho = sb("rho", [P, NT])
        ls = sb("ls", [P, 6, LC])
        par = sb("par", [P, 2])
        am = sb("am", [P, 2, 6, NCH])

        ps = ctx.enter_context(nc.psum_tensor("ps", [P, 4, 512], F32))
        px = ctx.enter_context(nc.psum_tensor("px", [P, 4, 512], F32))

        x_loaded = [sem(f"x_loaded{i}") for i in range(2)]
        par_loaded = sem("par_loaded")
        b_loaded = sem("b_loaded")
        wax_loaded = sem("wax_loaded")
        kd_loaded = sem("kd_loaded")
        landed = [sem(f"landed{s}") for s in range(NU)]
        tab_loaded = [sem(f"tab_loaded{s}") for s in range(2)]
        bc_loaded = sem("bc_loaded")
        tab_stored = sem("tab_stored")
        bbar_stored = sem("bbar_stored")
        out_stored = sem("out_stored")
        consts = sem("consts")
        hi_split = sem("hi_split")
        lo_split = sem("lo_split")
        unit_done = sem("unit_done")
        crossed = sem("crossed")
        pair_read = sem("pair_read")
        hid_ready = sem("hid_ready")
        op_hi = sem("op_hi")
        a1_ready = sem("a1_ready")
        a2_ready = sem("a2_ready")
        gated = sem("gated")
        x_final = sem("x_final")
        squared = sem("squared")
        rms_sum = sem("rms_sum")
        rms_var = sem("rms_var")
        rms_root = sem("rms_root")
        par_t = sem("par_t")
        par_ready = sem("par_ready")
        xt_done = sem("xt_done")
        dve_seq = sem("dve_seq")
        act_seq = sem("act_seq")
        pool_seq = sem("pool_seq")
        s5_exp = sem("s5_exp")
        s5_arg = sem("s5_arg")
        s5_small = sem("s5_small")
        bbar_ready = sem("bbar_ready")
        tab_made = sem("tab_made")
        lru_sp = sem("lru_sp"); lru_arg = sem("lru_arg"); conv_done = sem("conv_done"); xb_ready = sem("xb_ready"); g_ready = sem("g_ready")
        gates_mm = sem("gates_mm"); gates_sg = sem("gates_sg"); lru_a = sem("lru_a"); lru_m2 = sem("lru_m2")
        lru_m = sem("lru_m"); lru_h = sem("lru_h"); lru_y = sem("lru_y"); op_hi2 = sem("op_hi2")
        qk_sq = sem("qk_sq"); qk_sum = sem("qk_sum"); qk_var = sem("qk_var"); qk_root = sem("qk_root")
        qk_norm = sem("qk_norm"); kd_ready = sem("kd_ready"); qk_wide = sem("qk_wide"); q_normed = sem("q_normed"); v_t = sem("v_t"); v_ready = sem("v_ready")
        scored = sem("scored"); maxed = sem("maxed"); expd = sem("expd"); probs = sem("probs")
        p_t = sem("p_t"); p_copied = sem("p_copied"); att_o = sem("att_o")
        s5_bu = sem("s5_bu"); s5_rot = sem("s5_rot"); s5_z = sem("s5_z"); s5_g = sem("s5_g")
        s5_cs = sem("s5_cs"); s5_sn = sem("s5_sn"); s5_y = sem("s5_y"); s5_yf = sem("s5_yf"); s5_ge = sem("s5_ge")
        s5_mask = sem("s5_mask"); s5_tr = sem("s5_tr"); s5_lhs = sem("s5_lhs"); s5_neg = sem("s5_neg")
        bx_zero = sem("bx_zero"); u_ready = sem("u_ready"); out_t = sem("out_t"); out_c = sem("out_c"); zeroed = sem("zeroed")
        block = ctx.enter_context(nc.Block())

        def bu_bank(tl):
            return (px[:, 0], px[:, 1], ps[:, 2], ps[:, 3])[tl % 4]

        root18 = pb[0:NH, 0].rearrange("p n q -> p (n q)")[:, 0:L]

        def squares_of(j, c):
            return pt[:, j % 2].rearrange("p n q -> p (n q)")[:, c * L:c * L + L]

        def wide_root(half):
            return px[:, half // 2, (half % 2) * L:(half % 2) * L + L]

        def gain(col):
            return pcol[:, bass.ds(col, 1)]

        def double_pairs(eng, n_pairs, body, *per_pair, first=0, last=0):
            for j in range(first):
                body(j, j % 2)
            mid = (n_pairs - first - last) // 2
            if mid:
                with trips(eng, mid, *per_pair) as i:
                    body(i * 2 + first, 0)
                    body(i * 2 + (first + 1), 1)
            for j in range(n_pairs - last, n_pairs):
                body(j, j % 2)

        @block.sync
        def _(sp):
            for i in range(2):
                sp.dma_start(xin[:, i, :], x[0, i * P:(i + 1) * P, :]).then_inc(x_loaded[i], 16)

            def load_pair(g, wide, row0, col0, turn=0):
                for s in range(NU):
                    if not (isinstance(g, int) and g == 0):
                        sp.wait_ge(lo_split, (g - 1) * NU + (s + 1))
                    src = wide[bass.ds(row0 + (s + turn) % NU * UK * P, UK * P), bass.ds(col0, TW)]
                    sp.dma_start(raw[:, s], src.rearrange("(c p) n -> p c n", p=P)).then_inc(landed[s], 16)

            def load_mlp(g0, layer):
                with sp.Fori(0, QTR) as q:
                    with sp.Fori(0, 8) as j:
                        load_pair(q * 16 + j + g0, w_up[layer], 0, q * D + j * TW)
                    with sp.Fori(0, 8) as j:
                        load_pair(q * 16 + j + (g0 + 8), w_down[layer], q * D, j * TW)

            load_pair(0, w_in, 0, QKV0)
            with sp.Fori(1, 5) as j:
                load_pair(j + P_Q, w_in, 0, j * TW + QKV0)
            with sp.Fori(0, 8) as j:
                load_pair(j + P_XB, w_in, 0, j * TW)
            for j in range(8):
                load_pair(P_OUT + j, w_out, 0, j * TW, turn=2)
            load_mlp(P_MLP0, 0)
            for j in range(2):
                load_pair(P_GLU + j, w_gl, 0, j * D)
            sp.wait_ge(bbar_stored, 16)
            sp.dma_start(bch[:, :, :], bbar_d.rearrange("c p f -> p c f")).then_inc(bc_loaded, 16)
            for k, s5_c in enumerate((s5_c_re, s5_c_im)):
                rows = s5_c[0].rearrange("g h p -> (g h) p")
                sp.dma_start(craw[:, k], rows.rearrange("(c p) n -> p c n", p=P)).then_inc(bc_loaded, 16)

            def load_tables(c, b):
                if not isinstance(c, int):
                    sp.wait_ge(s5_yf, c - 1)
                sp.dma_start(tab[:, b].rearrange("p k j t -> p (k j t)"),
                             tab_d[bass.ds(c, 1)].rearrange("o p f -> p (o f)")).then_inc(tab_loaded[b], 16)

            sp.wait_ge(tab_stored, KC * 32)
            for c in range(2):
                load_tables(c, c)
            with sp.Fori(1, KC // 2) as i:
                for b in range(2):
                    load_tables(i * 2 + b, b)
            with sp.Fori(1, 8) as j:
                for h in range(2):
                    load_pair(j * 2 + (h + P_GLU), w_gl, 0, j * TW + h * D)
            load_mlp(P_MLP1, 1)
            with sp.Fori(0, KC // 2) as i:
                sp.wait_ge(out_c, i + 1)
                sp.dma_start(out[0].rearrange("(a p) d -> p a d", p=P)[:, :, bass.ds(i * TW, TW)],
                             xin.rearrange("p a (i d) -> p a i d", i=8)[:, :, bass.ds(i, 1), :]
                             .rearrange("p a o d -> p a (o d)")).then_inc(out_stored, 16)
            sp.wait_ge(out_stored, 16 * (KC // 2))

        @block.tensor
        def _(pe):
            mm = nc.tensor.matmul

            pe.wait_ge(consts, 1)
            pe.wait_ge(par_loaded, 16 * N_PAR)
            row = px[:, 3]
            nc.tensor.transpose(row[:, 0:N_PCOL], prow[:, :], ident[0:N_PCOL, 0:N_PCOL])
            nc.tensor.transpose(row[:, 120:120 + N_PCOL2], prow2[:, :], ident[0:N_PCOL2, 0:N_PCOL2])
            nc.tensor.transpose(row[:, 146:146 + P], lrow[:, :], ident[:, :])
            steps = srow[0:1, 0:2 * NT].rearrange("a (j g) -> a g j", g=2)
            snk = srow[0:1, 2 * NT:].rearrange("a (j g) -> a g j", g=2)
            for g in range(2):
                mm(row[64 * g:64 * g + 64, 274:274 + NT], ones[0:1, 0:64], steps[:, g], start=True, stop=True)
                last = mm(row[64 * g:64 * g + 64, 274 + NT:274 + NT + LC], ones[0:1, 0:64], snk[:, g],
                          start=True, stop=True)
            last.then_inc(par_t, 1)
            for i in range(2):
                pe.wait_ge(x_loaded[i], 16)
            for i in range(KC // 2):
                if i >= 3:
                    pe.wait_ge(op_hi, i - 2)
                for c in range(2):
                    for a in range(2):
                        last = nc.tensor.transpose(px[:, i % 3, c * L + a * P:c * L + a * P + P],
                                                   xin[:, a, bass.ts(2 * i + c, P)], ident[:, :])
                last.then_inc(xt_done, 1)

            def pair(g, d, A, ready=None, base=0, per_unit=0, turn=0, beside=None):
                b = 2 * d
                if not (isinstance(g, int) and g < 2):
                    pe.wait_ge(pair_read, g - 1)
                for s in range(NU):
                    pe.wait_ge(lo_split, g * NU + (s + 1))
                    if ready is not None:
                        pe.wait_ge(ready, base + per_unit * (s + 1))
                    for t in range(2):
                        for c in range(UK):
                            n = s * UK + c
                            k = (n + turn * UK) % KC
                            cols = slice(t * P, t * P + P)
                            wide = lambda: mm(ps[:, b + t, :], Wh[:, s, c, cols], A[:, k, :],
                                              start=(n == 0), stop=(n == KC - 1))
                            half = lambda: mm(ps[:, b + t, 0:L], Wl[:, s, c, cols], A[:, k, 0:L],
                                              start=False, stop=False)
                            if n == KC - 1:
                                half()
                                last = wide()
                            else:
                                wide()
                                last = half()
                    last.then_inc(unit_done, 1)
                    if beside:
                        beside(s)

            def channel_sum(n):
                pe.wait_ge(squared, 8 * n)
                mm(px[:, 3, 0:L], ones[:, :], ss[:, 0], start=True, stop=False)
                mm(px[:, 3, 0:L], ones[:, :], ss[:, 1], start=False, stop=True).then_inc(rms_sum, 1)

            def phase(g0, n, A, **ready):
                def body(j, d):
                    pair(j + g0, (g0 + d) % 2, A, **ready)
                double_pairs(pe, n, body)

            pair(0, 0, A1, a1_ready, 0, 2)
            pe.wait_ge(par_ready, 1)
            channel_sum(1)
            def head_sums(j):
                pe.wait_ge(qk_sq, j + 1)
                for c in range(2 if j < 4 else 1):
                    i = 2 * j + c
                    last = mm(px[0:NH, 3, L:2 * L], hsel[:, 16 - 2 * i:16 - 2 * i + NH], squares_of(j, c),
                              start=(i == 0), stop=(i == LC))
                last.then_inc(qk_sum, 1)

            for g in range(1, P_XB):
                pair(g, g % 2, A1)
                head_sums(g - 1)

            def values():
                for w in range(3):
                    last = nc.tensor.transpose(px[:, 2, w * P:w * P + P], kvT[:, 1, w * CH:w * CH + P], ident[:, :])
                last.then_inc(v_t, 1)

            def widen(i, half):
                return mm(px[:, half // 2, (half % 2) * L:(half % 2) * L + L],
                          rsel[:, 2 * i:2 * i + 2, :].rearrange("p h n -> p (h n)"), root18[:, :],
                          start=True, stop=True)

            def scores(i):
                if i == 0:
                    pe.wait_ge(q_normed, 2)
                    pe.wait_ge(kd_loaded, 32)
                if i >= 2:
                    pe.wait_ge(expd, i - 1)
                for n in range(NCH):
                    for h in range(2):
                        half = slice(64 * h, 64 * h + 64)
                        k0 = max(n - 1, 0) * CH
                        nk = P if n else CH
                        last = mm(px[half, i % 2, n * P:n * P + nk], qT[half, i, n * CH:n * CH + CH],
                                  kd[half, i // 4, k0:k0 + nk], start=True, stop=True)
                last.then_inc(scored, 1)

            def transpose_probs(i):
                pe.wait_ge(probs, i + 1)
                if i >= 1:
                    pe.wait_ge(p_copied, i)
                for n in range(NCH):
                    nk = P if n else CH
                    last = nc.tensor.transpose(px[0:nk, 2, n * P:n * P + P], pb[:, i % 2, n, 0:nk], ident[:, :])
                last.then_inc(p_t, 1)

            def weigh_values(i):
                pe.wait_ge(p_copied, i + 1)
                if i >= 1:
                    pe.wait_ge(a2_ready, i)
                for n in range(NCH):
                    for h in range(2):
                        nk = P if n else CH
                        last = mm(px[64 * h:64 * h + 64, 3, n * CH:n * CH + CH],
                                  vw[0:nk, max(n - 1, 0), 64 * (i // 4):64 * (i // 4) + 64],
                                  pt[0:nk, i % 2, n, 64 * h:64 * h + 64], start=True, stop=True)
                last.then_inc(att_o, 1)

            def gates(c):
                if c == 0:
                    pe.wait_ge(wax_loaded, 64)
                    pe.wait_ge(expd, LC)
                pe.wait_ge(conv_done, c // 2 + 1)
                if c >= 2:
                    pe.wait_ge(gates_sg, c - 1)
                for k in range(2):
                    last = mm(px[:, c % 2, k * L:k * L + L], wax[:, k, c, :], xc[:, c, :], start=True, stop=True)
                last.then_inc(gates_mm, 1)

            def beside(n):
                if n == SLOT_SUM:
                    head_sums(4)
                    values()
                if n == SLOT_WIDE:
                    pe.wait_ge(qk_norm, 1)
                    pe.wait_ge(zeroed, 2)
                    pe.wait_ge(v_ready, 1)
                    widen(LC, 7)
                    for i in range(LC - 1):
                        last = widen(i, i)
                    last.then_inc(qk_wide, 1)
                if n == SLOT_Q:
                    pe.wait_ge(q_normed, 1)
                    widen(LC - 1, 0).then_inc(qk_wide, 1)
                i, odd = divmod(n - ATT0, 2)
                if not odd and 0 <= i < LC:
                    scores(i)
                if not odd and 0 <= i - 2 < LC:
                    transpose_probs(i - 2)
                if odd and 0 <= i - 2 < LC:
                    weigh_values(i - 2)
                if 0 <= n - GATE0 < LC:
                    gates(n - GATE0)

            for g in range(P_XB, P_OUT):
                pair(g, g % 2, A1, beside=lambda s: beside((g - P_XB) * NU + s))
            if stop < 2:
                return

            pair(P_OUT, P_OUT % 2, A2, turn=2, ready=a2_ready, base=0, per_unit=4)
            double_pairs(pe, 7, lambda j, d: pair(j + (P_OUT + 1), (P_OUT + 1 + d) % 2, A2, turn=2), last=1)

            def mlp(g0, a1_at, a1_unit, a2_at, norm):
                def up(j, d, q=0, quarter0=True):
                    pair(q * 16 + j + g0, (g0 + d) % 2, A1, a1_ready, a1_at, a1_unit)
                    if quarter0 and isinstance(j, int) and j == 0:
                        channel_sum(norm)

                def down(j, d, q=0):
                    pair(q * 16 + j + (g0 + 8), (g0 + d) % 2, A2, a2_ready, q * 8 + a2_at, 2)

                double_pairs(pe, 8, up, first=2)
                double_pairs(pe, 8, down)
                with pe.Fori(1, QTR) as q:
                    double_pairs(pe, 8, lambda j, d: up(j, d, q, False))
                    double_pairs(pe, 8, lambda j, d: down(j, d, q))

            mlp(P_MLP0, 8, 2, 16, 2)
            if stop < 3:
                return

            channel_sum(3)
            pe.wait_ge(pair_read, P_GLU)

            def s5_prepare(c, b):
                pe.wait_ge(s5_mask, c + 1)
                for k in range(2):
                    nc.tensor.transpose(px[:, 2, k * P:k * P + P],
                                        bx[:, b, k].rearrange("p j g h -> p (j g h)"), ident[:, :])
                for k in range(2):
                    last = nc.tensor.transpose(px[:, 2, (2 + k) * P:(3 + k) * P], cx[:, b, k], ident[:, :])
                last.then_inc(s5_tr, 1)

            def s5_in(t, c, b, tl):
                if not isinstance(t, int) or t >= 4:
                    pe.wait_ge(s5_rot, t - 3)
                if tl == 0:
                    pe.wait_ge(s5_neg, c + 1)
                    pe.wait_ge(u_ready, c + 1)
                rows = slice(32 * tl, 32 * tl + 32)
                for k in range(2):
                    last = mm(bu_bank(tl)[:, k * L:k * L + L], lhs5[rows, b, k, :], uc[rows, b, :],
                              start=True, stop=True)
                last.then_inc(s5_bu, 1)

            def s5_out(t, b, tl):
                pe.wait_ge(s5_cs, t + 1)
                pe.wait_ge(s5_sn, t + 1)
                own = slice(32 * tl, 32 * tl + 32)
                y, d = ps[own, b, 0:L], tl % 2
                mm(y, lhs5[:, b, 2, own], cdb[:, d, 0, 0], start=True, stop=False)
                mm(y, ncim[:, b, 1, own], cdb[:, d, 0, 1], start=False, stop=False)
                mm(y, ncim[:, b, 0, own], cdb[:, d, 1, 1], start=False, stop=False)
                mm(y, ncim[:, b, 1, own], cdb[:, d, 1, 0], start=False, stop=True).then_inc(s5_y, 1)

            def s5_trip(i, more):
                for tl in range(2 * TPC):
                    t, c, b = i * (2 * TPC) + tl, i * 2 + tl // TPC, tl // TPC
                    n = tl + 3
                    if tl % TPC == 0 and (b == 0 or more):
                        s5_prepare(c + 1, 1 - b)
                    if n < 2 * TPC or more:
                        s5_in(t + 3, i * 2 + n // TPC, (n // TPC) % 2, n % TPC)
                    if tl % TPC == 0 and (not isinstance(c, int) or c >= 2):
                        pe.wait_ge(s5_yf, c - 1)
                    s5_out(t, b, tl % TPC)

            s5_prepare(0, 0)
            for tl in range(3):
                s5_in(tl, 0, 0, tl)
            s5_trip(0, True)
            with pe.Fori(1, KC // 2 - 1) as i:
                s5_trip(i, True)
            s5_trip(KC // 2 - 1, False)
            if stop < 4:
                return

            phase(P_GLU, 16, A2, ready=a2_ready, base=48, per_unit=4)
            mlp(P_MLP1, 16, 2, 64, 4)

            for i in range(KC // 2):
                pe.wait_ge(x_final, 73 + i)
                if i >= 2:
                    pe.wait_ge(out_c, i - 1)
                for a in range(2):
                    for c in range(2):
                        last = nc.tensor.transpose(px[:, i % 2, (2 * a + c) * P:(2 * a + c + 1) * P],
                                                   xT[:, 2 * i + c, a * P:a * P + P], ident[:, :])
                last.then_inc(out_t, 1)

        @block.scalar
        def _(act):
            fn = nc.scalar.activation
            def rows(col, src, n):
                act.dma_start(prow[col:col + n, :], src.rearrange("(c p) -> c p", p=P)).then_inc(par_loaded, 16)

            def rows2(col, src, n):
                act.dma_start(prow2[col:col + n, :], src.rearrange("(c p) -> c p", p=P)).then_inc(par_loaded, 16)

            rows(G_MIX0, mix_norm_e[0], KC)
            rows(G_MIX1, mix_norm_o[0], KC)
            rows(G_FF0, ffn_norm[0], KC)
            rows(G_FF1, ffn_norm[1], KC)
            rows(C_D, s5_d[0], KC)
            for k in range(4):
                rows(C_CW + k * LC, conv_w[0, k], LC)
            rows(C_CB, conv_b[0], LC)
            rows2(C_BA, lru_ba[0], LC)
            rows2(C_BX, lru_bx[0], LC)
            rows2(C_LAM, lru_lambda[0], LC)
            for col, src in ((C_QG, q_gain), (C_KG, k_gain)):
                for h in range(2):
                    act.dma_start(prow2[col:col + 1, h * HD:h * HD + HD], src).then_inc(par_loaded, 16)
            act.dma_start(lrow[0:NT, :], s5_lam_re[0].rearrange("(j g) p -> j (g p)", g=2)).then_inc(par_loaded, 16)
            act.dma_start(lrow[NT:P, :], s5_lam_im[0].rearrange("(j g) p -> j (g p)", g=2)).then_inc(par_loaded, 16)
            act.dma_start(srow[0:1, 0:2 * NT], s5_log_step).then_inc(par_loaded, 16)
            act.dma_start(srow[0:1, 2 * NT:], sinks).then_inc(par_loaded, 16)
            for k, s5_b in enumerate((s5_b_re, s5_b_im)):
                act.dma_start(braw[:, k], s5_b[0].rearrange("(j g) p h -> (g p) j h", g=2)).then_inc(b_loaded, 16)
            act.wait_ge(zeroed, 1)
            for k, w in enumerate((lru_wa, lru_wx)):
                for h in range(2):
                    half = slice(64 * h, 64 * h + 64)
                    act.dma_start(wax[half, k, :, half],
                                  w[0].rearrange("(c h) i j -> h i c j", h=2)[h]).then_inc(wax_loaded, 16)

            hi = Tally(op_hi)
            xf = Tally(x_final)
            hid = Tally(hid_ready)
            var = Tally(rms_var)
            root = Tally(rms_root)
            gate = Tally(gated)

            act.preload_act_table(ACT.Copy)
            act.wait_ge(par_ready, 1)
            for i in range(KC // 2):
                act.wait_ge(xt_done, i + 1)
                src = px[:, i % 3, :].rearrange("p (c t) -> p c t", c=2)
                fn(xT[:, 2 * i:2 * i + 2, :], src, ACT.Copy)
                for c in range(2):
                    last = fn(A1[:, 2 * i + c, 0:L], src[:, c], ACT.Copy, scale=gain(G_MIX0 + 2 * i + c))
                hi.inc(last)

            def split(g, s):
                act.wait_ge(landed[s], (g + 1) * 16)
                if not (isinstance(g, int) and g == 0):
                    act.wait_ge(unit_done, (g - 1) * NU + (s + 1))
                fn(Wh[:, s], raw[:, s], ACT.Copy).then_inc(hi_split, 1)

            def pair(g, d, nxt=True, before=None, beside=None):
                if nxt:
                    for s in range(NU):
                        split(g + 1, s)
                        if beside:
                            beside(s)
                if before:
                    before()
                act.wait_ge(unit_done, (g + 1) * NU)
                fn(cross[:, d], ps[:, 2 * d:2 * d + 2, L:2 * L], ACT.Copy).then_inc(crossed, 1)

            def rms():
                var.wait(act)
                root.inc(fn(rs[:, :], nv[:, :], ACT.Sqrt))

            def operand_from_x(j, col):
                xf.wait(act)
                for c in range(2):
                    last = fn(A1[:, bass.ds(j * 2 + c, 1), 0:L], xT[:, bass.ds(j * 2 + c, 1), :], ACT.Copy,
                              scale=gain(j * 2 + (col + c)))
                hi.inc(last)

            for s in range(NU):
                split(0, s)

            pair(0, 0, before=rms)
            fn(s5w[:, 0, :], scol[:, 0:NT], ACT.Exp).then_inc(s5_exp, 1)
            pair(1, 1)
            pair(2, 0)
            act.wait_ge(s5_arg, 2)
            fn(s5w[:, 7, :], s5w[:, 1, :], ACT.Exp)
            fn(s5w[:, 8, :], s5w[:, 6, :], ACT.Tanh, scale=0.5)
            fn(ls[:, 1, :], ls[:, 0, :], ACT.Exp, scale=-1.0)
            fn(s5w[:, 4, :], s5w[:, 4, :], ACT.Sin)
            fn(s5w[:, 5, :], s5w[:, 5, :], ACT.Sin).then_inc(s5_exp, 1)
            pair(3, 1)
            pair(4, 0)

            def softmax_exp(i):
                d = i % 2
                act.wait_ge(maxed, i + 1)
                if i >= 2:
                    act.wait_ge(p_t, i - 1)
                for n in range(NCH):
                    nk = P if n else CH
                    fn(pb[:, d, n, 0:nk], px[:, d, n * P:n * P + nk], ACT.Exp, bias=am[:, d, 1, n:n + 1],
                       scale=HD ** -0.5, accum_out=am[:, d, 2, n:n + 1])
                fn(am[:, d, 3, :], am[:, d, 1, :], ACT.Exp, bias=scol[:, NT + i:NT + i + 1]).then_inc(expd, 1)

            def copy_probs(i):
                d = i % 2
                act.wait_ge(p_t, i + 1)
                fn(pt[0:64, d, 0, :], px[0:64, 2, 0:P], ACT.Copy)
                fn(pt[:, d, 1:NCH, :], px[:, 2, P:NCH * P].rearrange("p (n q) -> p n q", n=NCH - 1), ACT.Copy)\
                    .then_inc(p_copied, 1)

            def attended(i):
                if i == 0:
                    act.wait_ge(bbar_stored, 16)
                act.wait_ge(att_o, i + 1)
                hi.inc(fn(A2[:, LC + i, 0:L], px[:, 3, 0:L], ACT.Copy))

            def gates(c):
                act.wait_ge(gates_mm, c + 1)
                fn(lr[:, c], px[:, c % 2, 0:L], ACT.Sigmoid, bias=pcol2[:, C_BA + c:C_BA + c + 1])
                fn(li[:, c], px[:, c % 2, L:2 * L], ACT.Sigmoid, bias=pcol2[:, C_BX + c:C_BX + c + 1])\
                    .then_inc(gates_sg, 1)

            def beside(n):
                if n == SLOT_ROOT:
                    act.wait_ge(qk_var, 1)
                    fn(root18[:, :], nv[0:NH, :], ACT.Sqrt).then_inc(qk_root, 1)
                if n == SLOT_Q:
                    act.wait_ge(kd_ready, 1)
                    act.dma_start(kd[64:P, 0, :], kvT[0:64, 0, :]).then_inc(kd_loaded, 16)
                    act.dma_start(kd[0:64, 1, :], kvT[64:P, 0, :]).then_inc(kd_loaded, 16)
                i, odd = divmod(n - ATT0, 2)
                if odd and 0 <= i < LC:
                    softmax_exp(i)
                if not odd and 0 <= i - 2 < LC:
                    copy_probs(i - 2)
                if odd and 0 <= i - 2 < LC:
                    attended(i - 2)
                if 0 <= n - GATE0 < LC:
                    gates(n - GATE0)

            for g in range(P_XB, P_OUT):
                pair(g, g % 2, beside=lambda s: beside((g - P_XB) * NU + s))

            act.wait_ge(gates_sg, LC)
            act.wait_ge(lru_sp, 1)
            act.wait_ge(unit_done, P_OUT * NU)
            for c in range(LC):
                fn(lt[:, c], lr[:, c], ACT.Tanh, scale=ls[:, 4, c:c + 1])
            for c in range(LC):
                fn(lr[:, c], lr[:, c], ACT.Exp, scale=ls[:, 5, c:c + 1]).then_inc(lru_a, 1)
            act.wait_ge(g_ready, 4)
            for c in range(0, LC, 4):
                fn(gT[:, c:c + 4], gT[:, c:c + 4], ACT.Gelu_apprx_tanh).then_inc(lru_h, 1)
            for c in range(0, LC, 4):
                act.wait_ge(lru_m2, c // 4 + 1)
                fn(lt[:, c:c + 4], lt[:, c:c + 4], ACT.Sqrt).then_inc(lru_m, 1)
            for c in range(LC):
                act.wait_ge(lru_y, c + 1)
                hi.inc(fn(A2[:, c, 0:L], gT[:, c], ACT.Copy))
            if stop < 2:
                return

            def out_pair(j, d):
                pair(j + P_OUT, (P_OUT + d) % 2)
                operand_from_x(j, G_FF0)
            double_pairs(act, 8, out_pair, (hi, 2), (xf, 2))

            def mlp(g0, last_gain, final):
                def up(j, d, q=0, quarter0=True):
                    pair(q * 16 + j + g0, (g0 + d) % 2,
                         before=rms if quarter0 and isinstance(j, int) and j == 0 else None)
                    hid.wait(act)
                    c = (g0 + d) % 2
                    hi.inc(fn(A2[:, bass.ds(j * 2, 2), 0:L], cross[:, c], ACT.Copy))

                def down(j, d, q=0, nxt=True):
                    pair(q * 16 + j + (g0 + 8), (g0 + d) % 2, nxt=nxt)

                double_pairs(act, 8, up, (hi, 2), (hid, 2), first=2)
                double_pairs(act, 8, down)
                with trips(act, QTR - 2, (hi, 8), (hid, 8)) as q:
                    double_pairs(act, 8, lambda j, d: up(j, d, q + 1, False), (hi, 2), (hid, 2))
                    double_pairs(act, 8, lambda j, d: down(j, d, q + 1))
                double_pairs(act, 8, lambda j, d: up(j, d, QTR - 1, False), (hi, 2), (hid, 2))
                xf.skip(8 * (QTR - 1))
                if not final:
                    double_pairs(act, 8, lambda j, d: down(j, d, QTR - 1))
                    xf.skip(8)
                else:
                    double_pairs(act, 8, lambda j, d: down(j, d, QTR - 1, nxt=not (isinstance(j, int) and j == 7)),
                                 last=2)

            mlp(P_MLP0, G_MIX1, False)
            if stop < 3:
                return

            rms()
            act.preload_act_table(ACT.Gelu_apprx_tanh)
            act.wait_ge(bc_loaded, 48)
            act.wait_ge(bx_zero, 1)

            def s5_masks(c, b):
                if not isinstance(c, int) or c >= 2:
                    act.wait_ge(s5_tr, c - 1)
                for g in range(2):
                    half = slice(64 * g, 64 * g + 64)
                    fn(bx[half, b, :, :, g, :].rearrange("p k j h -> p (k j) h"),
                       bch[half, bass.ds(c, 1), :].rearrange("p o (m h) -> p (o m) h", h=SH), ACT.Copy)
                for g in range(2):
                    last = fn(cx[:, b, :, 64 * g:64 * g + 64],
                              craw[:, :, bass.ds(c, 1), :].rearrange("p k o n -> p (k o) n"), ACT.Copy,
                              scale=par[:, g:g + 1])
                last.then_inc(s5_mask, 1)

            def s5_stationary(c, b):
                act.wait_ge(s5_tr, c + 1)
                fn(lhs5[:, b].rearrange("p k n -> p (k n)"), px[:, 2, :], ACT.Copy)
                fn(ncim[:, b].rearrange("p k n -> p (k n)"), px[:, 2, 2 * P:], ACT.Copy, scale=-1.0)\
                    .then_inc(s5_neg, 1)

            def s5_gelu(c, b):
                act.wait_ge(s5_yf, c + 1)
                fn(yb[:, b], yb[:, b], ACT.Gelu_apprx_tanh).then_inc(s5_ge, 1)
                act.wait_ge(s5_ge, c + 1)
                hi.inc(fn(A2[:, bass.ds(c, 1), 0:L], yb[:, b:b + 1], ACT.Copy))

            s5_masks(0, 0)
            s5_stationary(0, 0)
            s5_masks(1, 1)

            def s5_chunk(c, b, gelu=True, more=2):
                if more >= 1:
                    s5_stationary(c + 1, 1 - b)
                if gelu:
                    s5_gelu(c - 1, 1 - b)
                if more >= 2:
                    s5_masks(c + 2, b)

            s5_chunk(0, 0, gelu=False)
            s5_chunk(1, 1)
            with trips(act, KC // 2 - 2, (hi, 2)) as i:
                s5_chunk(i * 2 + 2, 0)
                s5_chunk(i * 2 + 3, 1)
            s5_chunk(KC - 2, 0, more=1)
            s5_chunk(KC - 1, 1, more=0)
            s5_gelu(KC - 1, 1)
            if stop < 4:
                return

            act.preload_act_table(ACT.Sigmoid)

            def glu(j, d):
                c = (P_GLU + d) % 2
                pair(j + P_GLU, c)
                if d == 1:
                    act.wait_ge(pair_read, j + (P_GLU + 1))
                    gate.inc(fn(cross[:, c], cross[:, c], ACT.Sigmoid))
                    xf.wait(act)
                    for k in range(2):
                        last = fn(A1[:, bass.ds(j + (k - 1), 1), 0:L], xT[:, bass.ds(j + (k - 1), 1), :], ACT.Copy,
                                  scale=gain(j + (G_FF1 + k - 1)))
                    hi.inc(last)
            double_pairs(act, 16, glu, (hi, 1), (xf, 1), (gate, 1))
            mlp(P_MLP1, None, True)

            for i in range(KC // 2):
                act.wait_ge(out_t, i + 1)
                fn(xin.rearrange("p a (i d) -> p a i d", i=8)[:, :, i, :],
                   px[:, i % 2, :].rearrange("p (a d) -> p a d", a=2), ACT.Copy).then_inc(out_c, 1)

        @block.vector
        def _(dve):
            tt, ts, stt = nc.vector.tensor_tensor, nc.vector.tensor_scalar, nc.vector.scalar_tensor_tensor
            seq = Tally(dve_seq)
            hi = Tally(op_hi)
            sums = Tally(rms_sum)
            root = Tally(rms_root)
            gate = Tally(gated)

            def link(ins):
                seq.inc(ins)
                seq.again(dve)

            dve.wait_ge(par_t, 1)
            row = px[:, 3]
            nc.vector.tensor_copy(pcol[:, :], row[:, 0:N_PCOL])
            nc.vector.tensor_copy(pcol2[:, :], row[:, 120:120 + N_PCOL2])
            nc.vector.tensor_copy(lcol[:, :, :], row[:, 146:146 + P].rearrange("p (k j) -> p k j", k=2))
            nc.vector.tensor_copy(scol[:, :], row[:, 274:274 + NT + LC]).then_inc(par_ready, 1)
            dve.wait_ge(par_ready, 1)
            dve.wait_ge(consts, 1)
            idv = ident.rearrange("p (a g h) -> p g a h", g=2, h=SH)
            link(nc.vector.tensor_reduce(par[:, :], idv, AX.XY, ALU.add))
            link(ts(ls[:, 1, :], pcol2[:, C_LAM:C_LAM + LC], -1.0, None, ALU.mult))
            tt(ls[:, 0, :], ls[:, 1, :], pcol2[:, C_LAM:C_LAM + LC], ALU.max).then_inc(s5_arg, 1)

            for i in range(KC // 2):
                hi.wait(dve)
                for c in range(2):
                    k = 2 * i + c
                    last = stt(A1[:, k, L:2 * L], xT[:, k, :], gain(G_MIX0 + k), A1[:, k, 0:L].bitcast(F32),
                               ALU.mult, ALU.subtract)
                last.then_inc(a1_ready, 1)

            def split(g, s):
                dve.wait_ge(hi_split, g * NU + (s + 1))
                tt(Wl[:, s], raw[:, s], Wh[:, s].bitcast(F32), ALU.subtract).then_inc(lo_split, 1)

            for s in range(NU):
                split(0, s)

            def inv_root(v, r, w, done=None):
                link(nc.vector.reciprocal(r, r))
                link(tt(w, r, r, ALU.mult))
                link(tt(w, w, v, ALU.mult))
                link(ts(w, w, -0.5, 1.5, ALU.mult, ALU.add))
                if done is None:
                    link(tt(r, r, w, ALU.mult))
                else:
                    tt(r, r, w, ALU.mult).then_inc(done, 1)

            def rms():
                sums.wait(dve)
                ts(nv[:, :], px[:, 3, 0:L], 1.0 / D, EPS, ALU.mult, ALU.add).then_inc(rms_var, 1)
                root.wait(dve)
                inv_root(nv[:, :], rs[:, :], nw[:, :])

            rs2 = rs[:, :].unsqueeze(1).to_broadcast([P, 2, L])

            def pair(g, d, nxt=True, before=None, beside=None):
                if nxt:
                    for s in range(NU):
                        split(g + 1, s)
                        if beside:
                            beside(s)
                if before:
                    before()
                dve.wait_ge(crossed, g + 1)
                tt(cross[:, d], ps[:, 2 * d:2 * d + 2, 0:L], cross[:, d], ALU.add).then_inc(pair_read, 1)
                dve.wait_ge(pair_read, g + 1)

            def projection(g, d, dest, **kw):
                pair(g, d, **kw)
                link(tt(dest, cross[:, d], rs2, ALU.mult))

            def residual(j, d):
                xs = xT[:, bass.ds(j * 2, 2), :]
                tt(xs, xs, cross[:, d], ALU.add).then_inc(x_final, 1)

            def operand_from_x(j, col):
                hi.wait(dve)
                for c in range(2):
                    k = bass.ds(j + c, 1)
                    last = stt(A1[:, k, L:2 * L], xT[:, k, :], gain(j + (col + c)), A1[:, k, 0:L].bitcast(F32),
                               ALU.mult, ALU.subtract)
                last.then_inc(a1_ready, 1)

            W = [s5w[:, k, :] for k in range(20)]
            step, a, hb, tmp, s2, c2, ac, ea, th = W[:9]
            lre, lim = lcol[:, 0, :], lcol[:, 1, :]
            em1, mask, t1, t2_, sinb, cosb, X, Y = W[9:17]
            cr, ci, n2 = W[17], W[18], W[19]
            S = [ls[:, k, :] for k in range(6)]

            def s5_arguments():
                dve.wait_ge(s5_exp, 1)
                link(tt(a, lre, step, ALU.mult))
                link(tt(hb, lim, step, ALU.mult))
                link(ts(hb, hb, 0.5, None, ALU.mult))
                link(ts(ac, a, -1.0, 1.0, ALU.max, ALU.min))
                for out_, turn in ((s2, 0.0), (c2, 0.25)):
                    link(ts(tmp, hb, TWO_PI_INV, turn, ALU.mult, ALU.add))
                    link(ts(tmp, tmp, MAGIC, None, ALU.add))
                    link(ts(tmp, tmp, -MAGIC, None, ALU.add))
                    link(stt(out_, tmp, -PI_HI, hb, ALU.mult, ALU.add))
                    link(stt(out_, tmp, -PI_MID, out_, ALU.mult, ALU.add))
                    link(stt(out_, tmp, -PI_LO, out_, ALU.mult, ALU.add))
                    link(ts(out_, out_, 2.0 * math.pi * turn, None, ALU.add))
                    link(ts(out_, out_, -PI_CLAMP, PI_CLAMP, ALU.max, ALU.min))
                ts(tmp, tmp, 0.0, None, ALU.mult).then_inc(s5_arg, 1)
                dve.wait_ge(s5_arg, 2)


            def softplus():
                link(ts(S[2], S[1], 2.0, None, ALU.add))
                link(nc.vector.reciprocal(S[2], S[2]))
                link(tt(S[2], S[1], S[2], ALU.mult))
                link(tt(S[3], S[2], S[2], ALU.mult))
                link(ts(S[4], S[3], 1.0 / 15, 1.0 / 13, ALU.mult, ALU.add))
                for k in (11, 9, 7, 5, 3, 1):
                    link(tt(S[4], S[4], S[3], ALU.mult))
                    link(ts(S[4], S[4], 1.0 / k, None, ALU.add))
                link(tt(S[4], S[4], S[2], ALU.mult))
                link(ts(S[5], pcol2[:, C_LAM:C_LAM + LC], -1.0, 0.0, ALU.mult, ALU.max))
                link(stt(S[4], S[4], 2.0, S[5], ALU.mult, ALU.add))
                link(ts(S[4], S[4], LRU_C, None, ALU.mult))
                ts(S[5], S[4], -1.0, None, ALU.mult).then_inc(lru_sp, 1)


            def s5_coefficients():
                dve.wait_ge(s5_exp, 2)
                link(ts(t1, th, -1.0, 1.0, ALU.mult, ALU.add))
                link(nc.vector.reciprocal(t1, t1))
                link(tt(t1, t1, th, ALU.mult))
                link(ts(mask, a, -1.0, None, ALU.is_gt))
                link(ts(t2_, a, 1.0, None, ALU.is_lt))
                link(tt(mask, mask, t2_, ALU.mult))
                link(ts(em1, ea, -1.0, None, ALU.add))
                link(stt(t1, t1, 2.0, em1, ALU.mult, ALU.subtract))
                link(tt(t1, t1, mask, ALU.mult))
                link(tt(em1, em1, t1, ALU.add))
                link(ts(rho[:, :], em1, 1.0, None, ALU.add))
                link(tt(t1, s2, s2, ALU.mult))
                link(ts(t1, t1, 2.0, None, ALU.mult))
                link(ts(cosb, t1, -1.0, 1.0, ALU.mult, ALU.add))
                link(tt(sinb, s2, c2, ALU.mult))
                link(ts(sinb, sinb, 2.0, None, ALU.mult))
                link(nc.vector.tensor_copy(rot1[:, 0, :], cosb))
                link(nc.vector.tensor_copy(rot1[:, 1, :], sinb))
                link(tt(X, em1, cosb, ALU.mult))
                link(tt(X, X, t1, ALU.subtract))
                link(tt(Y, rho[:, :], sinb, ALU.mult))
                link(tt(n2, lre, lre, ALU.mult))
                link(tt(t1, lim, lim, ALU.mult))
                link(tt(n2, n2, t1, ALU.add))
                link(nc.vector.reciprocal(n2, n2))
                link(tt(cr, X, lre, ALU.mult))
                link(tt(t1, Y, lim, ALU.mult))
                link(tt(cr, cr, t1, ALU.add))
                link(tt(cr, cr, n2, ALU.mult))
                link(tt(ci, Y, lre, ALU.mult))
                link(tt(t1, X, lim, ALU.mult))
                link(tt(ci, ci, t1, ALU.subtract))
                tt(ci, ci, n2, ALU.mult).then_inc(s5_small, 1)

            def head_squares(j):
                if j >= 2:
                    dve.wait_ge(qk_sum, j - 1)
                for c in range(2 if j < 4 else 1):
                    src = qT[:, 2 * j + c] if j < 4 else kvT[:, 0]
                    last = tt(squares_of(j, c), src, src, ALU.mult)
                last.then_inc(qk_sq, 1)

            for j in range(4):
                projection(j, j % 2, qT[:, 2 * j:2 * j + 2, :], before=rms if j == 0 else None)
                head_squares(j)
                if j == 1:
                    s5_arguments()
                if j == 3:
                    s5_coefficients()
            projection(P_KV, 0, kvT[:, :, :])
            head_squares(4)

            def softmax_max(i):
                d = i % 2
                dve.wait_ge(scored, i + 1)
                s = px[:, d, :].rearrange("p (n k) -> p n k", n=NCH)
                nc.vector.reduce_max(am[:, d, 0, 0:1], s[:, 0, 0:CH], AX.X)
                link(nc.vector.reduce_max(am[:, d, 0, 1:NCH], s[:, 1:NCH], AX.X))
                link(ts(am[:, d, 0, :], am[:, d, 0, :], HD ** -0.5, scol[:, NT + i:NT + i + 1], ALU.mult, ALU.max))
                ts(am[:, d, 1, :], am[:, d, 0, :], -1.0, None, ALU.mult).then_inc(maxed, 1)

            def softmax_norm(i):
                d = i % 2
                dve.wait_ge(expd, i + 1)
                link(tt(am[:, d, 4, :], am[:, d, 2, :], am[:, d, 3, :], ALU.add))
                link(nc.vector.reciprocal(am[:, d, 4, :], am[:, d, 4, :]))
                tt(pb[:, d, 0, 0:CH], pb[:, d, 0, 0:CH], am[:, d, 4, 0:1].to_broadcast([P, CH]), ALU.mult)
                tt(pb[:, d, 1:NCH], pb[:, d, 1:NCH], am[:, d, 4, 1:NCH].unsqueeze(2).to_broadcast([P, NCH - 1, P]),
                   ALU.mult).then_inc(probs, 1)

            def attended(i):
                hi.wait(dve)
                tt(A2[:, LC + i, L:2 * L], px[:, 3, 0:L], A2[:, LC + i, 0:L].bitcast(F32), ALU.subtract)\
                    .then_inc(a2_ready, 1)

            def normed(i, half):
                return stt(qT[:, i], qT[:, i], pcol2[:, C_QG:C_QG + 1], wide_root(half), ALU.mult, ALU.mult)

            def beside(n):
                if n == 0:
                    softplus()
                if n == SLOT_VAR:
                    dve.wait_ge(qk_sum, 5)
                    ts(nv[0:NH, :], px[0:NH, 3, L:2 * L], 1.0 / HD, EPS, ALU.mult, ALU.add).then_inc(qk_var, 1)
                    dve.wait_ge(v_t, 1)
                    nc.vector.tensor_copy(vw[:, :, :], px[:, 2, 0:3 * P].rearrange("p (w n) -> p w n", w=3))\
                        .then_inc(v_ready, 1)
                if n == SLOT_INV:
                    dve.wait_ge(qk_root, 1)
                    inv_root(nv[0:NH, :], root18[:, :], nw[0:NH, :], done=qk_norm)
                if n == SLOT_WIDE:
                    dve.wait_ge(qk_wide, 1)
                    link(stt(kvT[:, 0], kvT[:, 0], pcol2[:, C_KG:C_KG + 1], wide_root(7), ALU.mult, ALU.mult))
                    nc.vector.tensor_copy(kd[0:64, 0, :], kvT[0:64, 0, :])
                    nc.vector.tensor_copy(kd[64:P, 1, :], kvT[64:P, 0, :]).then_inc(kd_ready, 1)
                    normed(0, 0)
                    normed(1, 1).then_inc(q_normed, 1)
                    for i in range(2, 4):
                        normed(i, i)
                if n == SLOT_Q:
                    for i in range(4, LC - 1):
                        normed(i, i)
                if n == SLOT_Q + 1:
                    dve.wait_ge(qk_wide, 2)
                    normed(LC - 1, 0).then_inc(q_normed, 1)
                i, odd = divmod(n - ATT0, 2)
                if not odd and 0 <= i < LC:
                    softmax_max(i)
                if odd and 0 <= i - 1 < LC:
                    softmax_norm(i - 1)
                if odd and 0 <= i - 2 < LC:
                    attended(i - 2)

            for g in range(P_XB, P_OUT):
                j = g - P_XB
                dest = xb[:, 2 * j:2 * j + 2, 3:3 + L] if j < 4 else gT[:, 2 * j - 8:2 * j - 6, :]
                pair(g, g % 2, beside=lambda s: beside(j * NU + s))
                tt(dest, cross[:, g % 2], rs2, ALU.mult).then_inc(xb_ready if j < 4 else g_ready, 1)

            dve.wait_ge(gates_sg, LC)
            for c in range(0, LC, 4):
                tt(li[:, c:c + 4], li[:, c:c + 4], xc[:, c:c + 4], ALU.mult)
            for c in range(0, LC, 4):
                h = slice(c, c + 4)
                dve.wait_ge(lru_a, c + 4)
                link(tt(la[:, h], lr[:, h], lr[:, h], ALU.mult))
                stt(lt[:, h], la[:, h], 1.0, lt[:, h], ALU.add, ALU.mult).then_inc(lru_m2, 1)
            for c in range(0, LC, 4):
                h = slice(c, c + 4)
                dve.wait_ge(lru_m, c // 4 + 1)
                link(tt(li[:, h], li[:, h], lt[:, h], ALU.mult))
                for k in range(c, c + 4):
                    last = nc.vector.tensor_tensor_scan(la[:, k], lr[:, k], li[:, k], 0.0, ALU.mult, ALU.add)
                link(last)
                dve.wait_ge(lru_h, c // 4 + 1)
                for k in range(c, c + 4):
                    tt(gT[:, k], gT[:, k], la[:, k], ALU.mult).then_inc(lru_y, 1)
            for c in range(LC):
                hi.wait(dve)
                tt(A2[:, c, L:2 * L], gT[:, c], A2[:, c, 0:L].bitcast(F32), ALU.subtract).then_inc(a2_ready, 1)
            if stop < 2:
                return

            def out_pair(j, d):
                c = (P_OUT + d) % 2
                pair(j + P_OUT, c)
                residual(j, c)
                operand_from_x(j * 2, G_FF0)
            double_pairs(dve, 8, out_pair, (hi, 2))

            def mlp(g0, final):
                def up(j, d, q=0, quarter0=True):
                    c = (g0 + d) % 2
                    pair(q * 16 + j + g0, c, before=rms if quarter0 and isinstance(j, int) and j == 0 else None)
                    link(tt(cross[:, c], cross[:, c], rs2, ALU.mult))
                    stt(cross[:, c], cross[:, c], 0.0, cross[:, c], ALU.max, ALU.mult).then_inc(hid_ready, 1)
                    hi.wait(dve)
                    k = bass.ds(j * 2, 2)
                    tt(A2[:, k, L:2 * L], cross[:, c], A2[:, k, 0:L].bitcast(F32), ALU.subtract).then_inc(a2_ready, 1)

                def down(j, d, q=0, nxt=True):
                    c = (g0 + d) % 2
                    pair(q * 16 + j + (g0 + 8), c, nxt=nxt)
                    residual(j, c)

                double_pairs(dve, 8, up, (hi, 2), (seq, 2), first=2)
                double_pairs(dve, 8, down)
                with trips(dve, QTR - 2, (hi, 8), (seq, 8)) as q:
                    double_pairs(dve, 8, lambda j, d: up(j, d, q + 1, False), (hi, 2), (seq, 2))
                    double_pairs(dve, 8, lambda j, d: down(j, d, q + 1))
                double_pairs(dve, 8, lambda j, d: up(j, d, QTR - 1, False), (hi, 2), (seq, 2))
                double_pairs(dve, 8, lambda j, d: down(j, d, QTR - 1,
                                                       nxt=not (final and isinstance(j, int) and j == 7)), last=2)

            mlp(P_MLP0, False)
            if stop < 3:
                return

            rms()

            def s5_u(c, b):
                k = bass.ds(c, 1)
                if not isinstance(c, int) or c >= 2:
                    dve.wait_ge(s5_yf, c - 1)
                stt(uc[:, b:b + 1], xT[:, k, :], gain(c + G_MIX1), rs[:, :].unsqueeze(1), ALU.mult, ALU.mult)\
                    .then_inc(u_ready, 1)

            def comps(t):
                return t.unsqueeze(1).to_broadcast([P, 2, L])

            def s5_scan(t, tl, b):
                d = tl % 2
                dve.wait_ge(s5_z, t + 1)
                if not (isinstance(t, int) and t < 2):
                    dve.wait_ge(s5_sn, t - 1)
                for k in range(2):
                    last = nc.vector.tensor_tensor_scan(gb[:, d, k], rho[:, bass.ds(t, 1)].to_broadcast([P, L]),
                                                        zb[:, d, k], 0.0, ALU.mult, ALU.add)
                last.then_inc(s5_g, 1)
                dve.wait_ge(s5_g, t + 1)
                if not (isinstance(t, int) and t < 2):
                    dve.wait_ge(s5_y, t - 1)
                tt(cdb[:, d, 0], gb[:, d], comps(tab[:, b, 0, tl % TPC]), ALU.mult).then_inc(s5_cs, 1)

            def s5_finish(c, b):
                dve.wait_ge(s5_y, c * TPC + TPC)
                stt(yb[:, b], uc[:, b], gain(c + C_D), ps[:, b, 0:L], ALU.mult, ALU.add).then_inc(s5_yf, 1)

            def s5_lo(c, b):
                hi.wait(dve)
                k = bass.ds(c, 1)
                tt(A2[:, k, L:2 * L], yb[:, b:b + 1], A2[:, k, 0:L].bitcast(F32), ALU.subtract).then_inc(a2_ready, 1)

            def s5_trip(i, first=False, more=True):
                for tl in range(2 * TPC):
                    t, b = i * (2 * TPC) + tl, tl // TPC
                    c = i * 2 + b
                    if tl % TPC == 1:
                        if not (first and b == 0):
                            s5_finish(c - 1, 1 - b)
                        if b == 0 or more:
                            s5_u(c + 1, 1 - b)
                    if tl + 1 < 2 * TPC:
                        s5_rotate_at(t + 1, tl + 1, i, (tl + 1) // TPC)
                    elif more:
                        s5_rotate_at(t + 1, 0, i + 1, 0)
                    if tl % TPC == 2 and not (first and b == 0):
                        s5_lo(c - 1, 1 - b)
                    s5_scan(t, tl, b)

            def s5_rotate_at(t, tl, i, b):
                if tl % TPC == 0:
                    dve.wait_ge(tab_loaded[b], i * 16 + 16)
                d = tl % 2
                dve.wait_ge(s5_bu, t + 1)
                if not (isinstance(t, int) and t < 2):
                    dve.wait_ge(s5_z, t - 1)
                bu = bu_bank(tl).rearrange("p (k t) -> p k t", k=2)
                for w in range(2):
                    last = tt(ab[:, d, w], bu, comps(tab[:, b, w, tl % TPC]), ALU.mult)
                last.then_inc(s5_rot, 1)

            s5_u(0, 0)
            s5_rotate_at(0, 0, 0, 0)
            s5_trip(0, first=True)
            with trips(dve, KC // 2 - 2, (hi, 2)) as i:
                s5_trip(i + 1)
            s5_trip(KC // 2 - 1, more=False)
            s5_finish(KC - 1, 1)
            s5_lo(KC - 1, 1)
            if stop < 4:
                return

            def glu(j, d):
                c = (P_GLU + d) % 2
                pair(j + P_GLU, c)
                if d == 1:
                    gate.wait(dve)
                    link(tt(cross[:, c], cross[:, c], cross[:, 1 - c], ALU.mult))
                    xs = xT[:, bass.ds(j - 1, 2), :]
                    tt(xs, xs, cross[:, c], ALU.add).then_inc(x_final, 1)
                    operand_from_x(j - 1, G_FF1)
            double_pairs(dve, 16, glu, (hi, 1), (seq, 1), (gate, 1))
            mlp(P_MLP1, True)

        @block.gpsimd
        def _(pool):
            tt = nc.gpsimd.tensor_tensor
            seq = Tally(pool_seq)
            xf = Tally(x_final)

            def link(ins):
                seq.inc(ins)
                seq.again(pool)

            link(nc.gpsimd.memset(ident[:, :], 0.0))
            link(nc.gpsimd.memset(ones[:, :], 1.0))
            link(nc.gpsimd.memset(hsel[:, :], 0.0))
            link(nc.gpsimd.memset(hsel[0:64, 16:17], 1.0))
            link(nc.gpsimd.memset(hsel[64:P, 17:18], 1.0))
            nc.gpsimd.affine_select(out=ident[:, :], in_=ident[:, :], compare_op=ALU.not_equal, fill=1.0, base=0,
                                    pattern=[[-1, P]], channel_multiplier=1).then_inc(consts, 1)
            pool.wait_ge(consts, 1)
            nc.gpsimd.memset(wax[:, :, :, :], 0.0).then_inc(zeroed, 1)
            nc.gpsimd.tensor_copy(rsel[:, :, :], ident[0:NH, 0:NH].unsqueeze(2).to_broadcast([NH, NH, HD]))\
                .then_inc(zeroed, 1)

            def zero_squares():
                link(nc.gpsimd.memset(ss[:, :, :], 0.0))

            sqd = Tally(squared)

            def add_squares(xs):
                sqd.again(pool) if not (isinstance(sqd.value, int) and sqd.value == 0) else None
                link(tt(sq[:, :, :], xs, xs, ALU.mult))
                sqd.inc(tt(ss[:, :, :], ss[:, :, :], sq[:, :, :], ALU.add))

            zero_squares()
            for i in range(KC // 2):
                pool.wait_ge(op_hi, i + 1)
                add_squares(xT[:, 2 * i:2 * i + 2, :])
            pool.wait_ge(s5_small, 1)
            pool.wait_ge(b_loaded, 32)
            cr = s5w[:, 17, :].unsqueeze(2).to_broadcast([P, NT, SH])
            ci = s5w[:, 18, :].unsqueeze(2).to_broadcast([P, NT, SH])
            for k, (u, v, op) in enumerate(((cr, ci, ALU.subtract), (ci, cr, ALU.add))):
                link(tt(btmp[:, 0], braw[:, 0], u, ALU.mult))
                link(tt(btmp[:, 1], braw[:, 1], v, ALU.mult))
                t = btmp.rearrange("p k (c j) h -> p k c j h", c=KC)
                link(tt(bbar[:, :, k], t[:, 0], t[:, 1], op))
            pool.dma_start(bbar_d.rearrange("c p f -> p c f"), bbar.rearrange("p c k j h -> p c (k j h)"))\
                .then_inc(bbar_stored, 16)

            pool.wait_ge(par_ready, 1)
            pool.wait_ge(xt_done, KC // 2)
            link(nc.gpsimd.memset(xb[:, :, 0:3], 0.0))
            pool.wait_ge(bbar_stored, 16)
            for j in range(4):
                c = slice(2 * j, 2 * j + 2)
                pool.wait_ge(xb_ready, j + 1)

                def column(k):
                    return pcol[:, k + 2 * j:k + 2 * j + 2].unsqueeze(2).to_broadcast([P, 2, L])
                link(tt(xc[:, c], xb[:, c, 0:L], column(C_CW), ALU.mult))
                for k in range(1, 4):
                    link(tt(sq[:, :, :], xb[:, c, k:k + L], column(C_CW + k * LC), ALU.mult))
                    link(tt(xc[:, c], xc[:, c], sq[:, :, :], ALU.add))
                tt(xc[:, c], xc[:, c], column(C_CB), ALU.add).then_inc(conv_done, 1)

            pool.wait_ge(qk_wide, 2)

            def tables(i, stored):
                if stored:
                    pool.wait_ge(tab_stored, i * 16)
                link(nc.gpsimd.tensor_copy(ctab[:, :, :, 0], rot1[:, :, bass.ds(i * 2, 2)]))
                n = 1
                while n < L:
                    a, b = ttmp[:, 0, :, :, 0:n], ttmp[:, 1, :, :, 0:n]
                    turn = [ctab[:, k, :, n - 1:n].unsqueeze(1).to_broadcast([P, 2, 2, n]) for k in range(2)]
                    link(tt(a, ctab[:, :, :, 0:n], turn[0], ALU.mult))
                    link(tt(b, ctab[:, :, :, 0:n], turn[1], ALU.mult))
                    link(tt(ctab[:, 0, :, n:2 * n], a[:, 0], b[:, 1], ALU.subtract))
                    link(tt(ctab[:, 1, :, n:2 * n], a[:, 1], b[:, 0], ALU.add))
                    n *= 2

            def store(c, h):
                pool.dma_start(tab_d[bass.ds(c, 1)].rearrange("o p (k j t) -> p (o k) j t", k=2, j=TPC)
                               [:, :, 2 * h:2 * h + 2, :], ctab[:, :, :, :]).then_inc(tab_stored, 16)

            STEPS = 1 + 4 * 8
            EARLY = 3

            def table_chunks(first, n):
                with trips(pool, n, (seq, 2 * STEPS)) as c:
                    for h in range(2):
                        tables(c * 2 + (2 * first + h), True)
                        store(c + first, h)

            for h in range(2):
                tables(h, h > 0)
                store(0, h)
            table_chunks(1, EARLY - 1)

            def norm_squares(count, skip):
                pool.wait_ge(rms_sum, count - 1)
                xf.skip(skip)
                zero_squares()
                with trips(pool, KC // 2, (xf, 1), (seq, 1), (sqd, 1)) as i:
                    xf.wait(pool)
                    add_squares(xT[:, bass.ds(i * 2, 2), :])

            norm_squares(2, 0)
            table_chunks(EARLY, KC - EARLY)
            nc.gpsimd.memset(bx[:, :, :, :, :, :], 0.0).then_inc(bx_zero, 1)
            norm_squares(3, 8 * (QTR - 1))
            if stop < 3:
                return

            def s5_z_of(t, tl):
                d = tl % 2
                pool.wait_ge(s5_rot, t + 1)
                if not (isinstance(t, int) and t < 2):
                    pool.wait_ge(s5_g, t - 1)
                tt(zb[:, d, 0], ab[:, d, 0, 0], ab[:, d, 1, 1], ALU.add)
                tt(zb[:, d, 1], ab[:, d, 0, 1], ab[:, d, 1, 0], ALU.subtract).then_inc(s5_z, 1)

            def s5_sin(t, tl, b):
                d = tl % 2
                pool.wait_ge(s5_g, t + 1)
                if not (isinstance(t, int) and t < 2):
                    pool.wait_ge(s5_y, t - 1)
                tt(cdb[:, d, 1], gb[:, d], tab[:, b, 1, tl % TPC].unsqueeze(1).to_broadcast([P, 2, L]), ALU.mult)\
                    .then_inc(s5_sn, 1)

            def s5_trip(i, more=True):
                for tl in range(2 * TPC):
                    t = i * (2 * TPC) + tl
                    if tl + 1 < 2 * TPC or more:
                        s5_z_of(t + 1, tl + 1)
                    s5_sin(t, tl, tl // TPC)

            s5_z_of(0, 0)
            s5_trip(0)
            with pool.Fori(1, KC // 2 - 1) as i:
                s5_trip(i)
            s5_trip(KC // 2 - 1, more=False)
            if stop < 4:
                return
            norm_squares(4, 0)


_INS = ["x", "mix_norm_e", "w_in_e", "conv_w", "conv_b", "lru_wa", "lru_ba", "lru_wx", "lru_bx", "lru_lambda",
        "q_gain", "k_gain", "sinks", "w_out_e", "mix_norm_o", "s5_lam_re", "s5_lam_im", "s5_log_step",
        "s5_b_re", "s5_b_im", "s5_c_re", "s5_c_im", "s5_d", "w_glu", "ffn_norm", "w_up", "w_down"]
_OUTS = [((1, L, D), "float32")]


def kernel(**inputs):
    import numpy as _np
    import concourse.bacc as _bacc
    from concourse import mybir as _mybir
    from concourse.bass_utils import run_bass_kernel_spmd as _run

    nc = _bacc.Bacc("TRN2", target_bir_lowering=False, num_devices=1)
    arrays, args = {}, []
    for name in _INS:
        a = _np.ascontiguousarray(inputs[name])
        arrays[f"in_{name}_dram"] = a
        args.append(nc.dram_tensor(f"in_{name}_dram", a.shape, _mybir.dt.from_np(a.dtype), kind="ExternalInput").ap())
    for i, (shape, dtype) in enumerate(_OUTS):
        dt = _mybir.dt.from_np(_np.dtype(dtype))
        args.append(nc.dram_tensor(f"out_{i}_dram", shape, dt, kind="ExternalOutput").ap())
    trunk_kernel(nc, *args)
    r = _run(nc, [arrays], core_ids=[0])
    got = tuple(r.results[0][f"out_{i}_dram"] for i in range(len(_OUTS)))
    return got[0]
```

```python
from contextlib import ExitStack, contextmanager
import math

import concourse.bass as bass
from concourse import mybir

F32 = mybir.dt.float32
F32R = mybir.dt.float32r
ACT = mybir.ActivationFunctionType
ALU = mybir.AluOpType
AX = mybir.AxisListType

P = 128
D = 2048
L = 256
KC = D // P
EPS = 1e-6
DL = D // 2
LC = DL // P
NKV = 2
NH = 2 * LC + NKV
HD = 64
CH = 64
NCH = L // CH
QKV0 = 2 * DL
LRU_C = 8.0
FF = 4 * D
QTR = FF // D
UK = 4
NU = KC // UK
TW = 2 * P
NT = 64
TPC = 4
SH = 16
LH = L // 2
TWO_PI_INV = 1.0 / (2.0 * math.pi)
MAGIC = 1.5 * 2.0 ** 23
PI_HI = 6.28125
PI_MID = 0.0019350051879882812
PI_LO = 2.0 * math.pi - PI_HI - PI_MID
PI_CLAMP = 3.1415925

P_Q = 0
P_KV = P_Q + 4
P_XB = P_KV + 1
P_GT = P_XB + 4
P_OUT = P_GT + 4
P_MLP0 = P_OUT + 8
P_GLU = P_MLP0 + 16 * QTR
P_MLP1 = P_GLU + 16

SLOT_SUM, SLOT_ROOT, SLOT_INV, SLOT_WIDE, SLOT_Q = 1, 2, 3, 4, 5
ATT0 = 6
GATE0 = ATT0 + 2 * LC

G_MIX0, G_MIX1, G_FF0, G_FF1, C_D, C_CW, C_CB = 0, 16, 32, 48, 64, 80, 112
N_PCOL = 120
C_BA, C_BX, C_LAM, C_QG, C_KG = 0, 8, 16, 24, 25
N_PCOL2 = 26
N_PAR = 20


class Tally:

    def __init__(self, sem, value=0):
        self.sem, self.start, self.count, self.seen = sem, value, 0, 0

    @property
    def value(self):
        return self.start + self.count

    def skip(self, n):
        self.count += n
        self.seen += n

    def inc(self, ins):
        ins.then_inc(self.sem, 1)
        self.skip(1)

    def wait(self, eng, n=1):
        self.skip(n)
        eng.wait_ge(self.sem, self.value)

    def again(self, eng):
        eng.wait_ge(self.sem, self.value)


@contextmanager
def trips(eng, n, *per_trip):
    entry = [t.value for t, _ in per_trip]
    seen = [t.seen for t, _ in per_trip]
    with eng.Fori(0, n) as i:
        for (t, k), at in zip(per_trip, entry):
            t.start, t.count = at + i * k, 0
        yield i
        for (t, k), was in zip(per_trip, seen):
            assert t.seen - was == k, (t.sem, t.seen - was, k)
    for (t, k), at, was in zip(per_trip, entry, seen):
        t.start, t.count, t.seen = at + n * k, 0, was + n * k


def trunk_kernel(nc, x, mix_norm_e, w_in_e, conv_w, conv_b, lru_wa, lru_ba, lru_wx, lru_bx, lru_lambda,
                 q_gain, k_gain, sinks, w_out_e, mix_norm_o, s5_lam_re, s5_lam_im, s5_log_step,
                 s5_b_re, s5_b_im, s5_c_re, s5_c_im, s5_d, w_glu, ffn_norm, w_up, w_down, out):
    w_in, w_out, w_gl = w_in_e[0], w_out_e[0], w_glu[0]
    ctx = ExitStack()
    with ctx:
        def sb(name, shape, dt=F32, on=ctx):
            return on.enter_context(nc.sbuf_tensor(name, shape, dt))

        def sem(name):
            return ctx.enter_context(nc.semaphore(name))

        tab_d = nc.dram_tensor("s5_tables", (KC, P, 2 * TPC * LH), F32, kind="Internal").ap()
        bbar_d = nc.dram_tensor("s5_bbar", (KC, P, 4 * TPC * SH), F32, kind="Internal").ap()

        xT = sb("xT", [P, KC, L])
        with ExitStack() as o:
            tab = sb("tab", [P, 2, 2, TPC, LH], on=o)
            bch = sb("bch", [P, KC, 4 * TPC * SH], on=o)
            craw = sb("craw", [P, 2, KC, HD], on=o)
        A1 = sb("A1", [P, KC, 2 * L], F32R)
        with ExitStack() as o:
            braw = sb("braw", [P, 2, NT, SH], on=o)
            btmp = sb("btmp", [P, 2, NT, SH], on=o)
            bbar = sb("bbar", [P, KC, 2, 2, 2, SH], on=o)
            s5w = sb("s5w", [P, 20, NT], on=o)
            prow = sb("prow", [N_PCOL, P], on=o)
            prow2 = sb("prow2", [N_PCOL2, P], on=o)
            lrow = sb("lrow", [P, P], on=o)
            srow = sb("srow", [1, 2 * NT + 2 * LC], on=o)
        with ExitStack() as o:
            xc = sb("xc", [P, LC, L], on=o)
            lr = sb("lr", [P, LC, L], on=o)
        A2 = sb("A2", [P, KC, 2 * L], F32R)
        raw = sb("raw", [P, NU, UK, TW])
        Wh = sb("Wh", [P, NU, UK, TW], F32R)
        Wl = sb("Wl", [P, NU, UK, TW], F32R)
        with ExitStack() as o:
            xin = sb("xin", [P, 2, D], on=o)
        with ExitStack() as o:
            ab = sb("ab", [P, 2, 2, 2, 2, LH], on=o)
            zb = sb("zb", [P, 2, 2, 2, LH], on=o)
            gb = sb("gb", [P, 2, 2, 2, LH], on=o)
            cdb = sb("cdb", [P, 2, 2, 2, 2, LH], on=o)
            hb = sb("hb", [P, 2, 2, 2, LH + 1], on=o)
            du = sb("du", [P, 2, L], on=o)
            yb = sb("yb", [P, 2, L], on=o)
            us = sb("us", [P, 2, 2, LH], on=o)
            uc = sb("uc", [P, 2, L], on=o)
            bx = sb("bx", [P, 2, 8, 2, 2, SH], on=o)
            cx = sb("cx", [P, 2, 2, P], on=o)
            bst = sb("bst", [P, 2, 4, P], on=o)
            cst = sb("cst", [P, 2, 4, P], on=o)
            ctm = sb("ctm", [P, 2, 2, P], on=o)
            k0 = sb("k0", [P, 2, 2 * SH], on=o)
        with ExitStack() as o:
            lt = sb("lt", [P, LC, L], on=o)
        qT = sb("qT", [P, LC, L])
        kvT = sb("kvT", [P, 2, L])
        with ExitStack() as o:
            li = sb("li", [P, LC, L], on=o)
        xb = sb("xb", [P, LC, L + 3])
        gT = sb("gT", [P, LC, L])
        wax = sb("wax", [P, 2, LC, P])
        with ExitStack() as o:
            la = sb("la", [P, LC, L], on=o)
        pb = sb("pb", [P, 2, NCH, P])
        pt = sb("pt", [P, 2, NCH, P])
        kd = sb("kd", [P, NKV, L])
        vw = sb("vw", [P, 3, P])
        rsel = sb("rsel", [NH, NH, HD])
        ctab = sb("ctab", [P, 2, 2, LH])
        ttmp = sb("ttmp", [P, 2, 2, 2, LH // 2])
        cross = sb("cross", [P, 2, 2, L])
        sq = sb("sq", [P, 2, L])
        ss = sb("ss", [P, 2, L])
        rs = sb("rs", [P, L])
        nv = sb("nv", [P, L])
        nw = sb("nw", [P, L])
        ident = sb("ident", [P, P])
        ones = sb("ones", [P, P])
        hsel = sb("hsel", [P, 34])
        pcol = sb("pcol", [P, N_PCOL])
        pcol2 = sb("pcol2", [P, N_PCOL2])
        lcol = sb("lcol", [P, 2, NT])
        scol = sb("scol", [P, NT + LC])
        rot1 = sb("rot1", [P, 2, NT])
        rho = sb("rho", [P, NT])
        rho2 = sb("rho2", [P, NT])
        lam = sb("lam", [P, 2, NT])
        ls = sb("ls", [P, 6, LC])
        par = sb("par", [P, 2])
        am = sb("am", [P, 2, 6, NCH])

        ps = ctx.enter_context(nc.psum_tensor("ps", [P, 4, 512], F32))
        px = ctx.enter_context(nc.psum_tensor("px", [P, 4, 512], F32))

        x_loaded = [sem(f"x_loaded{i}") for i in range(2)]
        gain_loaded = sem("gain_loaded")
        x_copied = [sem(f"x_copied{i}") for i in range(2)]
        gain_t = sem("gain_t")
        gain_ready = sem("gain_ready")
        par_loaded = sem("par_loaded")
        b_loaded = sem("b_loaded")
        wax_loaded = sem("wax_loaded")
        kd_loaded = sem("kd_loaded")
        landed = [sem(f"landed{s}") for s in range(NU)]
        tab_loaded = [sem(f"tab_loaded{s}") for s in range(2)]
        bc_loaded = sem("bc_loaded")
        tab_stored = sem("tab_stored")
        bbar_stored = sem("bbar_stored")
        out_stored = sem("out_stored")
        consts = sem("consts")
        hi_split = sem("hi_split")
        lo_split = sem("lo_split")
        unit_done = sem("unit_done")
        crossed = sem("crossed")
        pair_read = sem("pair_read")
        hid_ready = sem("hid_ready")
        op_hi = sem("op_hi")
        a1_ready = sem("a1_ready")
        a2_ready = sem("a2_ready")
        gated = sem("gated")
        x_final = sem("x_final")
        squared = sem("squared")
        rms_sum = sem("rms_sum")
        rms_var = sem("rms_var")
        rms_root = sem("rms_root")
        par_t = sem("par_t")
        par_ready = sem("par_ready")
        xt_done = sem("xt_done")
        dve_seq = sem("dve_seq")
        pool_seq = sem("pool_seq")
        s5_exp = sem("s5_exp")
        s5_arg = sem("s5_arg")
        s5_small = sem("s5_small")
        lru_sp = sem("lru_sp")
        xb_ready = sem("xb_ready")
        g_ready = sem("g_ready")
        conv_done = sem("conv_done")
        gates_mm = sem("gates_mm")
        gates_sg = sem("gates_sg")
        lru_a = sem("lru_a")
        lru_m2 = sem("lru_m2")
        lru_m = sem("lru_m")
        lru_h = sem("lru_h")
        lru_y = sem("lru_y")
        qk_sq = sem("qk_sq")
        qk_sum = sem("qk_sum")
        qk_var = sem("qk_var")
        qk_root = sem("qk_root")
        qk_norm = sem("qk_norm")
        qk_wide = sem("qk_wide")
        q_normed = sem("q_normed")
        kd_ready = sem("kd_ready")
        v_t = sem("v_t")
        v_ready = sem("v_ready")
        scored = sem("scored")
        maxed = sem("maxed")
        expd = sem("expd")
        probs = sem("probs")
        p_t = sem("p_t")
        p_copied = sem("p_copied")
        att_o = sem("att_o")
        s5_mask = sem("s5_mask")
        s5_tr = sem("s5_tr")
        s5_bst = sem("s5_bst")
        s5_neg = sem("s5_neg")
        s5_ca = sem("s5_ca")
        s5_k0 = sem("s5_k0")
        s5_k0r = sem("s5_k0r")
        s5_bu = sem("s5_bu")
        s5_rot = sem("s5_rot")
        s5_z = sem("s5_z")
        s5_g = sem("s5_g")
        s5_cs = sem("s5_cs")
        s5_sn = sem("s5_sn")
        s5_h = sem("s5_h")
        s5_y = sem("s5_y")
        s5_yf = sem("s5_yf")
        s5_ge = sem("s5_ge")
        bx_zero = sem("bx_zero")
        u_ready = sem("u_ready")
        zeroed = sem("zeroed")
        out_t = sem("out_t")
        out_c = sem("out_c")
        us_ready = [sem(f"us_ready{h}") for h in range(2)]
        block = ctx.enter_context(nc.Block())

        def bu_banks(h):
            return (px[:, 0:2], ps[:, 2:4])[h]

        def stack_input(copy, b, h):
            for j in range(2):
                tl = 2 * h + j
                for e in range(2):
                    last = copy(us[64 * j + 32 * e:64 * j + 32 * e + 32, b, h, :],
                                uc[32 * tl:32 * tl + 32, b, e * LH:e * LH + LH])
            return last

        root18 = pb[0:NH, 0].rearrange("p n q -> p (n q)")[:, 0:L]

        def squares_of(j, c):
            return pt[:, j % 2].rearrange("p n q -> p (n q)")[:, c * L:c * L + L]

        def wide_root(half):
            return px[:, half // 2, (half % 2) * L:(half % 2) * L + L]

        def copied(eng, i):
            eng.wait_ge(x_copied[i % 2], i // 2 + 1)

        def out_before(j):
            return {6: range(5), 7: range(5, 6), 8: range(6, 8)}[j]

        def sum_bank(n):
            return px[:, 1 if n == 3 else 3, 0:L]

        def gain(col):
            return pcol[:, bass.ds(col, 1)]

        def double_pairs(eng, n_pairs, body, *per_pair, first=0, last=0):
            for j in range(first):
                body(j, j % 2)
            mid = (n_pairs - first - last) // 2
            if mid:
                with trips(eng, mid, *per_pair) as i:
                    body(i * 2 + first, 0)
                    body(i * 2 + (first + 1), 1)
            for j in range(n_pairs - last, n_pairs):
                body(j, j % 2)

        @block.sync
        def _(sp):
            for i in range(2):
                sp.dma_start(xin[:, i, :], x[0, i * P:(i + 1) * P, :]).then_inc(x_loaded[i], 16)

            def load_pair(g, wide, row0, col0, turn=0):
                for s in range(NU):
                    if not (isinstance(g, int) and g == 0):
                        sp.wait_ge(lo_split, (g - 1) * NU + (s + 1))
                    src = wide[bass.ds(row0 + (s + turn) % NU * UK * P, UK * P), bass.ds(col0, TW)]
                    sp.dma_start(raw[:, s], src.rearrange("(c p) n -> p c n", p=P)).then_inc(landed[s], 16)

            def load_mlp(g0, layer, quarters=QTR):
                with sp.Fori(0, quarters) as q:
                    with sp.Fori(0, 8) as j:
                        load_pair(q * 16 + j + g0, w_up[layer], 0, q * D + j * TW)
                    with sp.Fori(0, 8) as j:
                        load_pair(q * 16 + j + (g0 + 8), w_down[layer], q * D, j * TW)

            load_pair(0, w_in, 0, QKV0)

            def rows(col, src, n):
                sp.dma_start(prow[col:col + n, :], src.rearrange("(c p) -> c p", p=P)).then_inc(par_loaded, 16)

            def rows2(col, src, n):
                sp.dma_start(prow2[col:col + n, :], src.rearrange("(c p) -> c p", p=P)).then_inc(par_loaded, 16)

            rows(G_MIX1, mix_norm_o[0], KC)
            rows(G_FF0, ffn_norm[0], KC)
            rows(G_FF1, ffn_norm[1], KC)
            rows(C_D, s5_d[0], KC)
            for k in range(4):
                rows(C_CW + k * LC, conv_w[0, k], LC)
            rows(C_CB, conv_b[0], LC)
            rows2(C_BA, lru_ba[0], LC)
            rows2(C_BX, lru_bx[0], LC)
            rows2(C_LAM, lru_lambda[0], LC)
            for col, src in ((C_QG, q_gain), (C_KG, k_gain)):
                for h in range(2):
                    sp.dma_start(prow2[col:col + 1, h * HD:h * HD + HD], src).then_inc(par_loaded, 16)
            sp.dma_start(lrow[0:NT, :], s5_lam_re[0].rearrange("(j g) p -> j (g p)", g=2)).then_inc(par_loaded, 16)
            sp.dma_start(lrow[NT:P, :], s5_lam_im[0].rearrange("(j g) p -> j (g p)", g=2)).then_inc(par_loaded, 16)
            sp.dma_start(srow[0:1, 0:2 * NT], s5_log_step).then_inc(par_loaded, 16)
            sp.dma_start(srow[0:1, 2 * NT:], sinks).then_inc(par_loaded, 16)
            for k, s5_b in enumerate((s5_b_re, s5_b_im)):
                sp.dma_start(braw[:, k], s5_b[0].rearrange("(j g) p h -> (g p) j h", g=2)).then_inc(b_loaded, 16)
            sp.wait_ge(zeroed, 1)
            for k, w in enumerate((lru_wa, lru_wx)):
                for h in range(2):
                    half = slice(64 * h, 64 * h + 64)
                    sp.dma_start(wax[half, k, :, half],
                                  w[0].rearrange("(c h) i j -> h i c j", h=2)[h]).then_inc(wax_loaded, 16)

            with sp.Fori(1, 5) as j:
                load_pair(j + P_Q, w_in, 0, j * TW + QKV0)
            with sp.Fori(0, 8) as j:
                load_pair(j + P_XB, w_in, 0, j * TW)
            for j in range(8):
                load_pair(P_OUT + j, w_out, 0, j * TW, turn=2)
            load_mlp(P_MLP0, 0, QTR - 1)
            g = P_MLP0 + 16 * (QTR - 1)
            with sp.Fori(0, 8) as j:
                load_pair(j + g, w_up[0], 0, j * TW + (QTR - 1) * D)
            for j in range(2):
                load_pair(g + 8 + j, w_down[0], (QTR - 1) * D, j * TW)
            sp.wait_ge(unit_done, (g + 8) * NU)
            sp.wait_ge(bbar_stored, 32)
            sp.dma_start(bch[:, :, :], bbar_d.rearrange("c p f -> p c f")).then_inc(bc_loaded, 16)
            for k, s5_c in enumerate((s5_c_re, s5_c_im)):
                rows = s5_c[0].rearrange("g h p -> (g h) p")
                sp.dma_start(craw[:, k], rows.rearrange("(c p) n -> p c n", p=P)).then_inc(bc_loaded, 16)

            def load_tables(c, b):
                for h in range(2):
                    if not isinstance(c, int):
                        sp.wait_ge(s5_h, c * 2 + (h - 3))
                    sp.dma_start(tab[:, b, :, 2 * h:2 * h + 2].rearrange("p k j t -> p k (j t)"),
                                 tab_d[bass.ds(c, 1)].rearrange("o p (k h f) -> h p (o k) f", k=2, h=2)[h])\
                        .then_inc(tab_loaded[b], 16)

            sp.wait_ge(tab_stored, KC * 32)
            for c in range(2):
                load_tables(c, c)
            with sp.Fori(2, 8) as j:
                load_pair(j + (g + 8), w_down[0], (QTR - 1) * D, j * TW)
            for j in range(2):
                load_pair(P_GLU + j, w_gl, 0, j * D)
            with sp.Fori(1, KC // 2) as i:
                for b in range(2):
                    load_tables(i * 2 + b, b)
            with sp.Fori(1, 8) as j:
                for h in range(2):
                    load_pair(j * 2 + (h + P_GLU), w_gl, 0, j * TW + h * D)
            load_mlp(P_MLP1, 1)
            with sp.Fori(0, KC // 2) as i:
                sp.wait_ge(out_c, i + 1)
                sp.dma_start(out[0].rearrange("(a p) d -> p a d", p=P)[:, :, bass.ds(i * TW, TW)],
                             xin.rearrange("p a (i d) -> p a i d", i=8)[:, :, bass.ds(i, 1), :]
                             .rearrange("p a o d -> p a (o d)")).then_inc(out_stored, 16)
            sp.wait_ge(out_stored, 16 * (KC // 2))

        @block.tensor
        def _(pe):
            mm = nc.tensor.matmul

            pe.wait_ge(consts, 1)
            pe.wait_ge(gain_loaded, 16)
            nc.tensor.transpose(px[:, 3, 0:KC], prow[0:KC, :], ident[0:KC, 0:KC]).then_inc(gain_t, 1)
            for i in range(2):
                pe.wait_ge(x_loaded[i], 16)
            for i in range(KC // 2):
                if i >= 3:
                    pe.wait_ge(op_hi, i - 2)
                    copied(pe, i - 3)
                for c in range(2):
                    for a in range(2):
                        last = nc.tensor.transpose(px[:, i % 3, c * L + a * P:c * L + a * P + P],
                                                   xin[:, a, bass.ts(2 * i + c, P)], ident[:, :])
                last.then_inc(xt_done, 1)

            def pair(g, d, A, ready=None, base=0, per_unit=0, turn=0, beside=None):
                b = 2 * d
                if not (isinstance(g, int) and g < 2):
                    pe.wait_ge(pair_read, g - 1)
                for s in range(NU):
                    pe.wait_ge(lo_split, g * NU + (s + 1))
                    if ready is not None:
                        pe.wait_ge(ready, base + per_unit * (s + 1))
                    for t in range(2):
                        for c in range(UK):
                            n = s * UK + c
                            k = (n + turn * UK) % KC
                            cols = slice(t * P, t * P + P)
                            wide = lambda: mm(ps[:, b + t, :], Wh[:, s, c, cols], A[:, k, :],
                                              start=(n == 0), stop=(n == KC - 1))
                            half = lambda: mm(ps[:, b + t, 0:L], Wl[:, s, c, cols], A[:, k, 0:L],
                                              start=False, stop=False)
                            if n == KC - 1:
                                half()
                                last = wide()
                            else:
                                wide()
                                last = half()
                    last.then_inc(unit_done, 1)
                    if beside:
                        beside(s)

            def channel_sum(n):
                pe.wait_ge(squared, 8 * n)
                mm(sum_bank(n), ones[:, :], ss[:, 0], start=True, stop=False)
                mm(sum_bank(n), ones[:, :], ss[:, 1], start=False, stop=True).then_inc(rms_sum, 1)

            def phase(g0, n, A, **ready):
                def body(j, d):
                    pair(j + g0, (g0 + d) % 2, A, **ready)
                double_pairs(pe, n, body)

            def parameters():
                pe.wait_ge(gain_ready, 1)
                pe.wait_ge(par_loaded, 16 * N_PAR)
                row = px[:, 3]
                nc.tensor.transpose(row[:, 0:N_PCOL], prow[:, :], ident[0:N_PCOL, 0:N_PCOL])
                nc.tensor.transpose(row[:, 120:120 + N_PCOL2], prow2[:, :], ident[0:N_PCOL2, 0:N_PCOL2])
                nc.tensor.transpose(row[:, 146:146 + P], lrow[:, :], ident[:, :])
                steps = srow[0:1, 0:2 * NT].rearrange("a (j g) -> a g j", g=2)
                snk = srow[0:1, 2 * NT:].rearrange("a (j g) -> a g j", g=2)
                for g in range(2):
                    mm(row[64 * g:64 * g + 64, 274:274 + NT], ones[0:1, 0:64], steps[:, g], start=True, stop=True)
                    last = mm(row[64 * g:64 * g + 64, 274 + NT:274 + NT + LC], ones[0:1, 0:64], snk[:, g],
                              start=True, stop=True)
                last.then_inc(par_t, 1)

            pair(0, 0, A1, a1_ready, 0, 2)
            parameters()
            pair(1, 1, A1)
            pe.wait_ge(par_ready, 1)
            channel_sum(1)
            def head_sums(j):
                pe.wait_ge(qk_sq, j + 1)
                for c in range(2 if j < 4 else 1):
                    i = 2 * j + c
                    last = mm(px[0:NH, 3, L:2 * L], hsel[:, 16 - 2 * i:16 - 2 * i + NH], squares_of(j, c),
                              start=(i == 0), stop=(i == LC))
                last.then_inc(qk_sum, 1)

            pair(2, 0, A1)
            head_sums(0)
            head_sums(1)
            for g in range(3, P_XB):
                pair(g, g % 2, A1)
                head_sums(g - 1)

            def values():
                for w in range(3):
                    last = nc.tensor.transpose(px[:, 2, w * P:w * P + P], kvT[:, 1, w * CH:w * CH + P], ident[:, :])
                last.then_inc(v_t, 1)

            def widen(i, half):
                return mm(px[:, half // 2, (half % 2) * L:(half % 2) * L + L],
                          rsel[:, 2 * i:2 * i + 2, :].rearrange("p h n -> p (h n)"), root18[:, :],
                          start=True, stop=True)

            def scores(i):
                if i < 2:
                    pe.wait_ge(q_normed, i + 1)
                    pe.wait_ge(kd_loaded, 32)
                if i >= 2:
                    pe.wait_ge(expd, i - 1)
                for n in range(NCH):
                    for h in range(2):
                        half = slice(64 * h, 64 * h + 64)
                        k0 = max(n - 1, 0) * CH
                        nk = P if n else CH
                        last = mm(px[half, i % 2, n * P:n * P + nk], qT[half, i, n * CH:n * CH + CH],
                                  kd[half, i // 4, k0:k0 + nk], start=True, stop=True)
                last.then_inc(scored, 1)

            def transpose_probs(i):
                pe.wait_ge(probs, i + 1)
                if i >= 1:
                    pe.wait_ge(p_copied, i)
                for n in range(NCH):
                    nk = P if n else CH
                    last = nc.tensor.transpose(px[0:nk, 2, n * P:n * P + P], pb[:, i % 2, n, 0:nk], ident[:, :])
                last.then_inc(p_t, 1)

            def weigh_values(i):
                pe.wait_ge(p_copied, i + 1)
                if i >= 1:
                    pe.wait_ge(a2_ready, i)
                for n in range(NCH):
                    for h in range(2):
                        nk = P if n else CH
                        last = mm(px[64 * h:64 * h + 64, 3, n * CH:n * CH + CH],
                                  vw[0:nk, max(n - 1, 0), 64 * (i // 4):64 * (i // 4) + 64],
                                  pt[0:nk, i % 2, n, 64 * h:64 * h + 64], start=True, stop=True)
                last.then_inc(att_o, 1)

            def gates(c):
                if c == 0:
                    pe.wait_ge(wax_loaded, 64)
                    pe.wait_ge(expd, LC)
                pe.wait_ge(conv_done, c // 2 + 1)
                if c >= 2:
                    pe.wait_ge(gates_sg, c - 1)
                for k in range(2):
                    last = mm(px[:, c % 2, k * L:k * L + L], wax[:, k, c, :], xc[:, c, :], start=True, stop=True)
                last.then_inc(gates_mm, 1)

            def beside(n):
                if n == SLOT_SUM:
                    head_sums(4)
                    values()
                if n == SLOT_WIDE:
                    pe.wait_ge(qk_norm, 1)
                    pe.wait_ge(zeroed, 2)
                    pe.wait_ge(v_ready, 1)
                    widen(LC, 7)
                    for i in range(LC - 1):
                        last = widen(i, i)
                    last.then_inc(qk_wide, 1)
                if n == SLOT_Q:
                    pe.wait_ge(kd_ready, 1)
                    widen(LC - 1, 7).then_inc(qk_wide, 1)
                i, odd = divmod(n - ATT0, 2)
                if not odd and 0 <= i < LC:
                    scores(i)
                if not odd and 0 <= i - 2 < LC:
                    transpose_probs(i - 2)
                if odd and 0 <= i - 2 < LC:
                    weigh_values(i - 2)
                if 0 <= n - GATE0 < LC:
                    gates(n - GATE0)

            for g in range(P_XB, P_OUT):
                pair(g, g % 2, A1, beside=lambda s: beside((g - P_XB) * NU + s))

            pair(P_OUT, P_OUT % 2, A2, turn=2, ready=a2_ready, base=0, per_unit=4)
            double_pairs(pe, 7, lambda j, d: pair(j + (P_OUT + 1), (P_OUT + 1 + d) % 2, A2, turn=2), last=1)

            def mlp(g0, a1_at, a1_unit, a2_at, norm, last_hook=None):
                def up(j, d, q=0, quarter0=True):
                    pair(q * 16 + j + g0, (g0 + d) % 2, A1, a1_ready, a1_at, a1_unit)
                    if quarter0 and isinstance(j, int) and j == 0:
                        channel_sum(norm)

                def down(j, d, q=0):
                    pair(q * 16 + j + (g0 + 8), (g0 + d) % 2, A2, a2_ready, q * 8 + a2_at, 2)

                double_pairs(pe, 8, up, first=2)
                double_pairs(pe, 8, down)
                with pe.Fori(1, QTR - 1) as q:
                    double_pairs(pe, 8, lambda j, d: up(j, d, q, False))
                    double_pairs(pe, 8, lambda j, d: down(j, d, q))
                double_pairs(pe, 8, lambda j, d: up(j, d, QTR - 1, False))

                def last_down(j, d):
                    if last_hook and isinstance(j, int):
                        last_hook(j)
                    down(j, d, QTR - 1)
                double_pairs(pe, 8, last_down, last=2 if last_hook else 0)

            mlp(P_MLP0, 8, 2, 16, 2)

            def s5_prepare(c, b):
                pe.wait_ge(s5_mask, c + 1)
                if not isinstance(c, int) or c >= 1:
                    pe.wait_ge(s5_k0r, c)
                for k in range(4):
                    nc.tensor.transpose(px[:, 2, k * P:k * P + P],
                                        bx[:, b, 2 * k:2 * k + 2].rearrange("p t e g h -> p (t e g h)"), ident[:, :])
                for k in range(2):
                    last = nc.tensor.transpose(px[:, 3, k * P:k * P + P], cx[:, b, k], ident[:, :])
                last.then_inc(s5_tr, 1)

            def s5_direct(c, b):
                pe.wait_ge(s5_neg, c + 1)
                for tl in range(TPC):
                    own = slice(32 * tl, 32 * tl + 32)
                    for k in range(2):
                        last = mm(px[own, 3, 2 * P:2 * P + 32],
                                  bx[:, b, 4 * (tl // 2) + 2 * k + tl % 2, 1].rearrange("p g h -> p (g h)"), cst[:, b, k, own],
                                  start=(k == 0), stop=(k == 1))
                last.then_inc(s5_k0, 1)

            def s5_in(v, c, b, h):
                if not isinstance(v, int) or v >= 2:
                    pe.wait_ge(s5_rot, v - 1)
                if h == 0:
                    pe.wait_ge(s5_bst, c + 1)
                pe.wait_ge(us_ready[h], c + 1)
                for j in range(2):
                    rows = slice(64 * j, 64 * j + 64)
                    for k in range(2):
                        last = mm(bu_banks(h)[:, j, k * LH:k * LH + LH], bst[rows, b, 2 * h + k, :], us[rows, b, h, :],
                                  start=True, stop=True)
                last.then_inc(s5_bu, 1)

            def s5_out(v, c, b, h):
                if h == 0:
                    for tl in range(TPC):
                        own = slice(32 * tl, 32 * tl + 32)
                        mm(ps[own, b, 0:LH], k0[own, b, :], uc[own, b, 0:LH], start=True, stop=False)
                pe.wait_ge(s5_h, v + 1)
                for j in range(2):
                    own = slice(32 * (2 * h + j), 32 * (2 * h + j) + 32)
                    even, odd, re, im = ps[own, b, 0:LH], ps[own, b, LH:L], hb[:, h, 0, j], hb[:, h, 1, j]
                    mm(even, cst[:, b, 2, own], re[:, 0:LH], start=False, stop=False)
                    mm(even, cst[:, b, 3, own], im[:, 0:LH], start=False, stop=True)
                    mm(odd, cst[:, b, 0, own], re[:, 1:LH + 1], start=True, stop=False)
                    last = mm(odd, cst[:, b, 1, own], im[:, 1:LH + 1], start=False, stop=True)
                last.then_inc(s5_y, 1)

            def s5_trip(i, more):
                for b in range(2):
                    c, following = i * 2 + b, b == 0 or more
                    for h in range(2):
                        v = i * 4 + (2 * b + h)
                        if h == 0:
                            pe.wait_ge(s5_ca, c + 1)
                            pe.wait_ge(s5_k0r, c + 1)
                            if not isinstance(c, int) or c >= 2:
                                pe.wait_ge(s5_yf, c - 1)
                        if following:
                            s5_in(v + 2, c + 1, 1 - b, h)
                        if h == 1 and more:
                            s5_prepare(c + 2, b)
                        s5_out(v, c, b, h)
                        if h == 0 and following:
                            s5_direct(c + 1, 1 - b)

            s5_prepare(0, 0)
            s5_direct(0, 0)
            s5_prepare(1, 1)
            channel_sum(3)
            pe.wait_ge(pair_read, P_GLU)
            pe.wait_ge(rms_var, 3)
            for h in range(2):
                s5_in(h, 0, 0, h)
            s5_trip(0, True)
            with pe.Fori(1, KC // 2 - 1) as i:
                s5_trip(i, True)
            s5_trip(KC // 2 - 1, False)

            phase(P_GLU, 16, A2, ready=a2_ready, base=48, per_unit=4)
            def frames_major(i):
                pe.wait_ge(x_final, 73 + i)
                if i >= 2:
                    pe.wait_ge(out_c, i - 1)
                for a in range(2):
                    for c in range(2):
                        last = nc.tensor.transpose(px[:, i % 2, (2 * a + c) * P:(2 * a + c + 1) * P],
                                                   xT[:, 2 * i + c, a * P:a * P + P], ident[:, :])
                last.then_inc(out_t, 1)

            def finished(j):
                for i in out_before(j):
                    frames_major(i)
            mlp(P_MLP1, 16, 2, 64, 4, finished)
            finished(8)

        @block.scalar
        def _(act):
            fn = nc.scalar.activation
            act.dma_start(prow[0:KC, :], mix_norm_e[0].rearrange("(c p) -> c p", p=P)).then_inc(gain_loaded, 16)
            hi = Tally(op_hi)
            xf = Tally(x_final)
            hid = Tally(hid_ready)
            var = Tally(rms_var)
            root = Tally(rms_root)
            gate = Tally(gated)

            act.preload_act_table(ACT.Copy)
            def split(g, s):
                act.wait_ge(landed[s], (g + 1) * 16)
                if not (isinstance(g, int) and g == 0):
                    act.wait_ge(unit_done, (g - 1) * NU + (s + 1))
                fn(Wh[:, s], raw[:, s], ACT.Copy).then_inc(hi_split, 1)

            def pair(g, d, nxt=True, before=None, beside=None):
                if nxt:
                    for s in range(NU):
                        split(g + 1, s)
                        if beside:
                            beside(s)
                if before:
                    before()
                act.wait_ge(unit_done, (g + 1) * NU)
                fn(cross[:, d], ps[:, 2 * d:2 * d + 2, L:2 * L], ACT.Copy).then_inc(crossed, 1)

            def rms():
                act.preload_act_table(ACT.Sqrt)
                var.wait(act)
                root.inc(fn(rs[:, :], nv[:, :], ACT.Sqrt))

            def operand_from_x(j, col):
                xf.wait(act)
                for c in range(2):
                    last = fn(A1[:, bass.ds(j * 2 + c, 1), 0:L], xT[:, bass.ds(j * 2 + c, 1), :], ACT.Copy,
                              scale=gain(j * 2 + (col + c)))
                hi.inc(last)

            act.wait_ge(gain_ready, 1)
            for i in range(KC // 2):
                act.wait_ge(xt_done, i + 1)
                src = px[:, i % 3, :].rearrange("p (c t) -> p c t", c=2)
                if i % 2 == 0:
                    fn(xT[:, 2 * i:2 * i + 2, :], src, ACT.Copy).then_inc(x_copied[0], 1)
                for c in range(2):
                    last = fn(A1[:, 2 * i + c, 0:L], src[:, c], ACT.Copy, scale=gain(G_MIX0 + 2 * i + c))
                hi.inc(last)
                if i % 2 == 1:
                    split(0, i // 2)

            pair(0, 0)
            pair(1, 1)
            rms()
            act.wait_ge(par_ready, 1)
            fn(s5w[:, 0, :], scol[:, 0:NT], ACT.Exp).then_inc(s5_exp, 1)
            pair(2, 0)
            act.wait_ge(s5_arg, 2)
            fn(s5w[:, 7, :], s5w[:, 1, :], ACT.Exp)
            fn(s5w[:, 8, :], s5w[:, 6, :], ACT.Tanh, scale=0.5)
            fn(ls[:, 1, :], ls[:, 0, :], ACT.Exp, scale=-1.0)
            fn(s5w[:, 4, :], s5w[:, 4, :], ACT.Sin)
            fn(s5w[:, 5, :], s5w[:, 5, :], ACT.Sin).then_inc(s5_exp, 1)
            pair(3, 1)
            pair(4, 0)

            def softmax_exp(i):
                d = i % 2
                act.wait_ge(maxed, i + 1)
                if i >= 2:
                    act.wait_ge(p_t, i - 1)
                for n in range(NCH):
                    nk = P if n else CH
                    fn(pb[:, d, n, 0:nk], px[:, d, n * P:n * P + nk], ACT.Exp, bias=am[:, d, 1, n:n + 1],
                       scale=HD ** -0.5, accum_out=am[:, d, 2, n:n + 1])
                fn(am[:, d, 3, :], am[:, d, 1, :], ACT.Exp, bias=scol[:, NT + i:NT + i + 1]).then_inc(expd, 1)

            def copy_probs(i):
                d = i % 2
                act.wait_ge(p_t, i + 1)
                fn(pt[0:64, d, 0, :], px[0:64, 2, 0:P], ACT.Copy)
                fn(pt[:, d, 1:NCH, :], px[:, 2, P:NCH * P].rearrange("p (n q) -> p n q", n=NCH - 1), ACT.Copy)\
                    .then_inc(p_copied, 1)

            def attended(i):
                if i == 0:
                    act.wait_ge(bbar_stored, 32)
                act.wait_ge(att_o, i + 1)
                hi.inc(fn(A2[:, LC + i, 0:L], px[:, 3, 0:L], ACT.Copy))

            def gates(c):
                act.wait_ge(gates_mm, c + 1)
                fn(lr[:, c], px[:, c % 2, 0:L], ACT.Sigmoid, bias=pcol2[:, C_BA + c:C_BA + c + 1])
                fn(li[:, c], px[:, c % 2, L:2 * L], ACT.Sigmoid, bias=pcol2[:, C_BX + c:C_BX + c + 1])\
                    .then_inc(gates_sg, 1)

            def beside(n):
                if n == SLOT_ROOT:
                    act.wait_ge(qk_var, 1)
                    fn(root18[:, :], nv[0:NH, :], ACT.Sqrt).then_inc(qk_root, 1)
                if n == SLOT_Q:
                    act.wait_ge(kd_ready, 1)
                    act.dma_start(kd[64:P, 0, :], kvT[0:64, 0, :]).then_inc(kd_loaded, 16)
                    act.dma_start(kd[0:64, 1, :], kvT[64:P, 0, :]).then_inc(kd_loaded, 16)
                i, odd = divmod(n - ATT0, 2)
                if odd and 0 <= i < LC:
                    softmax_exp(i)
                if not odd and 0 <= i - 2 < LC:
                    copy_probs(i - 2)
                if odd and 0 <= i - 2 < LC:
                    attended(i - 2)
                if 0 <= n - GATE0 < LC:
                    gates(n - GATE0)
                if n == GATE0 + LC:
                    act.wait_ge(gates_sg, LC)
                    act.wait_ge(lru_sp, 1)
                    for c in range(LC):
                        fn(lt[:, c], lr[:, c], ACT.Tanh, scale=ls[:, 4, c:c + 1])
                if n == GATE0 + LC + 1:
                    for c in range(LC):
                        fn(lr[:, c], lr[:, c], ACT.Exp, scale=ls[:, 5, c:c + 1]).then_inc(lru_a, 1)

            for g in range(P_XB, P_OUT):
                pair(g, g % 2, beside=lambda s: beside((g - P_XB) * NU + s))

            for c in range(0, LC, 4):
                act.wait_ge(lru_m2, c // 4 + 1)
                fn(lt[:, c:c + 4], lt[:, c:c + 4], ACT.Sqrt).then_inc(lru_m, 1)
            act.wait_ge(g_ready, 4)
            for c in range(0, LC, 4):
                fn(gT[:, c:c + 4], gT[:, c:c + 4], ACT.Gelu_apprx_tanh).then_inc(lru_h, 1)
            for c in range(LC):
                act.wait_ge(lru_y, c + 1)
                hi.inc(fn(A2[:, c, 0:L], gT[:, c], ACT.Copy))

            def out_pair(j, d):
                pair(j + P_OUT, (P_OUT + d) % 2)
                operand_from_x(j, G_FF0)
            double_pairs(act, 8, out_pair, (hi, 2), (xf, 2))

            def store_frames(j):
                for i in out_before(j):
                    act.wait_ge(out_t, i + 1)
                    fn(xin.rearrange("p a (i d) -> p a i d", i=8)[:, :, i, :],
                       px[:, i % 2, :].rearrange("p (a d) -> p a d", a=2), ACT.Copy).then_inc(out_c, 1)

            def mlp(g0, final):
                def up(j, d, q=0, quarter0=True):
                    pair(q * 16 + j + g0, (g0 + d) % 2,
                         before=rms if quarter0 and isinstance(j, int) and j == 0 else None)
                    hid.wait(act)
                    c = (g0 + d) % 2
                    hi.inc(fn(A2[:, bass.ds(j * 2, 2), 0:L], cross[:, c], ACT.Copy))

                def down(j, d, q=0, nxt=True):
                    pair(q * 16 + j + (g0 + 8), (g0 + d) % 2, nxt=nxt)

                double_pairs(act, 8, up, (hi, 2), (hid, 2), first=2)
                double_pairs(act, 8, down)
                with trips(act, QTR - 2, (hi, 8), (hid, 8)) as q:
                    double_pairs(act, 8, lambda j, d: up(j, d, q + 1, False), (hi, 2), (hid, 2))
                    double_pairs(act, 8, lambda j, d: down(j, d, q + 1))
                double_pairs(act, 8, lambda j, d: up(j, d, QTR - 1, False), (hi, 2), (hid, 2))
                xf.skip(8 * (QTR - 1))
                if not final:
                    double_pairs(act, 8, lambda j, d: down(j, d, QTR - 1))
                    xf.skip(8)
                else:
                    def last_down(j, d):
                        if isinstance(j, int):
                            store_frames(j)
                        down(j, d, QTR - 1, nxt=not (isinstance(j, int) and j == 7))
                    double_pairs(act, 8, last_down, last=2)
                    store_frames(8)

            mlp(P_MLP0, False)

            act.wait_ge(bc_loaded, 48)
            act.wait_ge(bx_zero, 1)

            def s5_masks(c, b):
                if not isinstance(c, int) or c >= 2:
                    act.wait_ge(s5_tr, c - 1)
                    act.wait_ge(s5_k0, c - 1)
                for g in range(2):
                    half = slice(64 * g, 64 * g + 64)
                    fn(bx[half, b, :, :, g, :],
                       bch[half, bass.ds(c, 1), :].rearrange("p o (e m h) -> p (o m) e h", e=2, h=SH), ACT.Copy)
                for g in range(2):
                    last = fn(cx[:, b, :, 64 * g:64 * g + 64],
                              craw[:, :, bass.ds(c, 1), :].rearrange("p k o n -> p (k o) n"), ACT.Copy,
                              scale=par[:, g:g + 1])
                last.then_inc(s5_mask, 1)

            def s5_stationary_b(c, b):
                act.wait_ge(s5_tr, c + 1)
                if not isinstance(c, int) or c >= 2:
                    act.wait_ge(s5_bu, c * 2 - 2)
                fn(bst[:, b].rearrange("p k n -> p (k n)"), px[:, 2, :], ACT.Copy).then_inc(s5_bst, 1)

            def s5_stationary_c(c, b):
                if not isinstance(c, int) or c >= 2:
                    act.wait_ge(s5_y, c * 2 - 2)
                fn(cst[:, b, 0], px[:, 3, 0:P], ACT.Copy)
                fn(cst[:, b, 1], px[:, 3, P:2 * P], ACT.Copy, scale=-1.0).then_inc(s5_neg, 1)

            def s5_stack(c, b):
                act.wait_ge(u_ready, c + 1)
                if not isinstance(c, int) or c >= 2:
                    act.wait_ge(s5_bu, c * 2 - 2)
                stack_input(lambda out_, in_: fn(out_, in_, ACT.Copy), b, 1).then_inc(us_ready[1], 1)

            def s5_direct(c, b):
                act.wait_ge(s5_k0, c + 1)
                fn(k0[:, b], px[:, 3, 2 * P:2 * P + 32], ACT.Copy).then_inc(s5_k0r, 1)

            def s5_gelu(c, b):
                act.wait_ge(s5_yf, c + 1)
                fn(yb[:, b], yb[:, b], ACT.Gelu_apprx_tanh).then_inc(s5_ge, 1)
                act.wait_ge(s5_ge, c + 1)
                hi.inc(fn(A2[:, bass.ds(c, 1), 0:L], yb[:, b:b + 1], ACT.Copy))

            s5_masks(0, 0)
            s5_stationary_b(0, 0)
            s5_stationary_c(0, 0)
            s5_direct(0, 0)
            s5_masks(1, 1)
            s5_stationary_b(1, 1)
            rms()
            act.preload_act_table(ACT.Gelu_apprx_tanh)
            s5_stack(0, 0)

            def s5_chunk(c, b, gelu=True, more=2):
                if more >= 1:
                    s5_stationary_c(c + 1, 1 - b)
                    s5_stack(c + 1, 1 - b)
                if more >= 2:
                    s5_masks(c + 2, b)
                if gelu:
                    s5_gelu(c - 1, 1 - b)
                if more >= 1:
                    s5_direct(c + 1, 1 - b)
                if more >= 2:
                    s5_stationary_b(c + 2, b)

            s5_chunk(0, 0, gelu=False)
            s5_chunk(1, 1)
            with trips(act, KC // 2 - 2, (hi, 2)) as i:
                s5_chunk(i * 2 + 2, 0)
                s5_chunk(i * 2 + 3, 1)
            s5_chunk(KC - 2, 0, more=1)
            s5_chunk(KC - 1, 1, more=0)
            s5_gelu(KC - 1, 1)

            act.preload_act_table(ACT.Sigmoid)

            def glu(j, d):
                c = (P_GLU + d) % 2
                pair(j + P_GLU, c)
                if d == 1:
                    act.wait_ge(pair_read, j + (P_GLU + 1))
                    gate.inc(fn(cross[:, c], cross[:, c], ACT.Sigmoid))
                    xf.wait(act)
                    for k in range(2):
                        last = fn(A1[:, bass.ds(j + (k - 1), 1), 0:L], xT[:, bass.ds(j + (k - 1), 1), :], ACT.Copy,
                                  scale=gain(j + (G_FF1 + k - 1)))
                    hi.inc(last)
            double_pairs(act, 16, glu, (hi, 1), (xf, 1), (gate, 1))
            mlp(P_MLP1, True)

        @block.vector
        def _(dve):
            tt, ts, stt = nc.vector.tensor_tensor, nc.vector.tensor_scalar, nc.vector.scalar_tensor_tensor
            seq = Tally(dve_seq)
            hi = Tally(op_hi)
            sums = Tally(rms_sum)
            root = Tally(rms_root)
            gate = Tally(gated)

            def link(ins):
                seq.inc(ins)
                seq.again(dve)

            def split(g, s):
                dve.wait_ge(hi_split, g * NU + (s + 1))
                tt(Wl[:, s], raw[:, s], Wh[:, s].bitcast(F32), ALU.subtract).then_inc(lo_split, 1)

            def parameters():
                dve.wait_ge(par_t, 1)
                row = px[:, 3]
                nc.vector.tensor_copy(pcol[:, KC:N_PCOL], row[:, KC:N_PCOL])
                nc.vector.tensor_copy(pcol2[:, :], row[:, 120:120 + N_PCOL2])
                nc.vector.tensor_copy(lcol[:, :, :], row[:, 146:146 + P].rearrange("p (k j) -> p k j", k=2))
                nc.vector.tensor_copy(scol[:, :], row[:, 274:274 + NT + LC]).then_inc(par_ready, 1)
                dve.wait_ge(par_ready, 1)
                idv = ident.rearrange("p (a g h) -> p g a h", g=2, h=SH)
                link(nc.vector.tensor_reduce(par[:, :], idv, AX.XY, ALU.add))
                link(ts(ls[:, 1, :], pcol2[:, C_LAM:C_LAM + LC], -1.0, None, ALU.mult))
                tt(ls[:, 0, :], ls[:, 1, :], pcol2[:, C_LAM:C_LAM + LC], ALU.max).then_inc(s5_arg, 1)

            dve.wait_ge(gain_t, 1)
            nc.vector.tensor_copy(pcol[:, 0:KC], px[:, 3, 0:KC]).then_inc(gain_ready, 1)
            dve.wait_ge(gain_ready, 1)
            for i in range(KC // 2):
                hi.wait(dve)
                if i % 2 == 1:
                    src = px[:, i % 3, :].rearrange("p (c t) -> p c t", c=2)
                    nc.vector.tensor_copy(xT[:, 2 * i:2 * i + 2, :], src).then_inc(x_copied[1], 1)
                copied(dve, i)
                for c in range(2):
                    k = 2 * i + c
                    last = stt(A1[:, k, L:2 * L], xT[:, k, :], gain(G_MIX0 + k), A1[:, k, 0:L].bitcast(F32),
                               ALU.mult, ALU.subtract)
                last.then_inc(a1_ready, 1)
                if i % 2 == 1:
                    split(0, i // 2)

            def inv_root(v, r, w, done=None):
                link(nc.vector.reciprocal(r, r))
                link(tt(w, r, r, ALU.mult))
                link(tt(w, w, v, ALU.mult))
                link(ts(w, w, -0.5, 1.5, ALU.mult, ALU.add))
                if done is None:
                    link(tt(r, r, w, ALU.mult))
                else:
                    tt(r, r, w, ALU.mult).then_inc(done, 1)

            def rms():
                sums.wait(dve)
                ts(nv[:, :], sum_bank(sums.value), 1.0 / D, EPS, ALU.mult, ALU.add).then_inc(rms_var, 1)
                root.wait(dve)
                inv_root(nv[:, :], rs[:, :], nw[:, :])

            rs2 = rs[:, :].unsqueeze(1).to_broadcast([P, 2, L])

            def pair(g, d, nxt=True, before=None, beside=None, dest=None):
                if nxt:
                    for s in range(NU):
                        split(g + 1, s)
                        if beside:
                            beside(s)
                if before:
                    before()
                dve.wait_ge(crossed, g + 1)
                tt(cross[:, d] if dest is None else dest, ps[:, 2 * d:2 * d + 2, 0:L], cross[:, d], ALU.add)\
                    .then_inc(pair_read, 1)
                dve.wait_ge(pair_read, g + 1)

            def projection(g, d, dest, **kw):
                pair(g, d, **kw)
                link(tt(dest, cross[:, d], rs2, ALU.mult))

            def residual(j, d):
                xs = xT[:, bass.ds(j * 2, 2), :]
                tt(xs, xs, cross[:, d], ALU.add).then_inc(x_final, 1)

            def operand_from_x(j, col):
                hi.wait(dve)
                for c in range(2):
                    k = bass.ds(j + c, 1)
                    last = stt(A1[:, k, L:2 * L], xT[:, k, :], gain(j + (col + c)), A1[:, k, 0:L].bitcast(F32),
                               ALU.mult, ALU.subtract)
                last.then_inc(a1_ready, 1)

            W = [s5w[:, k, :] for k in range(20)]
            step, a, hb, tmp, s2, c2, ac, ea, th = W[:9]
            lre, lim = lcol[:, 0, :], lcol[:, 1, :]
            em1, mask, t1, t2_, sinb, cosb, X, Y = W[9:17]
            cr, ci, n2 = W[17], W[18], W[19]
            S = [ls[:, k, :] for k in range(6)]

            def s5_arguments(part):
                if part == 0:
                    dve.wait_ge(s5_exp, 1)
                    link(tt(a, lre, step, ALU.mult))
                    link(tt(hb, lim, step, ALU.mult))
                    link(ts(hb, hb, 0.5, None, ALU.mult))
                    link(ts(ac, a, -1.0, 1.0, ALU.max, ALU.min))
                    for out_, turn in ((s2, 0.0), (c2, 0.25)):
                        link(ts(tmp, hb, TWO_PI_INV, turn, ALU.mult, ALU.add))
                        link(ts(tmp, tmp, MAGIC, None, ALU.add))
                        link(ts(tmp, tmp, -MAGIC, None, ALU.add))
                        link(stt(out_, tmp, -PI_HI, hb, ALU.mult, ALU.add))
                        link(stt(out_, tmp, -PI_MID, out_, ALU.mult, ALU.add))
                        link(stt(out_, tmp, -PI_LO, out_, ALU.mult, ALU.add))
                        link(ts(out_, out_, 2.0 * math.pi * turn, None, ALU.add))
                        link(ts(out_, out_, -PI_CLAMP, PI_CLAMP, ALU.max, ALU.min))
                if part == 3:
                    ts(tmp, tmp, 0.0, None, ALU.mult).then_inc(s5_arg, 1)
                    dve.wait_ge(s5_arg, 2)

            def softplus(part):
                if part == 0:
                    link(ts(S[2], S[1], 2.0, None, ALU.add))
                    link(nc.vector.reciprocal(S[2], S[2]))
                    link(tt(S[2], S[1], S[2], ALU.mult))
                    link(tt(S[3], S[2], S[2], ALU.mult))
                    link(ts(S[4], S[3], 1.0 / 15, 1.0 / 13, ALU.mult, ALU.add))
                    for k in (11, 9, 7, 5, 3, 1):
                        link(tt(S[4], S[4], S[3], ALU.mult))
                        link(ts(S[4], S[4], 1.0 / k, None, ALU.add))
                if part == 1:
                    link(tt(S[4], S[4], S[2], ALU.mult))
                    link(ts(S[5], pcol2[:, C_LAM:C_LAM + LC], -1.0, 0.0, ALU.mult, ALU.max))
                    link(stt(S[4], S[4], 2.0, S[5], ALU.mult, ALU.add))
                    link(ts(S[4], S[4], LRU_C, None, ALU.mult))
                    ts(S[5], S[4], -1.0, None, ALU.mult).then_inc(lru_sp, 1)

            def s5_coefficients(part):
                if part == 0:
                    dve.wait_ge(s5_exp, 2)
                    link(ts(t1, th, -1.0, 1.0, ALU.mult, ALU.add))
                    link(nc.vector.reciprocal(t1, t1))
                    link(tt(t1, t1, th, ALU.mult))
                    link(ts(mask, a, -1.0, None, ALU.is_gt))
                    link(ts(t2_, a, 1.0, None, ALU.is_lt))
                    link(tt(mask, mask, t2_, ALU.mult))
                if part == 1:
                    link(ts(em1, ea, -1.0, None, ALU.add))
                    link(stt(t1, t1, 2.0, em1, ALU.mult, ALU.subtract))
                    link(tt(t1, t1, mask, ALU.mult))
                    link(tt(em1, em1, t1, ALU.add))
                    link(ts(rho[:, :], em1, 1.0, None, ALU.add))
                    tt(rho2[:, :], rho[:, :], rho[:, :], ALU.mult)
                if part == 2:
                    link(tt(t1, s2, s2, ALU.mult))
                    link(ts(t1, t1, 2.0, None, ALU.mult))
                    link(ts(cosb, t1, -1.0, 1.0, ALU.mult, ALU.add))
                    link(tt(sinb, s2, c2, ALU.mult))
                    link(ts(sinb, sinb, 2.0, None, ALU.mult))
                    link(tt(rot1[:, 0, :], sinb, sinb, ALU.mult))
                    link(ts(rot1[:, 0, :], rot1[:, 0, :], -2.0, 1.0, ALU.mult, ALU.add))
                if part == 3:
                    link(stt(rot1[:, 1, :], sinb, 2.0, cosb, ALU.mult, ALU.mult))
                    tt(lam[:, 0, :], rho[:, :], cosb, ALU.mult)
                    tt(lam[:, 1, :], rho[:, :], sinb, ALU.mult)
                    link(tt(X, em1, cosb, ALU.mult))
                    link(tt(X, X, t1, ALU.subtract))
                    link(tt(Y, rho[:, :], sinb, ALU.mult))
                    link(tt(n2, lre, lre, ALU.mult))
                if part == 4:
                    link(tt(t1, lim, lim, ALU.mult))
                    link(tt(n2, n2, t1, ALU.add))
                    link(nc.vector.reciprocal(n2, n2))
                    link(tt(cr, X, lre, ALU.mult))
                    link(tt(t1, Y, lim, ALU.mult))
                    link(tt(cr, cr, t1, ALU.add))
                if part == 5:
                    link(tt(cr, cr, n2, ALU.mult))
                    link(tt(ci, Y, lre, ALU.mult))
                    link(tt(t1, X, lim, ALU.mult))
                    link(tt(ci, ci, t1, ALU.subtract))
                    tt(ci, ci, n2, ALU.mult).then_inc(s5_small, 1)

            def head_squares(j):
                if j >= 2:
                    dve.wait_ge(qk_sum, j - 1)
                for c in range(2 if j < 4 else 1):
                    src = qT[:, 2 * j + c] if j < 4 else kvT[:, 0]
                    last = tt(squares_of(j, c), src, src, ALU.mult)
                last.then_inc(qk_sq, 1)

            pair(0, 0, dest=qT[:, 0:2])
            parameters()
            pair(1, 1, dest=qT[:, 2:4])
            rms()
            link(tt(qT[:, 0:4], qT[:, 0:4], rs[:, :].unsqueeze(1).to_broadcast([P, 4, L]), ALU.mult))
            head_squares(0)
            head_squares(1)
            projection(2, 0, qT[:, 4:6, :], beside=s5_arguments)
            head_squares(2)
            projection(3, 1, qT[:, 6:8, :])
            head_squares(3)
            projection(P_KV, 0, kvT[:, :, :], beside=s5_coefficients)
            head_squares(4)

            def softmax_max(i):
                d = i % 2
                dve.wait_ge(scored, i + 1)
                s = px[:, d, :].rearrange("p (n k) -> p n k", n=NCH)
                nc.vector.reduce_max(am[:, d, 0, 0:1], s[:, 0, 0:CH], AX.X)
                link(nc.vector.reduce_max(am[:, d, 0, 1:NCH], s[:, 1:NCH], AX.X))
                link(ts(am[:, d, 0, :], am[:, d, 0, :], HD ** -0.5, scol[:, NT + i:NT + i + 1], ALU.mult, ALU.max))
                ts(am[:, d, 1, :], am[:, d, 0, :], -1.0, None, ALU.mult).then_inc(maxed, 1)

            def softmax_norm(i):
                d = i % 2
                dve.wait_ge(expd, i + 1)
                link(tt(am[:, d, 4, :], am[:, d, 2, :], am[:, d, 3, :], ALU.add))
                link(nc.vector.reciprocal(am[:, d, 4, :], am[:, d, 4, :]))
                tt(pb[:, d, 0, 0:CH], pb[:, d, 0, 0:CH], am[:, d, 4, 0:1].to_broadcast([P, CH]), ALU.mult)
                tt(pb[:, d, 1:NCH], pb[:, d, 1:NCH], am[:, d, 4, 1:NCH].unsqueeze(2).to_broadcast([P, NCH - 1, P]),
                   ALU.mult).then_inc(probs, 1)

            def attended(i):
                hi.wait(dve)
                tt(A2[:, LC + i, L:2 * L], px[:, 3, 0:L], A2[:, LC + i, 0:L].bitcast(F32), ALU.subtract)\
                    .then_inc(a2_ready, 1)

            def normed(i, half):
                return stt(qT[:, i], qT[:, i], pcol2[:, C_QG:C_QG + 1], wide_root(half), ALU.mult, ALU.mult)

            def beside(n):
                if n < 2:
                    s5_coefficients(4 + n)
                if n in (7, 9):
                    softplus((n - 7) // 2)
                if n == SLOT_SUM:
                    dve.wait_ge(qk_sum, 5)
                    ts(nv[0:NH, :], px[0:NH, 3, L:2 * L], 1.0 / HD, EPS, ALU.mult, ALU.add).then_inc(qk_var, 1)
                    dve.wait_ge(v_t, 1)
                    nc.vector.tensor_copy(vw[:, :, :], px[:, 2, 0:3 * P].rearrange("p (w n) -> p w n", w=3))\
                        .then_inc(v_ready, 1)
                if n == SLOT_INV:
                    dve.wait_ge(qk_root, 1)
                    inv_root(nv[0:NH, :], root18[:, :], nw[0:NH, :], done=qk_norm)
                if n == SLOT_WIDE:
                    dve.wait_ge(qk_wide, 1)
                    link(stt(kvT[:, 0], kvT[:, 0], pcol2[:, C_KG:C_KG + 1], wide_root(7), ALU.mult, ALU.mult))
                    normed(LC - 2, LC - 2)
                    nc.vector.tensor_copy(kd[0:64, 0, :], kvT[0:64, 0, :])
                    nc.vector.tensor_copy(kd[64:P, 1, :], kvT[64:P, 0, :]).then_inc(kd_ready, 1)
                    normed(0, 0)
                    normed(1, 1).then_inc(q_normed, 1)
                    for i in range(2, 4):
                        last = normed(i, i)
                    last.then_inc(q_normed, 1)
                if n == SLOT_Q:
                    for i in range(4, LC - 2):
                        normed(i, i)
                if n == SLOT_Q + 1:
                    dve.wait_ge(qk_wide, 2)
                    normed(LC - 1, 7).then_inc(q_normed, 1)
                i, odd = divmod(n - ATT0, 2)
                if not odd and 0 <= i < LC:
                    softmax_max(i)
                if odd and 0 <= i - 1 < LC:
                    softmax_norm(i - 1)
                if odd and 0 <= i - 2 < LC:
                    attended(i - 2)
                if n == GATE0 + LC:
                    dve.wait_ge(gates_sg, LC)
                    for c in range(0, LC, 4):
                        tt(li[:, c:c + 4], li[:, c:c + 4], xc[:, c:c + 4], ALU.mult)
                if n == GATE0 + LC + 1:
                    for c in range(0, LC, 4):
                        h = slice(c, c + 4)
                        dve.wait_ge(lru_a, c + 4)
                        link(tt(la[:, h], lr[:, h], lr[:, h], ALU.mult))
                        stt(lt[:, h], la[:, h], 1.0, lt[:, h], ALU.add, ALU.mult).then_inc(lru_m2, 1)

            for g in range(P_XB, P_OUT):
                j = g - P_XB
                dest = xb[:, 2 * j:2 * j + 2, 3:3 + L] if j < 4 else gT[:, 2 * j - 8:2 * j - 6, :]
                pair(g, g % 2, beside=lambda s: beside(j * NU + s))
                tt(dest, cross[:, g % 2], rs2, ALU.mult).then_inc(xb_ready if j < 4 else g_ready, 1)

            for c in range(0, LC, 4):
                h = slice(c, c + 4)
                dve.wait_ge(lru_m, c // 4 + 1)
                link(tt(li[:, h], li[:, h], lt[:, h], ALU.mult))
                for k in range(c, c + 4):
                    last = nc.vector.tensor_tensor_scan(la[:, k], lr[:, k], li[:, k], 0.0, ALU.mult, ALU.add)
                link(last)
                dve.wait_ge(lru_h, c // 4 + 1)
                for k in range(c, c + 4):
                    tt(gT[:, k], gT[:, k], la[:, k], ALU.mult).then_inc(lru_y, 1)
            for c in range(LC):
                hi.wait(dve)
                tt(A2[:, c, L:2 * L], gT[:, c], A2[:, c, 0:L].bitcast(F32), ALU.subtract).then_inc(a2_ready, 1)

            def out_pair(j, d):
                c = (P_OUT + d) % 2
                pair(j + P_OUT, c)
                residual(j, c)
                operand_from_x(j * 2, G_FF0)
            double_pairs(dve, 8, out_pair, (hi, 2))

            def mlp(g0, final):
                def up(j, d, q=0, quarter0=True):
                    c = (g0 + d) % 2
                    pair(q * 16 + j + g0, c, before=rms if quarter0 and isinstance(j, int) and j == 0 else None)
                    link(tt(cross[:, c], cross[:, c], rs2, ALU.mult))
                    stt(cross[:, c], cross[:, c], 0.0, cross[:, c], ALU.max, ALU.mult).then_inc(hid_ready, 1)
                    hi.wait(dve)
                    k = bass.ds(j * 2, 2)
                    tt(A2[:, k, L:2 * L], cross[:, c], A2[:, k, 0:L].bitcast(F32), ALU.subtract).then_inc(a2_ready, 1)

                def down(j, d, q=0, nxt=True):
                    c = (g0 + d) % 2
                    pair(q * 16 + j + (g0 + 8), c, nxt=nxt)
                    residual(j, c)

                double_pairs(dve, 8, up, (hi, 2), (seq, 2), first=2)
                double_pairs(dve, 8, down)
                with trips(dve, QTR - 2, (hi, 8), (seq, 8)) as q:
                    double_pairs(dve, 8, lambda j, d: up(j, d, q + 1, False), (hi, 2), (seq, 2))
                    double_pairs(dve, 8, lambda j, d: down(j, d, q + 1))
                double_pairs(dve, 8, lambda j, d: up(j, d, QTR - 1, False), (hi, 2), (seq, 2))
                double_pairs(dve, 8, lambda j, d: down(j, d, QTR - 1,
                                                       nxt=not (final and isinstance(j, int) and j == 7)), last=2)

            mlp(P_MLP0, False)

            rms()

            def s5_u(c, b):
                k = bass.ds(c, 1)
                if not isinstance(c, int) or c >= 2:
                    dve.wait_ge(s5_y, c * 2 - 3)
                stt(uc[:, b].rearrange("p (e m) -> p e m", e=2), xT[:, k, :].rearrange("p o (m e) -> p (o e) m", e=2),
                    gain(c + G_MIX1), rs.rearrange("p (m e) -> p e m", e=2), ALU.mult, ALU.mult)\
                    .then_inc(u_ready, 1)
                dve.wait_ge(u_ready, c + 1)
                if not isinstance(c, int) or c >= 2:
                    dve.wait_ge(s5_bu, c * 2 - 2)
                stack_input(nc.vector.tensor_copy, b, 0).then_inc(us_ready[0], 1)

            def s5_du(c, b):
                dve.wait_ge(u_ready, c + 1)
                if not isinstance(c, int) or c >= 2:
                    dve.wait_ge(s5_yf, c - 1)
                link(ts(du[:, b], uc[:, b], gain(c + C_D), None, ALU.mult))

            def s5_lam(c, b):
                dve.wait_ge(s5_neg, c + 1)
                k = bass.ds(c * TPC, TPC)
                C = cst[:, b, 0:2].rearrange("p k (j n) -> p k j n", j=TPC)
                prod = ctm.rearrange("p w k (j n) -> p w k j n", j=TPC)
                for w in range(2):
                    last = tt(prod[:, w], C, lam[:, w, k].unsqueeze(1).unsqueeze(3).to_broadcast([P, 2, TPC, 2 * SH]),
                              ALU.mult)
                link(last)
                tt(cst[:, b, 2], ctm[:, 0, 0], ctm[:, 1, 1], ALU.add)
                tt(cst[:, b, 3], ctm[:, 0, 1], ctm[:, 1, 0], ALU.subtract).then_inc(s5_ca, 1)

            def s5_rotate(v, i, b, h):
                if h == 0:
                    dve.wait_ge(tab_loaded[b], i * 32 + 32)
                dve.wait_ge(s5_bu, v + 1)
                if not (isinstance(v, int) and v < 2):
                    dve.wait_ge(s5_z, v - 1)
                bu = bu_banks(h)[:, :, 0:L].rearrange("p j (k m) -> p j k m", k=2)
                for w in range(2):
                    last = tt(ab[:, h, w], bu, tab[:, b, w, 2 * h:2 * h + 2].unsqueeze(2).to_broadcast([P, 2, 2, LH]),
                              ALU.mult)
                last.then_inc(s5_rot, 1)

            def s5_scan(v, b, h):
                dve.wait_ge(s5_z, v + 1)
                if not (isinstance(v, int) and v < 2):
                    dve.wait_ge(s5_sn, v - 1)
                for k in range(2):
                    for j in range(2):
                        last = nc.vector.tensor_tensor_scan(
                            gb[:, h, k, j], rho2[:, bass.ds(v * 2 + j, 1)].to_broadcast([P, LH]), zb[:, h, k, j],
                            0.0, ALU.mult, ALU.add)
                last.then_inc(s5_g, 1)
                dve.wait_ge(s5_g, v + 1)
                if not (isinstance(v, int) and v < 2):
                    dve.wait_ge(s5_h, v - 1)
                cos = tab[:, b, 0, 2 * h:2 * h + 2].rearrange("p j m -> p (j m)")
                tt(cdb[:, h, 0].rearrange("p k j m -> p k (j m)"), gb[:, h].rearrange("p k j m -> p k (j m)"),
                   cos.unsqueeze(1).to_broadcast([P, 2, L]), ALU.mult).then_inc(s5_cs, 1)

            def s5_finish(c, b):
                dve.wait_ge(s5_y, c * 2 + 2)
                tt(yb[:, b].rearrange("p (m e) -> p e m", e=2), du[:, b].rearrange("p (e m) -> p e m", e=2),
                   ps[:, b, 0:L].rearrange("p (e m) -> p e m", e=2), ALU.add).then_inc(s5_yf, 1)

            def s5_lo(c, b):
                hi.wait(dve)
                k = bass.ds(c, 1)
                tt(A2[:, k, L:2 * L], yb[:, b:b + 1], A2[:, k, 0:L].bitcast(F32), ALU.subtract).then_inc(a2_ready, 1)

            def s5_trip(i, first=False, more=True):
                for b in range(2):
                    c, before, following = i * 2 + b, not (first and b == 0), b == 0 or more
                    for h in range(2):
                        v = i * 4 + (2 * b + h)
                        if h == 0 and following and not (first and b == 0):
                            s5_u(c + 1, 1 - b)
                        if h == 0:
                            s5_rotate(v + 1, i, b, 1)
                        elif following:
                            s5_rotate(v + 1, i + b, 1 - b, 0)
                            s5_lam(c + 1, 1 - b)
                        s5_scan(v, b, h)
                        if h == 0:
                            if before:
                                s5_finish(c - 1, 1 - b)
                            if following:
                                s5_du(c + 1, 1 - b)
                        elif before:
                            s5_lo(c - 1, 1 - b)

            s5_u(0, 0)
            s5_u(1, 1)
            s5_lam(0, 0)
            s5_rotate(0, 0, 0, 0)
            s5_du(0, 0)
            s5_trip(0, first=True)
            with trips(dve, KC // 2 - 2, (hi, 2), (seq, 4)) as i:
                s5_trip(i + 1)
            s5_trip(KC // 2 - 1, more=False)
            s5_finish(KC - 1, 1)
            s5_lo(KC - 1, 1)

            def glu(j, d):
                c = (P_GLU + d) % 2
                pair(j + P_GLU, c)
                if d == 1:
                    gate.wait(dve)
                    link(tt(cross[:, c], cross[:, c], cross[:, 1 - c], ALU.mult))
                    xs = xT[:, bass.ds(j - 1, 2), :]
                    tt(xs, xs, cross[:, c], ALU.add).then_inc(x_final, 1)
                    operand_from_x(j - 1, G_FF1)
            double_pairs(dve, 16, glu, (hi, 1), (seq, 1), (gate, 1))
            mlp(P_MLP1, True)

        @block.gpsimd
        def _(pool):
            tt = nc.gpsimd.tensor_tensor
            seq = Tally(pool_seq)
            xf = Tally(x_final)

            def link(ins):
                seq.inc(ins)
                seq.again(pool)

            link(nc.gpsimd.memset(ident[:, :], 0.0))
            link(nc.gpsimd.memset(ones[:, :], 1.0))
            link(nc.gpsimd.memset(hsel[:, :], 0.0))
            link(nc.gpsimd.memset(hsel[0:64, 16:17], 1.0))
            link(nc.gpsimd.memset(hsel[64:P, 17:18], 1.0))
            nc.gpsimd.affine_select(out=ident[:, :], in_=ident[:, :], compare_op=ALU.not_equal, fill=1.0, base=0,
                                    pattern=[[-1, P]], channel_multiplier=1).then_inc(consts, 1)
            pool.wait_ge(consts, 1)
            nc.gpsimd.memset(wax[:, :, :, :], 0.0).then_inc(zeroed, 1)
            nc.gpsimd.tensor_copy(rsel[:, :, :], ident[0:NH, 0:NH].unsqueeze(2).to_broadcast([NH, NH, HD]))\
                .then_inc(zeroed, 1)

            def zero_squares():
                link(nc.gpsimd.memset(ss[:, :, :], 0.0))

            sqd = Tally(squared)

            def add_squares(xs):
                sqd.again(pool) if not (isinstance(sqd.value, int) and sqd.value == 0) else None
                link(tt(sq[:, :, :], xs, xs, ALU.mult))
                sqd.inc(tt(ss[:, :, :], ss[:, :, :], sq[:, :, :], ALU.add))

            zero_squares()
            for i in range(KC // 2):
                copied(pool, i)
                add_squares(xT[:, 2 * i:2 * i + 2, :])
            pool.wait_ge(s5_small, 1)
            pool.wait_ge(b_loaded, 32)
            def halves(t):
                return t.rearrange("p (c t) h -> p c t h", t=2)

            def by_tile(t):
                return t.rearrange("p c q t h -> p (c q) t h")
            cr = s5w[:, 17, :].unsqueeze(2).to_broadcast([P, NT, SH])
            ci = s5w[:, 18, :].unsqueeze(2).to_broadcast([P, NT, SH])
            for k, (u, v, op) in enumerate(((cr, ci, ALU.subtract), (ci, cr, ALU.add))):
                link(tt(btmp[:, 0], braw[:, 0], u, ALU.mult))
                link(tt(btmp[:, 1], braw[:, 1], v, ALU.mult))
                link(tt(by_tile(bbar[:, :, :, k]), halves(btmp[:, 0]), halves(btmp[:, 1]), op))
            bbar_to = bbar_d.rearrange("c p f -> p c f")
            pool.dma_start(bbar_to[:, :, 2 * TPC * SH:], bbar.rearrange("p c q k t h -> p c (q k t h)"))\
                .then_inc(bbar_stored, 16)
            lb = braw.rearrange("p k j h -> p (k j h)").rearrange("p (c q k t h) -> p c q k t h", q=2, k=2, t=2, h=SH)
            lr_, li_ = [lam[:, k].rearrange("p (c t) -> p c t", t=2).unsqueeze(3).to_broadcast([P, NT // 2, 2, SH])
                        for k in range(2)]
            for k, (u, v, op) in enumerate(((lr_, li_, ALU.subtract), (li_, lr_, ALU.add))):
                link(tt(halves(btmp[:, 0]), by_tile(bbar[:, :, :, 0]), u, ALU.mult))
                link(tt(halves(btmp[:, 1]), by_tile(bbar[:, :, :, 1]), v, ALU.mult))
                link(tt(by_tile(lb[:, :, :, k]), halves(btmp[:, 0]), halves(btmp[:, 1]), op))
            pool.dma_start(bbar_to[:, :, 0:2 * TPC * SH], lb.rearrange("p c q k t h -> p c (q k t h)"))\
                .then_inc(bbar_stored, 16)

            pool.wait_ge(par_ready, 1)
            pool.wait_ge(xt_done, KC // 2)
            link(nc.gpsimd.memset(xb[:, :, 0:3], 0.0))
            pool.wait_ge(bbar_stored, 32)
            for j in range(4):
                c = slice(2 * j, 2 * j + 2)
                pool.wait_ge(xb_ready, j + 1)

                def column(k):
                    return pcol[:, k + 2 * j:k + 2 * j + 2].unsqueeze(2).to_broadcast([P, 2, L])
                link(tt(xc[:, c], xb[:, c, 0:L], column(C_CW), ALU.mult))
                for k in range(1, 4):
                    link(tt(sq[:, :, :], xb[:, c, k:k + L], column(C_CW + k * LC), ALU.mult))
                    link(tt(xc[:, c], xc[:, c], sq[:, :, :], ALU.add))
                tt(xc[:, c], xc[:, c], column(C_CB), ALU.add).then_inc(conv_done, 1)

            def tables(i, stored):
                if stored:
                    pool.wait_ge(tab_stored, i * 16)
                link(nc.gpsimd.tensor_copy(ctab[:, :, :, 0], rot1[:, :, bass.ds(i * 2, 2)]))
                n = 1
                while n < LH:
                    a, b = ttmp[:, 0, :, :, 0:n], ttmp[:, 1, :, :, 0:n]
                    turn = [ctab[:, k, :, n - 1:n].unsqueeze(1).to_broadcast([P, 2, 2, n]) for k in range(2)]
                    link(tt(a, ctab[:, :, :, 0:n], turn[0], ALU.mult))
                    link(tt(b, ctab[:, :, :, 0:n], turn[1], ALU.mult))
                    link(tt(ctab[:, 0, :, n:2 * n], a[:, 0], b[:, 1], ALU.subtract))
                    link(tt(ctab[:, 1, :, n:2 * n], a[:, 1], b[:, 0], ALU.add))
                    n *= 2

            def store(c, h):
                pool.dma_start(tab_d[bass.ds(c, 1)].rearrange("o p (k j t) -> p (o k) j t", k=2, j=TPC)
                               [:, :, 2 * h:2 * h + 2, :], ctab[:, :, :, :]).then_inc(tab_stored, 16)

            STEPS = 1 + 4 * 7
            EARLY = 3

            def table_chunks(first, n):
                with trips(pool, n, (seq, 2 * STEPS)) as c:
                    for h in range(2):
                        tables(c * 2 + (2 * first + h), True)
                        store(c + first, h)

            for h in range(2):
                tables(h, h > 0)
                store(0, h)
            table_chunks(1, EARLY - 1)

            def norm_squares(count, skip):
                pool.wait_ge(rms_sum, count - 1)
                xf.skip(skip)
                zero_squares()
                with trips(pool, KC // 2, (xf, 1), (seq, 1), (sqd, 1)) as i:
                    xf.wait(pool)
                    add_squares(xT[:, bass.ds(i * 2, 2), :])

            norm_squares(2, 0)
            table_chunks(EARLY, KC - EARLY)
            nc.gpsimd.memset(hb[:, :, :, :, 0:1], 0.0)
            nc.gpsimd.memset(bx[:, :, :, :, :, :], 0.0).then_inc(bx_zero, 1)
            norm_squares(3, 8 * (QTR - 1))

            def s5_z_of(v, h):
                pool.wait_ge(s5_rot, v + 1)
                if not (isinstance(v, int) and v < 2):
                    pool.wait_ge(s5_g, v - 1)
                tt(zb[:, h, 0], ab[:, h, 0, :, 0], ab[:, h, 1, :, 1], ALU.add)
                tt(zb[:, h, 1], ab[:, h, 0, :, 1], ab[:, h, 1, :, 0], ALU.subtract).then_inc(s5_z, 1)

            def s5_state(v, b, h):
                pool.wait_ge(s5_g, v + 1)
                if not (isinstance(v, int) and v < 2):
                    pool.wait_ge(s5_h, v - 1)
                    pool.wait_ge(s5_y, v - 1)
                sin = tab[:, b, 1, 2 * h:2 * h + 2].rearrange("p j m -> p (j m)")
                tt(cdb[:, h, 1].rearrange("p k j m -> p k (j m)"), gb[:, h].rearrange("p k j m -> p k (j m)"),
                   sin.unsqueeze(1).to_broadcast([P, 2, L]), ALU.mult).then_inc(s5_sn, 1)
                pool.wait_ge(s5_sn, v + 1)
                pool.wait_ge(s5_cs, v + 1)
                tt(hb[:, h, 0, :, 1:LH + 1], cdb[:, h, 0, 0], cdb[:, h, 1, 1], ALU.subtract)
                tt(hb[:, h, 1, :, 1:LH + 1], cdb[:, h, 0, 1], cdb[:, h, 1, 0], ALU.add).then_inc(s5_h, 1)

            def s5_trip(i, more=True):
                for n in range(4):
                    v = i * 4 + n
                    if n + 1 < 4 or more:
                        s5_z_of(v + 1, (n + 1) % 2)
                    s5_state(v, n // 2, n % 2)

            s5_z_of(0, 0)
            s5_trip(0)
            with pool.Fori(1, KC // 2 - 1) as i:
                s5_trip(i)
            s5_trip(KC // 2 - 1, more=False)

            norm_squares(4, 0)


_INS = ["x", "mix_norm_e", "w_in_e", "conv_w", "conv_b", "lru_wa", "lru_ba", "lru_wx", "lru_bx", "lru_lambda",
        "q_gain", "k_gain", "sinks", "w_out_e", "mix_norm_o", "s5_lam_re", "s5_lam_im", "s5_log_step",
        "s5_b_re", "s5_b_im", "s5_c_re", "s5_c_im", "s5_d", "w_glu", "ffn_norm", "w_up", "w_down"]
_OUTS = [((1, L, D), "float32")]


def kernel(**inputs):
    import numpy as _np
    import concourse.bacc as _bacc
    from concourse import mybir as _mybir
    from concourse.bass_utils import run_bass_kernel_spmd as _run

    nc = _bacc.Bacc("TRN2", target_bir_lowering=False, num_devices=1)
    arrays, args = {}, []
    for name in _INS:
        a = _np.ascontiguousarray(inputs[name])
        arrays[f"in_{name}_dram"] = a
        args.append(nc.dram_tensor(f"in_{name}_dram", a.shape, _mybir.dt.from_np(a.dtype), kind="ExternalInput").ap())
    for i, (shape, dtype) in enumerate(_OUTS):
        dt = _mybir.dt.from_np(_np.dtype(dtype))
        args.append(nc.dram_tensor(f"out_{i}_dram", shape, dt, kind="ExternalOutput").ap())
    trunk_kernel(nc, *args)
    r = _run(nc, [arrays], core_ids=[0])
    got = tuple(r.results[0][f"out_{i}_dram"] for i in range(len(_OUTS)))
    return got[0]
```
